# Optimizing a Trainium2 kernel written in Bass

```python
import math
import jax, jax.numpy as jnp
from jax import lax
import numpy as np

D_MODEL = 1024
BATCH = 1
SEQ = 256
DEPTH = 2

CHUNK = 64
HEAD_DIM = 64
N_MIXERS = 4
GROUP_WIDTH = D_MODEL // N_MIXERS
D_MIX = N_MIXERS * GROUP_WIDTH

SWA_HEADS = GROUP_WIDTH // HEAD_DIM
SWA_KV_HEADS = SWA_HEADS // 2
SWA_WINDOW = 128
SWA_WIN_CHUNKS = -(-SWA_WINDOW // CHUNK)

DSA_HEADS = GROUP_WIDTH // HEAD_DIM
DSA_Q_RANK = D_MODEL // 8
IDX_HEADS = 4
IDX_DIM = 32
DSA_TOPK = 256
DSA_QBLOCK = 128

MLSTM_HEADS = GROUP_WIDTH // HEAD_DIM
MLSTM_CONV = 4

S5_GROUP_CH = 16
S5_GROUPS = GROUP_WIDTH // S5_GROUP_CH
S5_STATE = 64

D_FF = 2816
N_SUB = 3
ALPHA = (2 * DEPTH) ** 0.25
BETA = (8 * DEPTH) ** -0.25
LN_EPS = 1e-5
NEG_INF = -1e30
N_SOFTMAX_HEADS = SWA_HEADS + DSA_HEADS

IN_SIZES = (
    SWA_HEADS * HEAD_DIM,
    SWA_KV_HEADS * HEAD_DIM,
    SWA_KV_HEADS * HEAD_DIM,
    DSA_Q_RANK,
    HEAD_DIM,
    HEAD_DIM,
    IDX_DIM,
    IDX_HEADS,
    2 * MLSTM_HEADS * HEAD_DIM,
    MLSTM_HEADS * HEAD_DIM,
    MLSTM_HEADS,
    MLSTM_HEADS,
    MLSTM_HEADS * HEAD_DIM,
    GROUP_WIDTH,
)
D_IN = sum(IN_SIZES)

kernel_name = "hybrid_chunk_causal_parallel_heads"

def _layer_norm(x, g, b):
    xf = x.astype(jnp.float32)
    mu = xf.mean(-1, keepdims=True)
    var = jnp.square(xf - mu).mean(-1, keepdims=True)
    y = (xf - mu) * lax.rsqrt(var + LN_EPS) * g.astype(jnp.float32) + b.astype(jnp.float32)
    return y.astype(x.dtype)

def _alibi_slopes(n):
    return jnp.exp2(-8.0 * jnp.arange(1, n + 1, dtype=jnp.float32) / n)

def _swiglu(u, w13, w2):
    a, g = jnp.split(u @ w13, 2, axis=-1)
    return (jax.nn.silu(a) * g) @ w2

def _split_cols(z, sizes):
    outs, off = [], 0
    for s in sizes:
        outs.append(z[..., off:off + s])
        off += s
    return outs

def _causal_conv(x, w, b):
    k = w.shape[0]
    y = lax.conv_general_dilated(x, w.astype(x.dtype)[:, None, :], window_strides=(1,),
                                 padding=[(k - 1, 0)], dimension_numbers=('NWC', 'WIO', 'NWC'),
                                 feature_group_count=x.shape[-1])
    return y + b.astype(x.dtype)

def _sliding_window_sink_attention(q, k, v, sinks, slopes):
    f32 = jnp.float32
    bn, t, hq, dh = q.shape
    hkv = k.shape[2]
    rep = hq // hkv
    nc = t // CHUNK
    nb = SWA_WIN_CHUNKS + 1
    qc = q.astype(f32).reshape(bn, nc, CHUNK, hkv, rep, dh)

    def band(a):
        a = a.astype(f32).reshape(bn, nc, CHUNK, hkv, dh)
        a = jnp.pad(a, ((0, 0), (SWA_WIN_CHUNKS, 0), (0, 0), (0, 0), (0, 0)))
        return jnp.concatenate([a[:, i:i + nc] for i in range(nb)], axis=2)

    kb, vb = band(k), band(v)
    s = jnp.einsum('bcqgrd,bckgd->bgrcqk', qc, kb) * dh ** -0.5
    qi = jnp.arange(CHUNK)
    kj = jnp.arange(nb * CHUNK)
    dist = jnp.abs(qi[:, None] + SWA_WIN_CHUNKS * CHUNK - kj[None, :]).astype(f32)
    key_chunk = jnp.arange(nc)[:, None] - SWA_WIN_CHUNKS + kj[None, :] // CHUNK
    s = s - slopes.reshape(hkv, rep)[:, :, None, None, None] * dist
    s = jnp.where((key_chunk >= 0)[:, None, :], s, NEG_INF)
    sink = jnp.broadcast_to(sinks.astype(f32).reshape(hkv, rep, 1, 1, 1), s.shape[:-1] + (1,))
    p = jax.nn.softmax(jnp.concatenate([s, sink], axis=-1), axis=-1)[..., :-1]
    o = jnp.einsum('bgrcqk,bckgd->bcqgrd', p, vb)
    return o.reshape(bn, t, hq * dh)

def _dsa_attention(q, k, v, q_idx, k_idx, w_idx, slopes):
    f32 = jnp.float32
    bn, t, h, dh = q.shape
    topk = min(DSA_TOPK, t // 4)
    nqb = t // DSA_QBLOCK
    key_chunk = jnp.arange(t) // CHUNK
    kf, vf, kif = k.astype(f32), v.astype(f32), k_idx.astype(f32)
    idx_scale = (IDX_DIM * IDX_HEADS) ** -0.5

    def blocks(a):
        return jnp.swapaxes(a.astype(f32).reshape((bn, nqb, DSA_QBLOCK) + a.shape[2:]), 0, 1)

    qpos = jnp.arange(t).reshape(nqb, DSA_QBLOCK)

    def one_block(args):
        qb, qib, wb, pos = args
        rel = jax.nn.relu(jnp.einsum('bqhd,bsd->bqhs', qib, kif))
        score = jnp.einsum('bqhs,bqh->bqs', rel, wb) * idx_scale
        qchunk = pos // CHUNK
        score = jnp.where(key_chunk[None, :] <= qchunk[:, None], score, NEG_INF)
        _, sel = lax.top_k(score, topk)
        kg = jax.vmap(lambda a, i: a[i])(kf, sel)
        vg = jax.vmap(lambda a, i: a[i])(vf, sel)
        valid = key_chunk[sel] <= qchunk[None, :, None]
        dist = jnp.abs(pos[None, :, None] - sel).astype(f32)
        s = jnp.einsum('bqhd,bqkd->bhqk', qb, kg) * dh ** -0.5 - slopes[None, :, None, None] * dist[:, None]
        s = jnp.where(valid[:, None], s, NEG_INF)
        p = jax.nn.softmax(s, axis=-1)
        return jnp.einsum('bhqk,bqkd->bqhd', p, vg)

    o = lax.map(one_block, (blocks(q), blocks(q_idx), blocks(w_idx), qpos))
    return jnp.swapaxes(o, 0, 1).reshape(bn, t, h * dh)

def _mlstm(q, k, v, ig, fg, norm_g):
    f32 = jnp.float32
    bn, t, h, dh = q.shape
    nc = t // CHUNK
    k = k * dh ** -0.5
    lf = jax.nn.log_sigmoid(fg)

    def chunks4(a):
        return a.reshape(bn, nc, CHUNK, h, dh).transpose(1, 0, 3, 2, 4)

    def chunks3(a):
        return a.reshape(bn, nc, CHUNK, h).transpose(1, 0, 3, 2)

    causal = jnp.tril(jnp.ones((CHUNK, CHUNK), dtype=bool))

    def step(carry, xs):
        cmat, nvec, m = carry
        qj, kj, vj, igj, lfj = xs
        b = jnp.cumsum(lfj, axis=-1)
        dlog = b[..., :, None] - b[..., None, :] + igj[..., None, :]
        dlog = jnp.where(causal, dlog, -jnp.inf)
        inter = b + m[..., None]
        mj = jnp.maximum(inter, dlog.max(-1))
        dw = jnp.exp(dlog - mj[..., None])
        iw = jnp.exp(inter - mj)
        sc = jnp.einsum('bhjd,bhsd->bhjs', qj, kj) * dw
        num = iw[..., None] * jnp.einsum('bhjd,bhde->bhje', qj, cmat) + jnp.einsum('bhjs,bhse->bhje', sc, vj)
        den = iw * jnp.einsum('bhjd,bhd->bhj', qj, nvec) + sc.sum(-1)
        hj = num / jnp.maximum(jnp.abs(den), jnp.exp(-mj))[..., None]
        bl = b[..., -1]
        dec = bl[..., None] - b + igj
        m_new = jnp.maximum(bl + m, dec.max(-1))
        wc = jnp.exp(bl + m - m_new)
        ws = jnp.exp(dec - m_new[..., None])
        cmat = wc[..., None, None] * cmat + jnp.einsum('bhs,bhsd,bhse->bhde', ws, kj, vj)
        nvec = wc[..., None] * nvec + jnp.einsum('bhs,bhsd->bhd', ws, kj)
        return (cmat, nvec, m_new), hj

    init = (jnp.zeros((bn, h, dh, dh), f32), jnp.zeros((bn, h, dh), f32), jnp.zeros((bn, h), f32))
    _, hs = lax.scan(step, init, (chunks4(q), chunks4(k), chunks4(v), chunks3(ig), chunks3(lf)))
    hs = hs.transpose(1, 0, 3, 2, 4).reshape(bn, t, h, dh)
    mu = hs.mean(-1, keepdims=True)
    var = jnp.square(hs - mu).mean(-1, keepdims=True)
    hs = (hs - mu) * lax.rsqrt(var + LN_EPS) * norm_g.astype(f32).reshape(h, dh)
    return hs.reshape(bn, t, h * dh)

def _complex_affine_combine(e1, e2):
    a1r, a1i, b1r, b1i = e1
    a2r, a2i, b2r, b2i = e2
    ar = a2r * a1r - a2i * a1i
    ai = a2r * a1i + a2i * a1r
    br = a2r * b1r - a2i * b1i + b2r
    bi = a2r * b1i + a2i * b1r + b2i
    return (ar, ai, br, bi)

def _s5_glu(u, lam_re, lam_im, log_step, b_re, b_im, c_re, c_im, d_skip, glu_w, glu_b):
    f32 = jnp.float32
    bn, t, w = u.shape
    uf = u.astype(f32).reshape(bn, t, S5_GROUPS, S5_GROUP_CH)
    lr, li = lam_re.astype(f32), lam_im.astype(f32)
    dt = jnp.exp(log_step.astype(f32))[:, None]
    mag = jnp.exp(lr * dt)
    a_re, a_im = mag * jnp.cos(li * dt), mag * jnp.sin(li * dt)
    den = lr * lr + li * li
    kap_re = ((a_re - 1.0) * lr + a_im * li) / den
    kap_im = (a_im * lr - (a_re - 1.0) * li) / den
    br, bi = b_re.astype(f32), b_im.astype(f32)
    bb_re = kap_re[..., None] * br - kap_im[..., None] * bi
    bb_im = kap_re[..., None] * bi + kap_im[..., None] * br
    bu_re = jnp.einsum('btgh,gph->btgp', uf, bb_re)
    bu_im = jnp.einsum('btgh,gph->btgp', uf, bb_im)
    a_re_t = jnp.broadcast_to(a_re, (1, t) + a_re.shape)
    a_im_t = jnp.broadcast_to(a_im, (1, t) + a_im.shape)
    _, _, s_re, s_im = lax.associative_scan(_complex_affine_combine, (a_re_t, a_im_t, bu_re, bu_im), axis=1)
    y = (jnp.einsum('gop,btgp->btgo', c_re.astype(f32), s_re)
         - jnp.einsum('gop,btgp->btgo', c_im.astype(f32), s_im)
         + d_skip.astype(f32).reshape(S5_GROUPS, S5_GROUP_CH) * uf)
    y = jax.nn.gelu(y.reshape(bn, t, w))
    return y * jax.nn.sigmoid(y @ glu_w.astype(f32) + glu_b.astype(f32))

def _hybrid_mixer(u, w_in, w_out, sinks, w_uq, w_iq, conv_w, conv_b, ig_b, fg_b, mh_norm_g,
                  lam_re, lam_im, log_step, b_re, b_im, c_re, c_im, d_skip, glu_w, glu_b,
                  slopes_a, slopes_b):
    bn, t, _ = u.shape
    f32 = jnp.float32
    z = u @ w_in
    (qa, ka, va, cq, kb, vb, ki, wi, qkc, vc, igc, fgc, oc, ud) = _split_cols(z, IN_SIZES)
    o_a = _sliding_window_sink_attention(qa.reshape(bn, t, SWA_HEADS, HEAD_DIM),
                                         ka.reshape(bn, t, SWA_KV_HEADS, HEAD_DIM),
                                         va.reshape(bn, t, SWA_KV_HEADS, HEAD_DIM), sinks, slopes_a)
    qb = (cq @ w_uq).reshape(bn, t, DSA_HEADS, HEAD_DIM)
    qi = (cq @ w_iq).reshape(bn, t, IDX_HEADS, IDX_DIM)
    o_b = _dsa_attention(qb, kb, vb, qi, ki, wi, slopes_b)
    qk = jax.nn.silu(_causal_conv(qkc, conv_w, conv_b))
    qm, km = jnp.split(qk.astype(f32), 2, axis=-1)
    h_c = _mlstm(qm.reshape(bn, t, MLSTM_HEADS, HEAD_DIM), km.reshape(bn, t, MLSTM_HEADS, HEAD_DIM),
                 vc.astype(f32).reshape(bn, t, MLSTM_HEADS, HEAD_DIM),
                 (igc + ig_b).astype(f32), (fgc + fg_b).astype(f32), mh_norm_g)
    o_c = jax.nn.sigmoid(oc.astype(f32)) * h_c
    o_d = _s5_glu(ud, lam_re, lam_im, log_step, b_re, b_im, c_re, c_im, d_skip, glu_w, glu_b)
    o = jnp.concatenate([o_a, o_b, o_c, o_d], axis=-1).astype(u.dtype)
    return o @ w_out

def setup_inputs(seed: int = 0) -> dict:
    key = jax.random.key(seed)
    ks = jax.random.split(key, 28)
    f32 = jnp.float32

    def nrm(k, shape, s):
        return jax.random.normal(k, shape, f32) * s

    L = DEPTH
    return {
        "x": nrm(ks[0], (BATCH, SEQ, D_MODEL), 1.0),
        "c": nrm(ks[1], (BATCH, D_MODEL), 1.0),
        "ada_w": nrm(ks[2], (L, D_MODEL, N_SUB * 3 * D_MODEL), D_MODEL ** -0.5),
        "ada_b": nrm(ks[3], (L, N_SUB * 3 * D_MODEL), 0.02),
        "ln_g": 1.0 + nrm(ks[4], (L, N_SUB, D_MODEL), 0.02),
        "ln_b": nrm(ks[5], (L, N_SUB, D_MODEL), 0.02),
        "ffn_w13": nrm(ks[6], (L, 2, D_MODEL, 2 * D_FF), D_MODEL ** -0.5),
        "ffn_w2": nrm(ks[7], (L, 2, D_FF, D_MODEL), BETA * D_FF ** -0.5),
        "w_in": nrm(ks[8], (L, D_MODEL, D_IN), D_MODEL ** -0.5),
        "w_out": nrm(ks[9], (L, D_MIX, D_MODEL), BETA * D_MIX ** -0.5),
        "sinks": nrm(ks[10], (L, SWA_HEADS), 0.5),
        "w_uq": nrm(ks[11], (L, DSA_Q_RANK, DSA_HEADS * HEAD_DIM), DSA_Q_RANK ** -0.5),
        "w_iq": nrm(ks[12], (L, DSA_Q_RANK, IDX_HEADS * IDX_DIM), DSA_Q_RANK ** -0.5),
        "conv_w": nrm(ks[13], (L, MLSTM_CONV, 2 * MLSTM_HEADS * HEAD_DIM), MLSTM_CONV ** -0.5),
        "conv_b": nrm(ks[14], (L, 2 * MLSTM_HEADS * HEAD_DIM), 0.02),
        "ig_b": nrm(ks[15], (L, MLSTM_HEADS), 0.1),
        "fg_b": jnp.linspace(3.0, 6.0, MLSTM_HEADS, dtype=f32)[None, :] + nrm(ks[16], (L, MLSTM_HEADS), 0.1),
        "mh_norm_g": 1.0 + nrm(ks[17], (L, MLSTM_HEADS * HEAD_DIM), 0.02),
        "lam_re": -0.5 + nrm(ks[18], (L, S5_GROUPS, S5_STATE), 0.01),
        "lam_im": jnp.pi * jnp.arange(S5_STATE, dtype=f32) + nrm(ks[19], (L, S5_GROUPS, S5_STATE), 0.01),
        "log_step": jax.random.uniform(ks[20], (L, S5_GROUPS), f32, math.log(1e-3), math.log(1e-1)),
        "b_re": nrm(ks[21], (L, S5_GROUPS, S5_STATE, S5_GROUP_CH), (2 * S5_GROUP_CH) ** -0.5),
        "b_im": nrm(ks[22], (L, S5_GROUPS, S5_STATE, S5_GROUP_CH), (2 * S5_GROUP_CH) ** -0.5),
        "c_re": nrm(ks[23], (L, S5_GROUPS, S5_GROUP_CH, S5_STATE), S5_STATE ** -0.5),
        "c_im": nrm(ks[24], (L, S5_GROUPS, S5_GROUP_CH, S5_STATE), S5_STATE ** -0.5),
        "d_skip": nrm(ks[25], (L, GROUP_WIDTH), 1.0),
        "glu_w": nrm(ks[26], (L, GROUP_WIDTH, GROUP_WIDTH), GROUP_WIDTH ** -0.5),
        "glu_b": nrm(ks[27], (L, GROUP_WIDTH), 0.02),
    }

def reference(x, c, ada_w, ada_b, ln_g, ln_b, ffn_w13, ffn_w2, w_in, w_out, sinks, w_uq, w_iq,
              conv_w, conv_b, ig_b, fg_b, mh_norm_g, lam_re, lam_im, log_step, b_re, b_im,
              c_re, c_im, d_skip, glu_w, glu_b):
    bn = x.shape[0]
    slopes = _alibi_slopes(N_SOFTMAX_HEADS)
    slopes_a, slopes_b = slopes[0::2], slopes[1::2]
    cs = jax.nn.silu(c)
    for l in range(DEPTH):
        mod = (cs @ ada_w[l] + ada_b[l]).reshape(bn, N_SUB, 3, D_MODEL)
        shift, scale, gate = mod[:, :, 0, None], mod[:, :, 1, None], mod[:, :, 2, None]
        u = x * (1.0 + scale[:, 0]) + shift[:, 0]
        y = _swiglu(u, ffn_w13[l, 0], ffn_w2[l, 0])
        x = _layer_norm(ALPHA * x + 0.5 * gate[:, 0] * y, ln_g[l, 0], ln_b[l, 0])
        u = x * (1.0 + scale[:, 1]) + shift[:, 1]
        y = _hybrid_mixer(u, w_in[l], w_out[l], sinks[l], w_uq[l], w_iq[l], conv_w[l], conv_b[l],
                          ig_b[l], fg_b[l], mh_norm_g[l], lam_re[l], lam_im[l], log_step[l],
                          b_re[l], b_im[l], c_re[l], c_im[l], d_skip[l], glu_w[l], glu_b[l],
                          slopes_a, slopes_b)
        x = _layer_norm(ALPHA * x + gate[:, 1] * y, ln_g[l, 1], ln_b[l, 1])
        u = x * (1.0 + scale[:, 2]) + shift[:, 2]
        y = _swiglu(u, ffn_w13[l, 1], ffn_w2[l, 1])
        x = _layer_norm(ALPHA * x + 0.5 * gate[:, 2] * y, ln_g[l, 2], ln_b[l, 2])
    return x


_drawn_inputs = setup_inputs


def setup_inputs(seed=0):
    import zlib

    import numpy as np

    out = dict(_drawn_inputs(seed))
    spreads = {}
    factors = {'ada_b': 2.964,
     'sinks': 21.467,
     'conv_b': 8.0,
     'ig_b': 64.0,
     'fg_b': 23.136,
     'mh_norm_g': 36.808,
     'lam_re': 64.0,
     'lam_im': 41.64,
     'log_step': 62.848,
     'b_re': 64.0,
     'b_im': 58.376,
     'c_re': 64.0,
     'c_im': 60.32,
     'glu_b': 200.0,
     'w_iq': 3.269,
     'glu_w': 5.635}
    for name, (base, spread) in spreads.items():
        noise = np.random.default_rng([zlib.crc32(name.encode()), seed]).standard_normal(out[name].shape)
        drawn = base * np.exp(spread * noise) if base else spread * noise
        out[name] = __import__('jax').numpy.asarray(drawn.astype(out[name].dtype))
    for name, factor in factors.items():
        out[name] = (out[name] * factor).astype(out[name].dtype)
    return out
```

```python
from contextlib import ExitStack

import concourse.bass as bass
from concourse import mybir

F32 = mybir.dt.float32
BF16 = mybir.dt.bfloat16
ALU = mybir.AluOpType
ACT = mybir.ActivationFunctionType
AX = mybir.AxisListType.X

P = 128
D = 1024
KT = D // P
T = 256
DEPTH = 2
D_FF = 2816
CW = 256
CHUNKS = D_FF // CW
PAIRS = CHUNKS // 2
MIX_CHUNKS = 6
GPL = 2 * CHUNKS + MIX_CHUNKS
G_MIX = CHUNKS
G_FFN2 = CHUNKS + MIX_CHUNKS
HD = 64
H = 4
N_SUB = 3
ALPHA = (2 * DEPTH) ** 0.25
LN_EPS = 1e-5
NEG = -1e30
TAKEN = -3e38
TOPK = 64
IDX_SCALE = (32 * 4) ** -0.5
SLOPES = [2.0 ** -(i + 1) for i in range(8)]
SLOPES_A, SLOPES_B = SLOPES[0::2], SLOPES[1::2]
MAGIC = 1.5 * 2.0 ** 23
INV_2PI = 0.15915494309189535
TWO_PI_1, TWO_PI_2, TWO_PI_3 = 6.28125, 1.9350051879882812e-3, 3.0198289163009303e-07
PI_BELOW = 3.1415925
GELU_C, GELU_S = 0.044715, 0.7978845608028654

C_QA, C_KA, C_VA, C_CQ, C_KB, C_VB, C_KI, C_WI, C_QK, C_VC, C_IG, C_FG, C_OC, C_UD = (
    0, 256, 384, 512, 640, 704, 768, 800, 804, 1316, 1572, 1576, 1580, 1836)
MIX_PIECES = [
    [(0, C_UD, 256), (256, C_KI, 32), (288, C_KI, 32), (320, C_KI, 32), (352, C_KI, 32), (384, C_CQ, 128)],
    [(0, C_VB, 64), (64, C_VA, 128), (192, C_WI, 4), (196, C_KB, 64), (260, C_KB, 64), (324, C_IG, 4), (328, C_FG, 4)],
    [(0, C_QK, 512)],
    [(0, C_QA, 256), (256, C_KA, 64), (320, C_KA, 64), (384, C_KA + 64, 64), (448, C_KA + 64, 64)],
    [(0, C_VC, 256)],
    [(0, C_OC, 256)],
]
OUT_TILES = [[6, 7], [2, 3], [0], [1], [4], [5]]
LOADS = [2] * CHUNKS + [len(p) for p in MIX_PIECES] + [2] * CHUNKS
LOADS_PER_LAYER = [sum(LOADS[s::2]) for s in range(2)]
LOADS_BEFORE = [sum(LOADS[g % 2:g:2]) for g in range(GPL)]

R_LNG, R_LNB, R_CW, R_CB, R_MHG, R_DS, R_GB, R_LR, R_LI, ROWS = 0, 24, 48, 64, 68, 70, 72, 74, 82, 90
PARAM_DMAS = 24

ADA_FIRST = 12
ADA_PER_LAYER = 36
TURN_ORDER = [0, 1, 4, 5, 2, 3, 6, 7]
NZ = 24


def trunk(nc, x, c, ada_w, ada_b, ln_g, ln_b, ffn_w13, ffn_w2, w_in, w_out, sinks, w_uq, w_iq,
          conv_w, conv_b, ig_b, fg_b, mh_norm_g, lam_re, lam_im, log_step, b_re, b_im, c_re, c_im,
          d_skip, glu_w, glu_b, out):
    ctx = ExitStack()
    with ctx:
        def sb(name, shape, dt=F32):
            return ctx.enter_context(nc.sbuf_tensor(name, shape, dt))

        sems = {}

        def sem(name):
            if name not in sems:
                sems[name] = ctx.enter_context(nc.semaphore(name))
            return sems[name]

        w_in_ring = [sb(f"w_in_ring{s}", [P, KT, 512]) for s in range(2)]
        w_out_ring = [sb(f"w_out_ring{s}", [P, 2, D]) for s in range(2)]
        arena = sb("arena", [P, 6144])
        ada_ring = [arena[:, s * 2304:(s + 1) * 2304].rearrange("p (t n) -> p t n", n=CW) for s in range(2)]
        h_ring = arena[:, 4608:5632].rearrange("p (s n) -> p s n", n=T)
        silu_ring = arena[:, 5632:6144].rearrange("p (s n) -> p s n", n=T)
        st_re = arena[:, 0:2048].rearrange("p (i n) -> p i n", n=T)
        st_im = arena[:, 2048:4096].rearrange("p (i n) -> p i n", n=T)
        tmp = [arena[:, 4096 + 512 * k:4608 + 512 * k] for k in range(4)]

        x_sb = sb("x_sb", [P, 2, D])
        xn = sb("xn", [P, 2, D])
        uT = sb("uT", [P, KT, T])
        oT = uT
        gate_bc = sb("gate_bc", [P, D])
        ln_bc = sb("ln_bc", [P, 2, D])
        qk_raw = ln_bc[:, 0, :].rearrange("p (t n) -> p t n", n=T)
        rows = ln_bc[0:H, 1, :].rearrange("p (t n) -> p t n", n=T)
        acc = [sb(f"acc{s}", [P, CW]) for s in range(2)]
        cos_t = sb("cos_t", [P, 8, T])
        sin_t = sb("sin_t", [P, 8, T])
        bias_a = sb("bias_a", [P, H, 384])
        dist = sb("dist", [P, 384])
        mask_b = sb("mask_b", [P, 384])
        mask_c = sb("mask_c", [P, T])
        ident = sb("ident", [P, P])
        ones = sb("ones", [P, P])
        block_mask = sb("block_mask", [P, P])
        zeros_bf = sb("zeros_bf", [1, 512], BF16)
        neg_half = sb("neg_half", [P, 8])
        c_sb = sb("c_sb", [P, 8])
        cs = sb("cs", [P, 8])
        mod = sb("mod", [P, 9 * 8])
        mod_a = sb("mod_a", [P, N_SUB, 8])
        mod_b = sb("mod_b", [P, N_SUB, 8])
        stats = sb("stats", [P, 2, 2, 6])
        mv = sb("mv", [P, 2, 2])
        var_eps = sb("var_eps", [P, 2])
        rstd = sb("rstd", [P, 2])
        nmr = sb("nmr", [P, 2])
        prow = sb("prow", [ROWS, P])
        prm = sb("prm", [P, ROWS])
        log_dt = sb("log_dt", [P, 8])
        b_raw = sb("b_raw", [P, 2, 8, 16])
        b_blk = sb("b_blk", [P, 2, 8, 32])
        c_blk = sb("c_blk", [P, 2, 2, P])
        bbT = sb("bbT", [P, 2, 2, P])
        cT = sb("cT", [P, 2, 2, P])
        glu_sb = sb("glu_sb", [P, 2, 256])
        uq_sb = sb("uq_sb", [P, 256])
        iq_sb = sb("iq_sb", [P, P])
        sinks_sb = sb("sinks_sb", [P, 2, H])
        gate_bias = sb("gate_bias", [H, 2])
        s5p = sb("s5p", [P, 24, 8])
        udT = sb("udT", [P, 2, T])
        kiT = sb("kiT", [P, T])
        cqT = sb("cqT", [P, T])
        kbT = sb("kbT", [P, T])
        qiT = sb("qiT", [P, T])
        qbT = sb("qbT", [P, 2, T])
        qaT = sb("qaT", [P, 2, T])
        kaT = sb("kaT", [P, 2, T])
        tokv = sb("tokv", [P, 2, 196])
        vaug = sb("vaug", [P, 2, H, 65])
        qkT = sb("qkT", [P, 4, T])
        sig_o = sb("sig_o", [P, 2, T])
        work_flat = sb("work_flat", [P, 4 * H * 384])
        work = [work_flat[:, k * 1536:(k + 1) * 1536].rearrange("p (h n) -> p h n", h=H) for k in range(4)]
        mask_a = work_flat[:, 1536:1920]
        qk_tanh = work_flat[:, 1536:2560]
        hs, hn = (work_flat[:, 1536 + 512 * k:2048 + 512 * k].rearrange("p (t h e) -> p t h e", t=2, h=H) for k in range(2))
        sc = sb("sc", [P, 384])
        m8 = sb("m8", [P, 2, 8])
        small = sb("small", [P, 32, 8])
        diag = work_flat[:, 5376:5888]
        PS = ctx.enter_context(nc.psum_tensor("PS", [P, 8, 512], F32))

        S5 = {n: s5p[:, k, :] for k, n in enumerate(
            ["dt", "th", "lrdt", "rho", "n", "r", "sin", "sinh", "sh2", "cos", "a_re", "a_im", "am1", "t1", "t2",
             "den", "rden", "k1", "k2", "k_re", "k3", "k4", "k_im", "r0"])}
        mx_b, nmx_b, rs_b, ri_b, mx_a, nmx_a, rs_a, ri_a, es_a, ds_a, rcol, nmcol, enm, den, dmx, rden_c, \
            s1, mu, s2, var_c, rstd_c, gb_half, t8 = (small[:, k, :] for k in range(23))

        def heads(ap):
            return ap.rearrange("p (t h) -> p t h", t=2)

        def col(r, k=0):
            return prm[:, r + k:r + k + 1]

        block = ctx.enter_context(nc.Block())

        def settle(eng):
            eng.wait_ge(sem("const_step"), 1)

        def waited(eng):
            eng.sem_inc(sem("waits_passed"), 1)

        def ring_use(l, g, it=0):
            return l * (GPL // 2) + (g // 2 + it)

        def ada_use(l, n, it_uses=0):
            return l * (ADA_PER_LAYER // 2) + (ADA_FIRST // 2 + n // 2) + it_uses

        @block.sync
        def _(sp):
            sp.dma_start(c_sb[:, :], c.rearrange("o (p t) -> p (o t)", t=8)).then_inc(sem("c_loaded"), 16)
            sp.wait_ge(sem("pad_zeroed"), 2)

            def load_ada(l, slot, layer, column, use, wait):
                if wait:
                    settle(sp)
                    sp.wait_ge(sem("acc_step"), use * 16 + (8 * slot - 8))
                sp.dma_start(ada_ring[slot][:, 0:8, :],
                             ada_w[layer, :, column].rearrange("o (p t) n -> p (o t) n", t=8)
                             ).then_inc(sem(f"ada_loaded{slot}"), 16)
                sp.dma_start(ada_ring[slot][0:1, 8, :], ada_b[layer, column]
                             ).then_inc(sem(f"ada_loaded{slot}"), 16)

            for n in range(ADA_FIRST):
                load_ada(0, n % 2, slice(0, 1), slice(n * CW, (n + 1) * CW), n // 2, n >= 2)
                if n == 1:
                    for tt in range(2):
                        sp.dma_start(x_sb[:, tt, :], x[0, tt * P:(tt + 1) * P, :]).then_inc(sem("x_loaded"), 16)

            def load_ffn(l, f, g, slot, column, use):
                sp.wait_ge(sem(f"w_in_used{slot}"), use + 1)
                waited(sp)
                for half, off in ((0, 0), (1, D_FF)):
                    cols = bass.ds(column + off, CW)
                    sp.dma_start(w_in_ring[slot][:, :, half * CW:(half + 1) * CW],
                                 ffn_w13[bass.ds(l, 1), f, :, cols].rearrange("o (t p) n -> p (o t) n", p=P)
                                 ).then_inc(sem(f"w_in_loaded{slot}"), 16)
                sp.wait_ge(sem(f"w_out_used{slot}"), use + 1)
                waited(sp)
                sp.dma_start(w_out_ring[slot][:, :, :],
                             ffn_w2[bass.ds(l, 1), f, bass.ds(column, CW), :].rearrange("o (t p) n -> p (o t) n", p=P)
                             ).then_inc(sem(f"w_out_loaded{slot}"), 16)

            def load_ln(l, s):
                for k, src in enumerate((ln_g, ln_b)):
                    sp.dma_start(ln_bc[:, k, :], src[bass.ds(l, 1), s, :].to_broadcast([P, D])
                                 ).then_inc(sem("ln_bc_loaded"), 16)

            with sp.Fori(0, DEPTH) as l:
                L = bass.ds(l, 1)
                settle(sp)
                sp.wait_ge(sem("mixer_params_used"), l + 1)
                pl = sem("params_loaded")
                for r, src in ((R_LNG, ln_g), (R_LNB, ln_b)):
                    sp.dma_start(prow[r:r + 24, :], src[L].rearrange("o s (j p) -> (o s j) p", p=P)).then_inc(pl, 16)
                sp.dma_start(prow[R_CW:R_CW + 16, :], conv_w[L].rearrange("o s (j p) -> (o s j) p", p=P)).then_inc(pl, 16)
                for r, n, src in ((R_CB, 4, conv_b), (R_MHG, 2, mh_norm_g), (R_DS, 2, d_skip), (R_GB, 2, glu_b)):
                    sp.dma_start(prow[r:r + n, :], src[L].rearrange("o (j p) -> (o j) p", p=P)).then_inc(pl, 16)
                for r, src in ((R_LR, lam_re), (R_LI, lam_im)):
                    sp.dma_start(prow[r:r + 8, :], src[L].rearrange("o (i two) p -> (o i) (two p)", two=2)).then_inc(pl, 16)
                for half in range(2):
                    sp.dma_start(log_dt[64 * half:64 * half + 64, :],
                                 log_step[L].rearrange("o (i two) -> two (o i)", two=2)[half:half + 1].to_broadcast([64, 8]),
                                 allow_slow_non_contiguous=True).then_inc(pl, 16)
                for k, src in enumerate((b_re, b_im)):
                    sp.dma_start(b_raw[:, k, :, :], src[L].rearrange("o (i two) p c -> (two p) (o i) c", two=2)).then_inc(pl, 16)
                for k, src in enumerate((c_re, c_im)):
                    for rep in range(2):
                        sp.dma_start(c_blk[:, k, :, rep * 64:(rep + 1) * 64],
                                     src[L].rearrange("o (t g) c p -> (g c) (o t) p", t=2)).then_inc(pl, 16)
                sp.dma_start(glu_sb[:, :, :], glu_w[L].rearrange("o (t p) n -> p (o t) n", p=P)).then_inc(pl, 16)
                sp.dma_start(uq_sb[:, :], w_uq[bass.ds(l, 1)].rearrange("o p n -> p (o n)")).then_inc(pl, 16)
                sp.dma_start(iq_sb[:, :], w_iq[bass.ds(l, 1)].rearrange("o p n -> p (o n)")).then_inc(pl, 16)
                for k in range(2):
                    sp.dma_start(sinks_sb[:, k, :], sinks[L].to_broadcast([P, H])).then_inc(pl, 16)
                for k, src in enumerate((ig_b, fg_b)):
                    sp.dma_start(gate_bias[:, k:k + 1], src[L].rearrange("o h -> h o")).then_inc(pl, 16)
                settle(sp)
                sp.wait_ge(sem("ln_bc_used"), l * 3 + 1)
                load_ln(l, 0)
                with sp.Fori(0, PAIRS) as it:
                    for j in range(2):
                        load_ffn(l, 0, j, j, it * 2 * CW + j * CW, ring_use(l, 0, it))
                        for a in range(2):
                            load_ada(l, a, L, bass.ds(3 * D + it * D + (2 * j + a) * CW, CW),
                                     ada_use(l, 0, it * 2 + j), True)
                load_ffn(l, 0, 10, 0, 10 * CW, ring_use(l, 10))
                for n in range(4):
                    load_ada(l, n % 2, L, slice(3 * D + 5 * D + n * CW, 3 * D + 5 * D + (n + 1) * CW),
                             ada_use(l, 20 + n), True)
                def load_mix_in(m):
                    g = G_MIX + m
                    slot = g % 2
                    sp.wait_ge(sem(f"w_in_used{slot}"), ring_use(l, g) + 1)
                    waited(sp)
                    for dst, src, w in MIX_PIECES[m]:
                        sp.dma_start(w_in_ring[slot][:, :, dst:dst + w],
                                     w_in[L, :, src:src + w].rearrange("o (t p) n -> p (o t) n", p=P)
                                     ).then_inc(sem(f"w_in_loaded{slot}"), 16)

                def load_mix_out(m):
                    g = G_MIX + m
                    slot = g % 2
                    sp.wait_ge(sem(f"w_out_used{slot}"), ring_use(l, g) + 1)
                    waited(sp)
                    t0, tn = OUT_TILES[m][0], len(OUT_TILES[m])
                    sp.dma_start(w_out_ring[slot][:, 0:tn, :],
                                 w_out[L, t0 * P:(t0 + tn) * P, :].rearrange("o (t p) n -> p (o t) n", p=P)
                                 ).then_inc(sem(f"w_out_loaded{slot}"), 16)

                for m in range(2):
                    load_mix_in(m)
                for m in range(2):
                    load_mix_out(m)
                for m in range(2, MIX_CHUNKS):
                    load_mix_in(m)
                for m in range(2, MIX_CHUNKS):
                    load_mix_out(m)
                sp.wait_ge(sem("cols_turned"), l + 1)
                sp.wait_ge(sem("g_spread"), l + 1)
                waited(sp)
                sp.wait_ge(sem("conv_step"), l * 16 + 16)
                waited(sp)
                load_ln(l, 1)
                sp.wait_ge(sem("pad_zeroed"), l * 2 + 4)
                waited(sp)
                with sp.Fori(0, PAIRS) as it:
                    for j in range(2):
                        slot = (G_FFN2 + j) % 2
                        load_ffn(l, 1, G_FFN2 + j, slot, it * 2 * CW + j * CW, ring_use(l, G_FFN2 + j, it))
                        load_ada(l, j, slice(DEPTH - 1, DEPTH), bass.ds(it * 2 * CW + j * CW, CW),
                                 ada_use(l, 24, it), True)
                load_ffn(l, 1, G_FFN2 + 10, 1, 10 * CW, ring_use(l, G_FFN2 + 10))
                for n in range(2):
                    load_ada(l, n, slice(DEPTH - 1, DEPTH), slice(10 * CW + n * CW, 11 * CW + n * CW),
                             ada_use(l, 34 + n), True)
                settle(sp)
                sp.wait_ge(sem("ln_bc_used"), l * 3 + 3)
                load_ln(l, 2)
            for tt in range(2):
                sp.wait_ge(sem("x_ready"), 2 * N_SUB * DEPTH + 1 + tt)
                sp.dma_start(out[0, tt * P:(tt + 1) * P, :], x_sb[:, tt, :]).then_inc(sem("out_stored"), 16)
            sp.wait_ge(sem("out_stored"), 32)

        @block.tensor
        def _(pe):
            for s in range(2):
                pe.sem_inc(sem(f"w_in_used{s}"), 1)
                pe.sem_inc(sem(f"w_out_used{s}"), 1)
            pe.sem_inc(sem("mixer_params_used"), 1)
            pe.wait_ge(sem("const_step"), 10)

            pe.transpose(PS[:, 4, 0:P], work[0][:, 0, 0:P], ident[:, :]).then_inc(sem("mask_turned"), 1)

            def ada_cols(chunk, base):
                for a in range(2):
                    mm = pe.matmul(PS[:, 6, 2 * base + a:2 * base + a + 1], acc[chunk][:, a * P:(a + 1) * P],
                                   ones[:, 0:1], start=True, stop=True)
                mm.then_inc(sem("ada_summed"), 1)

            def turn(src, l, s):
                for tt in range(2):
                    if s is not None:
                        pe.wait_ge(sem("xn_ready"), l * 6 + (2 * s + tt + 1))
                    for j in TURN_ORDER:
                        mm = pe.transpose(PS[:, 4 + j // 2, (j % 2) * T + tt * P:(j % 2) * T + (tt + 1) * P],
                                          src[:, tt, j * P:(j + 1) * P], ident[:, :])
                        if tt == 1:
                            mm.then_inc(sem("x_turned"), 1)

            def spread_gate(n):
                for hf in range(2):
                    pe.wait_ge(sem("diag_ready"), n * 2 + (hf + 1))
                    if hf == 1:
                        pe.wait_ge(sem("gate_ready"), n * 2 + hf)
                    pe.matmul(PS[:, 7, :], ones[:, :], diag, start=True, stop=True).then_inc(sem("gate_spread"), 1)

            def seed_y():
                for b in range(4):
                    pe.matmul(PS[:, b, :], zeros_bf[0:1, 0:P], zeros_bf[0:1, :], start=True, stop=False)

            def ffn_chunk(l, f, slot, loads, use, tile, last):
                pe.wait_ge(sem(f"w_in_loaded{slot}"), loads)
                for ft in range(2):
                    pe.wait_ge(sem("h_done"), tile + (ft + 1))
                    for half in range(2):
                        for kt in range(KT):
                            mm = pe.matmul(PS[:, 4 + ft, half * T:(half + 1) * T],
                                           w_in_ring[slot][:, kt, half * CW + ft * P:half * CW + (ft + 1) * P],
                                           uT[:, kt, :], start=(kt == 0), stop=(kt == KT - 1))
                    mm.then_inc(sem("ag_ready"), 1)
                pe.wait_ge(sem(f"w_out_loaded{slot}"), use * 16 + 16)
                for ft in range(2):
                    pe.wait_ge(sem("h_done"), tile + (ft + 3))
                    for tt in range(2):
                        for hf in range(2):
                            mm = pe.matmul(PS[:, 2 * tt + hf, :], h_ring[:, ft, tt * P:(tt + 1) * P],
                                            w_out_ring[slot][:, ft, hf * 512:(hf + 1) * 512],
                                            start=False, stop=(last and ft == 1))
                            if (ft, tt, hf) == (0, 0, 0):
                                mm.then_inc(sem(f"w_in_used{slot}"), 1)
                            elif last and ft == 1:
                                mm.then_inc(sem("y_ready"), 1)
                            elif (ft, tt, hf) == (1, 1, 1):
                                mm.then_inc(sem(f"w_out_used{slot}"), 1)

            def release_out(slot):
                pe.drain().then_inc(sem(f"w_out_used{slot}"), 1)

            def ada_sum(before, n, groups):
                pe.wait_ge(sem("acc_step"), before * 8 + 8)
                if n == 0 and groups is not None:
                    pe.wait_ge(sem("mod_ready"), groups)
                ada_cols(n % 2, n)

            for gr in range(3):
                for n in range(4):
                    ada_sum(4 * gr + n, n, gr or None)
            pe.wait_ge(sem("x_loaded"), 32)
            pe.wait_ge(sem("block_mask_ready"), 1)
            pe.wait_ge(sem("mod_ready"), 3)
            turn(x_sb, 0, None)

            with pe.Fori(0, DEPTH) as l:
                pe.wait_ge(sem("params_loaded"), (l + 1) * (16 * PARAM_DMAS))
                pe.wait_ge(sem("uT_act"), l * 12 + 4)
                pe.wait_ge(sem("uT_dve"), l * 12 + 4)
                pe.transpose(PS[:, 4, 0:ROWS], prow[:, :], ident[0:ROWS, 0:ROWS]).then_inc(sem("prm_turned"), 1)
                pe.wait_ge(sem("prm_ready"), l + 1)
                pe.wait_ge(sem("y_read"), l * 12 + 4)
                seed_y()
                with pe.Fori(0, PAIRS) as it:
                    for j in range(2):
                        ffn_chunk(l, 0, j, 16 * (l * LOADS_PER_LAYER[j] + 2 + it * 2), ring_use(l, 0, it),
                                  l * 44 + it * 4 + 2 * j, False)
                        for n in (2 * j, 2 * j + 1):
                            ada_sum(l * 36 + it * 4 + (12 + n), n, l * 12 + it + 3)
                spread_gate(l * 3)
                pe.wait_ge(sem("b_blk_ready"), l * 4 + 4)
                pe.wait_ge(sem("gate_ready"), l * 6 + 2)
                for k in range(2):
                    for t in range(2):
                        mm = pe.transpose(PS[:, 7, (2 * k + t) * P:(2 * k + t + 1) * P],
                                          b_blk[:, k, 4 * t:4 * t + 4, :].rearrange("p a b -> p (a b)"), ident[:, :])
                mm.then_inc(sem("bb_turned"), 1)
                pe.wait_ge(sem("c_blk_ready"), l * 2 + 2)
                pe.wait_ge(sem("bbT_ready"), l + 1)
                for k in range(2):
                    for t in range(2):
                        mm = pe.transpose(PS[:, 7, (2 * k + t) * P:(2 * k + t + 1) * P], c_blk[:, k, t, :], ident[:, :])
                mm.then_inc(sem("c_turned"), 1)
                ffn_chunk(l, 0, 0, 16 * (l * LOADS_PER_LAYER[0] + 12), ring_use(l, 10), l * 44 + 20, True)
                release_out(0)
                for n in range(4):
                    ada_sum(l * 36 + (32 + n), n, l * 12 + 8)
                pe.wait_ge(sem("mod_ready"), l * 12 + 9)
                pe.wait_ge(sem("h_done"), l * 44 + 24)
                pe.wait_ge(sem("cT_ready"), l + 1)
                turn(xn, l, 0)

                pe.wait_ge(sem("uT_act"), l * 12 + 8)
                pe.wait_ge(sem("uT_dve"), l * 12 + 8)
                pe.wait_ge(sem("y_read"), l * 12 + 8)
                spread_gate(l * 3 + 1)

                def z_out(n):
                    if n == 3:
                        pe.wait_ge(sem("gate_ready"), l * 6 + 4)
                    if n >= 4:
                        pe.wait_ge(sem("z_read"), l * NZ + (n - 3))
                    return PS[:, 4 + n % 4, 0:T]

                def z_feature(n, slot, c0, m=P):
                    o = z_out(n)
                    for kt in range(KT):
                        mm = pe.matmul(o[0:m, :], w_in_ring[slot][:, kt, c0:c0 + m], uT[:, kt, :],
                                       start=(kt == 0), stop=(kt == KT - 1))
                    mm.then_inc(sem("z_ready"), 1)

                def z_token(n, slot, c0, w, tt):
                    o = z_out(n)
                    for kt in range(KT):
                        mm = pe.matmul(o[:, 0:w], uT[:, kt, tt * P:(tt + 1) * P], w_in_ring[slot][:, kt, c0:c0 + w],
                                       start=(kt == 0), stop=(kt == KT - 1))
                    mm.then_inc(sem("z_ready"), 1)

                def chunk_in(m):
                    g = G_MIX + m
                    pe.wait_ge(sem(f"w_in_loaded{g % 2}"), 16 * (l * LOADS_PER_LAYER[g % 2] + LOADS_BEFORE[g] + LOADS[g]))

                def chunk_done(m):
                    pe.drain().then_inc(sem(f"w_in_used{(G_MIX + m) % 2}"), 1)

                def s5_inputs(b):
                    if b >= 2:
                        pe.wait_ge(sem("bu_read"), l * 4 + (b - 1))
                    for k in range(2):
                        i = 2 * b + k
                        q, t = i % 4, i // 4
                        for ri in range(2):
                            mm = pe.matmul(PS[:, 2 * (b % 2) + k, ri * T:(ri + 1) * T],
                                           bbT[32 * q:32 * q + 32, ri, t, :], udT[32 * q:32 * q + 32, t, :],
                                           start=True, stop=True)
                    mm.then_inc(sem("bu_ready"), 1)

                def scores(q_of, k_of, rows_of, signal):
                    for h in range(H):
                        r = rows_of(h)
                        for tt, w in ((0, P), (1, T)):
                            mm = pe.matmul(PS[:, h, (0, P)[tt]:(0, P)[tt] + w], q_of(h)[r, tt * P:(tt + 1) * P],
                                           k_of(h)[r, 0:w], start=True, stop=True)
                    mm.then_inc(sem(signal), 1)

                def half(h):
                    return slice(64 * (h % 2), 64 * (h % 2) + 64)

                chunk_in(0)
                s0, s1_ = G_MIX % 2, (G_MIX + 1) % 2
                z_feature(0, s0, 0)
                z_feature(1, s0, 128)
                pe.wait_ge(sem("z_read"), l * NZ + 2)
                s5_inputs(0)
                s5_inputs(1)
                z_feature(2, s0, 256)
                z_feature(3, s0, 384)
                chunk_done(0)
                chunk_in(1)
                for tt in range(2):
                    z_token(4 + tt, s1_, 0, 196, tt)
                z_feature(6, s1_, 196)
                z_feature(7, s1_, 324, H)
                z_feature(8, s1_, 328, H)
                chunk_done(1)
                s5_inputs(2)
                for n, w in ((9, iq_sb[:, :]), (10, uq_sb[:, 0:P]), (11, uq_sb[:, P:2 * P])):
                    pe.matmul(z_out(n), w, cqT[:, :], start=True, stop=True).then_inc(sem("z_ready"), 1)
                s5_inputs(3)
                chunk_in(2)
                for t in range(2):
                    z_feature(12 + t, s0, t * P)
                pe.wait_ge(sem("z_read"), l * NZ + 12)
                pe.wait_ge(sem("bu_read"), l * 4 + 4)
                scores(lambda h: qiT, lambda h: kiT, lambda h: slice(32 * h, 32 * h + 32), "idx_ready")
                for t in range(2, 4):
                    z_feature(12 + t, s0, t * P)
                chunk_done(2)
                pe.wait_ge(sem("idx_read"), l + 1)
                scores(lambda h: qbT[:, h // 2, :], lambda h: kbT, half, "sb_ready")
                chunk_in(3)
                for t in range(4):
                    z_feature(16 + t, s1_, t * P)
                chunk_done(3)
                chunk_in(4)
                for tt in range(2):
                    z_token(20 + tt, s0, 0, T, tt)
                chunk_done(4)
                pe.wait_ge(sem("sb_read"), l + 1)
                pe.wait_ge(sem("z_read"), l * NZ + 20)
                scores(lambda h: qaT[:, h // 2, :], lambda h: kaT[:, h // 2, :], half, "sa_ready")
                chunk_in(5)
                for t in range(2):
                    z_feature(22 + t, s1_, t * P)
                chunk_done(5)
                pe.wait_ge(sem("z_read"), l * NZ + NZ)

                def turn_probs(src, signal):
                    for b, c0 in enumerate((0, P, 2 * P)):
                        for h in range(H):
                            mm = pe.transpose(PS[:, 4 + b, h * P:(h + 1) * P], src[:, h, c0:c0 + P], ident[:, :])
                        mm.then_inc(sem(signal), 1)

                def mix_values(pt, v_of, bank):
                    for h in range(H):
                        o = PS[half(h), bank, (h // 2) * T:(h // 2 + 1) * T]
                        ptv = pt[:, :, :].rearrange("p h n -> p (h n)")
                        mm = pe.matmul(o[:, 0:P], v_of(0, h), ptv[:, h * P:(h + 1) * P], start=True, stop=True)
                        for kt in range(2):
                            mm = pe.matmul(o[:, P:T], v_of(kt, h), ptv[:, 512 * (kt + 1) + h * P:512 * (kt + 1) + (h + 1) * P],
                                           start=(kt == 0), stop=(kt == 1))
                    return mm

                pe.wait_ge(sem("rotated_out"), l * 8 + 8)
                for i in range(8):
                    q, t = i % 4, i // 4
                    for ri, st in ((0, st_re), (1, st_im)):
                        mm = pe.matmul(PS[32 * q:32 * q + 32, 7, t * T:(t + 1) * T], cT[:, ri, t, 32 * q:32 * q + 32],
                                       st[:, i, :], start=(ri == 0), stop=(ri == 1))
                mm.then_inc(sem("yd_ready"), 1)
                pe.wait_ge(sem("pb_ready"), l * 2 + 2)
                turn_probs(work[0], "ptb_turned")
                pe.wait_ge(sem("ptb_ready"), l * 3 + 3)
                mix_values(work[1], lambda kt, h: tokv[:, kt, 0:64], 4).then_inc(sem("ob_ready"), 1)
                pe.wait_ge(sem("pa_ready"), l * 2 + 2)
                pe.wait_ge(sem("ob_read"), l + 1)
                turn_probs(work[2], "pta_turned")
                pe.wait_ge(sem("yg_ready"), l + 1)
                for t in range(2):
                    for kt in range(2):
                        mm = pe.matmul(PS[:, 7, t * T:(t + 1) * T], glu_sb[:, kt, t * P:(t + 1) * P],
                                       tmp[3][:, kt * T:(kt + 1) * T], start=(kt == 0), stop=(kt == 1))
                mm.then_inc(sem("glu_ready"), 1)
                pe.wait_ge(sem("pta_ready"), l * 3 + 3)
                mix_values(work[3], lambda kt, h: tokv[:, kt, 64 + 64 * (h // 2):128 + 64 * (h // 2)], 4
                           ).then_inc(sem("oa_ready"), 1)
                settle(pe)
                pe.wait_ge(sem("rows_ready"), l * 2 + 2)
                for k in range(2):
                    for tt in range(2):
                        mm = pe.transpose(PS[:, 6, (2 * k + tt) * 4:(2 * k + tt) * 4 + 4],
                                          rows[:, (2, 3)[k], tt * P:(tt + 1) * P], ident[0:H, 0:H])
                mm.then_inc(sem("cols_turned"), 1)
                pe.wait_ge(sem("oa_read"), l + 1)
                for h in range(H):
                    mm = pe.matmul(PS[:, 4 + h // 2, (h % 2) * T:(h % 2 + 1) * T], ident[0:H, h:h + 1].to_broadcast([H, P]),
                                   rows[:, 1, :], start=True, stop=True)
                mm.then_inc(sem("g_spread"), 1)

                def y_chunk(m):
                    g = G_MIX + m
                    pe.wait_ge(sem(f"w_out_loaded{g % 2}"), ring_use(l, g) * 16 + 16)
                    for k, kt in enumerate(OUT_TILES[m]):
                        for b in range(4):
                            tt, hf = b // 2, b % 2
                            mm = pe.matmul(PS[:, b, :], oT[:, kt, tt * P:(tt + 1) * P],
                                           w_out_ring[g % 2][:, k, hf * 512:(hf + 1) * 512],
                                           start=False, stop=(m == 5))
                            if m == 5:
                                mm.then_inc(sem("y_ready"), 1)
                    pe.drain().then_inc(sem(f"w_out_used{g % 2}"), 1)

                pe.wait_ge(sem("sa_read"), l + 1)
                seed_y()
                pe.wait_ge(sem("od_ready"), l + 1)
                y_chunk(0)
                pe.wait_ge(sem("w_args_ready"), l + 1)
                pe.wait_ge(sem("cols_ready"), l * 2 + 2)
                pe.wait_ge(sem("qk_ready"), l + 1)
                for h in range(H):
                    for s_t, w in ((0, T), (1, P)):
                        mm = pe.matmul(PS[:, 4 + h, (0, T)[s_t]:(0, T)[s_t] + w],
                                       qkT[half(h), 2 + h // 2, s_t * P:(s_t + 1) * P], qkT[half(h), h // 2, T - w:T],
                                       start=True, stop=True)
                mm.then_inc(sem("st_ready"), 1)
                y_chunk(1)
                pe.wait_ge(sem("pc_ready"), l + 1)
                for tt in range(2):
                    for h in range(H):
                        o = PS[:, 4 + tt, h * 65:(h + 1) * 65]
                        mm = pe.matmul(o, work[0][:, h, tt * P:(tt + 1) * P], vaug[:, 0, h, :], start=True, stop=(tt == 0))
                        if tt == 1:
                            mm = pe.matmul(o, work[0][:, h, T:T + P], vaug[:, 1, h, :], start=False, stop=True)
                mm.then_inc(sem("num_ready"), 1)
                y_chunk(2)
                y_chunk(3)
                pe.wait_ge(sem("hn_ready"), l + 1)
                for pr in range(2):
                    for tt in range(2):
                        mm = pe.transpose(PS[:, 6, pr * T + tt * P:pr * T + (tt + 1) * P],
                                          hn[:, tt, 2 * pr:2 * pr + 2, :].rearrange("p h e -> p (h e)"), ident[:, :])
                mm.then_inc(sem("hn_turned"), 1)
                pe.wait_ge(sem("oc_ready"), l * 2 + 2)
                y_chunk(4)
                y_chunk(5)
                pe.drain().then_inc(sem("mixer_params_used"), 1)
                turn(xn, l, 1)

                pe.wait_ge(sem("uT_act"), l * 12 + 12)
                pe.wait_ge(sem("uT_dve"), l * 12 + 12)
                pe.wait_ge(sem("y_read"), l * 12 + 12)
                seed_y()
                with pe.Fori(0, PAIRS) as it:
                    for j in range(2):
                        g = G_FFN2 + j
                        ffn_chunk(l, 1, g % 2, 16 * (l * LOADS_PER_LAYER[g % 2] + (LOADS_BEFORE[g] + 2) + it * 2),
                                  ring_use(l, g, it), l * 44 + (22 + 2 * j) + it * 4, False)
                        ada_sum(l * 36 + it * 2 + (36 + j), j, l * 12 + it + 9)
                spread_gate(l * 3 + 2)
                g = G_FFN2 + 10
                ffn_chunk(l, 1, 1, 16 * (l * LOADS_PER_LAYER[1] + (LOADS_BEFORE[g] + 2)), ring_use(l, g), l * 44 + 42, True)
                release_out(1)
                for n in range(2):
                    ada_sum(l * 36 + (46 + n), n, l * 12 + 14)
                pe.wait_ge(sem("mod_ready"), l * 12 + 15)
                pe.wait_ge(sem("h_done"), l * 44 + 46)
                pe.wait_ge(sem("gate_ready"), l * 6 + 6)
                turn(xn, l, 2)

        @block.vector
        def _(v):
            v.sem_inc(sem("h_done"), 2)
            v.wait_ge(sem("const_step"), 19)
            v.scalar_tensor_tensor(dist[:, :], dist[:, :], -1.0, dist[:, :], ALU.mult, ALU.max).then_inc(sem("dist_ready"), 1)
            v.wait_ge(sem("dist_ready"), 1)
            for h in range(H):
                v.scalar_tensor_tensor(bias_a[:, h, :], dist[:, :], -SLOPES_A[h], mask_a, ALU.mult, ALU.add
                                       ).then_inc(sem("bias_a_ready"), 1)
            v.wait_ge(sem("mask_turned"), 1)
            v.tensor_copy(block_mask[:, :], PS[:, 4, 0:P]).then_inc(sem("block_mask_ready"), 1)
            v.memset(b_blk[:, :, :, :], 0.0)
            v.memset(cos_t[:, :, 0:1], 1.0).then_inc(sem("rot_start"), 1)
            v.memset(sin_t[:, :, 0:1], 0.0).then_inc(sem("rot_start"), 1)
            v.memset(vaug[:, :, :, 64:65], 1.0).then_inc(sem("vaug_ones"), 1)

            def ada_chunk(slot, loaded, n, first=False):
                v.wait_ge(sem(f"ada_loaded{slot}"), loaded)
                if not first:
                    v.wait_ge(sem("ada_summed"), n - 1)
                w = ada_ring[slot]
                for t in range(8):
                    if t:
                        v.wait_ge(sem("acc_step"), n * 8 + t)
                    ins = v.scalar_tensor_tensor(acc[slot][:, :], w[:, t, :], cs[:, t:t + 1],
                                                 w[:, 8, :] if t == 0 else acc[slot][:, :], ALU.mult, ALU.add)
                    ins.then_inc(sem("acc_step"), 1)

            def mod_cols(dst, width, summed):
                v.wait_ge(sem("ada_summed"), summed)
                v.tensor_copy(mod[:, dst], PS[:, 6, 0:width]).then_inc(sem("mod_ready"), 1)

            def mod_ab(s, lng, n, mods):
                v.wait_ge(sem("mod_ready"), mods)
                sh, scl = mod[:, 24 * s:24 * s + 8], mod[:, 24 * s + 8:24 * s + 16]
                if lng is None:
                    v.tensor_scalar(mod_a[:, s, :], scl, 1.0, None, ALU.add).then_inc(sem("mod_step"), 1)
                    v.tensor_copy(mod_b[:, s, :], sh).then_inc(sem("mod_step"), 1)
                    v.tensor_copy(t8, sh).then_inc(sem("mod_step"), 1)
                else:
                    g, b = prm[:, R_LNG + 8 * lng:R_LNG + 8 * lng + 8], prm[:, R_LNB + 8 * lng:R_LNB + 8 * lng + 8]
                    v.scalar_tensor_tensor(mod_a[:, s, :], scl, 1.0, g, ALU.add, ALU.mult).then_inc(sem("mod_step"), 1)
                    v.wait_ge(sem("mod_step"), n * 3)
                    v.scalar_tensor_tensor(t8, scl, 1.0, b, ALU.add, ALU.mult).then_inc(sem("mod_step"), 1)
                    v.wait_ge(sem("mod_step"), n * 3 + 2)
                    v.tensor_tensor(mod_b[:, s, :], t8, sh, ALU.add).then_inc(sem("mod_step"), 1)

            def evac_uT(s, turned, ab):
                v.wait_ge(sem("mod_step"), ab * 3)
                for j in range(4, KT):
                    if j % 2 == 0:
                        v.wait_ge(sem("x_turned"), turned + (TURN_ORDER.index(j + 1) + 1))
                    v.tensor_scalar(uT[:, j, :], PS[:, 4 + j // 2, (j % 2) * T:(j % 2 + 1) * T], mod_a[:, s, j:j + 1], mod_b[:, s, j:j + 1],
                                    ALU.mult, ALU.add).then_inc(sem("uT_dve"), 1)

            def gate_diag(s, n):
                for hf in range(2):
                    if hf:
                        v.wait_ge(sem("gate_spread"), n * 2 + 1)
                    k = 24 * s + 16 + 4 * hf
                    v.tensor_tensor(diag.rearrange("p (a b) -> p a b", a=4), ident[:, :].unsqueeze(1).to_broadcast([P, 4, P]),
                                    mod[:, k:k + 4].unsqueeze(2).to_broadcast([P, 4, P]), ALU.mult
                                    ).then_inc(sem("diag_ready"), 1)

            def ffn_tile(ft, tile):
                v.wait_ge(sem("silu_ready"), tile + (ft + 1))
                v.tensor_tensor(h_ring[:, ft, :], silu_ring[:, ft, :], PS[:, 4 + ft, T:2 * T], ALU.mult
                                ).then_inc(sem("h_done"), 1)

            def deepnorm(l, s):
                n = l * 3 + s
                v.wait_ge(sem("gate_ready"), n * 2 + 2)
                v.wait_ge(sem("x_ready"), n * 2 + 2)
                for tt in range(2):
                    for hf in range(2):
                        b = 2 * tt + hf
                        v.wait_ge(sem("y_ready"), n * 4 + (b + 1))
                        v.tensor_tensor(xn[:, tt, hf * 512:(hf + 1) * 512], PS[:, b, :], gate_bc[:, hf * 512:(hf + 1) * 512],
                                        ALU.mult).then_inc(sem("y_read"), 1)
                    for hf in range(2):
                        b = 2 * tt + hf
                        v.wait_ge(sem("y_read"), n * 4 + (b + 5))
                        v.scalar_tensor_tensor(xn[:, tt, hf * 512:(hf + 1) * 512], x_sb[:, tt, hf * 512:(hf + 1) * 512], ALPHA,
                                               xn[:, tt, hf * 512:(hf + 1) * 512], ALU.mult, ALU.add
                                               ).then_inc(sem("r_ready"), 1)
                    for hf in range(2):
                        v.wait_ge(sem("r_ready"), n * 4 + (2 * tt + hf + 1))
                        v.bn_stats(stats[:, tt, hf, :], xn[:, tt, hf * 512:(hf + 1) * 512]).then_inc(sem("stats_ready"), 1)
                    settle(v)
                    v.wait_ge(sem("stats_ready"), n * 4 + (2 * tt + 2))
                    v.bn_aggr(mv[:, tt, :], stats[:, tt, :, :].rearrange("p a b -> p (a b)")).then_inc(sem("mv_ready"), 1)
                    v.wait_ge(sem("mv_ready"), n * 2 + (tt + 1))
                    v.tensor_scalar(var_eps[:, tt:tt + 1], mv[:, tt, 1:2], LN_EPS, None, ALU.add).then_inc(sem("var_ready"), 1)
                for tt in range(2):
                    v.wait_ge(sem("rstd_ready"), n * 2 + (tt + 1))
                    v.tensor_scalar(nmr[:, tt:tt + 1], mv[:, tt, 0:1], rstd[:, tt:tt + 1], -1.0, ALU.mult, ALU.mult
                                    ).then_inc(sem("nmr_ready"), 1)
                    v.wait_ge(sem("nmr_ready"), n * 2 + (tt + 1))
                    v.tensor_scalar(xn[:, tt, :], xn[:, tt, :], rstd[:, tt:tt + 1], nmr[:, tt:tt + 1], ALU.mult, ALU.add
                                    ).then_inc(sem("xn_ready"), 1)

            v.sem_inc(sem("y_read"), 4)
            v.wait_ge(sem("cs_ready"), 1)
            for gr in range(3):
                for n in range(4):
                    k = 4 * gr + n
                    ada_chunk(n % 2, 32 * (k // 2 + 1), k, first=k < 2)
                mod_cols(slice(8 * gr, 8 * gr + 8), 8, 4 * gr + 4)
            mod_ab(0, None, 0, 3)
            evac_uT(0, 0, 1)

            with v.Fori(0, DEPTH) as l:
                v.wait_ge(sem("prm_turned"), l + 1)
                v.tensor_copy(prm[:, :], PS[:, 4, 0:ROWS]).then_inc(sem("prm_ready"), 1)
                v.wait_ge(sem("prm_ready"), l + 1)
                step = [0]
                STEPS = 27

                def s5(ins):
                    ins.then_inc(sem("s5_step"), 1)
                    step[0] += 1
                    v.wait_ge(sem("s5_step"), l * STEPS + step[0])

                lr, li = prm[:, R_LR:R_LR + 8], prm[:, R_LI:R_LI + 8]
                v.wait_ge(sem("dt_ready"), l + 1)
                v.tensor_tensor(S5["lrdt"], lr, S5["dt"], ALU.mult).then_inc(sem("lrdt_ready"), 1)
                s5(v.tensor_tensor(S5["th"], li, S5["dt"], ALU.mult))
                s5(v.tensor_scalar(S5["n"], S5["th"], INV_2PI, MAGIC, ALU.mult, ALU.add))
                s5(v.tensor_scalar(S5["n"], S5["n"], MAGIC, None, ALU.subtract))
                s5(v.scalar_tensor_tensor(S5["r"], S5["n"], -TWO_PI_1, S5["th"], ALU.mult, ALU.add))
                s5(v.scalar_tensor_tensor(S5["r"], S5["n"], -TWO_PI_2, S5["r"], ALU.mult, ALU.add))
                s5(v.scalar_tensor_tensor(S5["r"], S5["n"], -TWO_PI_3, S5["r"], ALU.mult, ALU.add))
                v.tensor_scalar(S5["r0"], S5["r"], PI_BELOW, -PI_BELOW, ALU.min, ALU.max).then_inc(sem("angle_ready"), 1)
                v.wait_ge(sem("sin_ready"), l + 1)
                s5(v.tensor_tensor(S5["sh2"], S5["sinh"], S5["sinh"], ALU.mult))
                s5(v.tensor_scalar(S5["cos"], S5["sh2"], -2.0, 1.0, ALU.mult, ALU.add))
                v.tensor_copy(cos_t[:, :, 1:2], S5["cos"].unsqueeze(2)).then_inc(sem("rot_start"), 1)
                v.tensor_copy(sin_t[:, :, 1:2], S5["sin"].unsqueeze(2)).then_inc(sem("rot_start"), 1)
                s5(v.tensor_tensor(S5["a_re"], S5["rho"], S5["cos"], ALU.mult))
                s5(v.tensor_tensor(S5["a_im"], S5["rho"], S5["sin"], ALU.mult))
                s5(v.tensor_scalar(S5["am1"], S5["a_re"], 1.0, None, ALU.subtract))
                s5(v.tensor_tensor(S5["t1"], lr, lr, ALU.mult))
                s5(v.tensor_tensor(S5["t2"], li, li, ALU.mult))
                s5(v.tensor_tensor(S5["den"], S5["t1"], S5["t2"], ALU.add))
                s5(v.reciprocal(S5["rden"], S5["den"]))
                s5(v.tensor_tensor(S5["k1"], S5["am1"], lr, ALU.mult))
                s5(v.tensor_tensor(S5["k2"], S5["a_im"], li, ALU.mult))
                s5(v.tensor_tensor(S5["k1"], S5["k1"], S5["k2"], ALU.add))
                s5(v.tensor_tensor(S5["k_re"], S5["k1"], S5["rden"], ALU.mult))
                s5(v.tensor_tensor(S5["k3"], S5["a_im"], lr, ALU.mult))
                s5(v.tensor_tensor(S5["k4"], S5["am1"], li, ALU.mult))
                s5(v.tensor_tensor(S5["k3"], S5["k3"], S5["k4"], ALU.subtract))
                s5(v.tensor_tensor(S5["k_im"], S5["k3"], S5["rden"], ALU.mult))
                kre = S5["k_re"].unsqueeze(2).to_broadcast([P, 8, 16])
                kim = S5["k_im"].unsqueeze(2).to_broadcast([P, 8, 16])
                bt = [work[3][:, 0, k * P:(k + 1) * P].rearrange("p (i c) -> p i c", c=16) for k in range(3)] + \
                     [work[3][:, 1, 0:P].rearrange("p (i c) -> p i c", c=16)]
                s5(v.tensor_tensor(bt[0], b_raw[:, 0, :, :], kre, ALU.mult))
                s5(v.tensor_tensor(bt[1], b_raw[:, 1, :, :], kim, ALU.mult))
                s5(v.tensor_tensor(bt[2], b_raw[:, 1, :, :], kre, ALU.mult))
                s5(v.tensor_tensor(bt[3], b_raw[:, 0, :, :], kim, ALU.mult))
                for two_ in range(2):
                    ph = slice(64 * two_, 64 * two_ + 64)
                    v.tensor_tensor(b_blk[ph, 0, :, 16 * two_:16 * two_ + 16], bt[0][ph], bt[1][ph], ALU.subtract
                                    ).then_inc(sem("b_blk_ready"), 1)
                    v.tensor_tensor(b_blk[ph, 1, :, 16 * two_:16 * two_ + 16], bt[2][ph], bt[3][ph], ALU.add
                                    ).then_inc(sem("b_blk_ready"), 1)
                for k, sign in ((0, 1.0), (1, -1.0)):
                    v.scalar_tensor_tensor(c_blk[:, k, :, :], c_blk[:, k, :, :], sign,
                                           block_mask[:, :].unsqueeze(1).to_broadcast([P, 2, P]), ALU.mult, ALU.mult
                                           ).then_inc(sem("c_blk_ready"), 1)
                assert step[0] == STEPS

                with v.Fori(0, PAIRS) as it:
                    for j in range(2):
                        for ft in range(2):
                            ffn_tile(ft, l * 44 + it * 4 + 2 * j)
                            n = 2 * j + ft
                            ada_chunk(ft, 32 * (ada_use(l, 0, it * 2 + j) + 1), l * 36 + it * 4 + (12 + n))
                    mod_cols(bass.ds(24 + it * 8, 8), 8, l * 36 + it * 4 + 16)
                gate_diag(0, l * 3)
                v.wait_ge(sem("bb_turned"), l + 1)
                v.tensor_copy(bbT[:, :, :, :].rearrange("p a b c -> p (a b c)"), PS[:, 7, :]).then_inc(sem("bbT_ready"), 1)
                v.wait_ge(sem("c_turned"), l + 1)
                v.tensor_copy(cT[:, :, :, :].rearrange("p a b c -> p (a b c)"), PS[:, 7, :]).then_inc(sem("cT_ready"), 1)
                for ft in range(2):
                    ffn_tile(ft, l * 44 + 20)
                    for n in (2 * ft, 2 * ft + 1):
                        ada_chunk(n % 2, 32 * (ada_use(l, 20 + n) + 1), l * 36 + (32 + n))
                mod_cols(slice(64, 72), 8, l * 36 + 36)
                mod_ab(1, 0, l * 3 + 1, l * 12 + 9)
                mod_ab(2, 1, l * 3 + 2, l * 12 + 9)
                deepnorm(l, 0)
                evac_uT(1, l * 24 + 8, l * 3 + 2)

                gate_diag(1, l * 3 + 1)

                def tiles2(ap):
                    return ap.rearrange("p (a b) -> p a b", a=2)

                def s5_rotate_in(b):
                    v.wait_ge(sem("bu_ready"), l * 4 + (b + 1))
                    if b >= 2:
                        v.wait_ge(sem("rotated_in"), l * 8 + 2 * (b - 1))
                    tl = slice(2 * b, 2 * b + 2)
                    bk = 2 * (b % 2)
                    re, im = PS[:, bk:bk + 2, 0:T], PS[:, bk:bk + 2, T:2 * T]
                    v.tensor_tensor(st_re[:, tl, :], re, cos_t[:, tl, :], ALU.mult)
                    v.tensor_tensor(tiles2(tmp[2 * (b % 2)]), im, sin_t[:, tl, :], ALU.mult)
                    v.tensor_tensor(st_im[:, tl, :], im, cos_t[:, tl, :], ALU.mult)
                    v.tensor_tensor(tiles2(tmp[2 * (b % 2) + 1]), re, sin_t[:, tl, :], ALU.mult).then_inc(sem("bu_read"), 1)

                def s5_scan(b):
                    v.wait_ge(sem("rotated_in"), l * 8 + 2 * (b + 1))
                    for i in (2 * b, 2 * b + 1):
                        for st in (st_re, st_im):
                            ins = v.tensor_tensor_scan(st[:, i, :], S5["rho"][:, i:i + 1].to_broadcast([P, T]), st[:, i, :],
                                                       0.0, ALU.mult, ALU.add)
                    ins.then_inc(sem("scanned"), 1)

                def s5_rotate_out(b):
                    v.wait_ge(sem("scanned"), l * 4 + (b + 1))
                    v.wait_ge(sem("rotated_in"), l * 8 + 8)
                    if b:
                        v.wait_ge(sem("rotated_out"), l * 8 + 2 * b)
                    tl = slice(2 * b, 2 * b + 2)
                    v.tensor_tensor(tiles2(tmp[0]), st_re[:, tl, :], cos_t[:, tl, :], ALU.mult)
                    v.tensor_tensor(tiles2(tmp[1]), st_im[:, tl, :], sin_t[:, tl, :], ALU.mult)
                    v.tensor_tensor(tiles2(tmp[2]), st_re[:, tl, :], sin_t[:, tl, :], ALU.mult)
                    v.tensor_tensor(tiles2(tmp[3]), st_im[:, tl, :], cos_t[:, tl, :], ALU.mult).then_inc(sem("rotating_out"), 1)

                v.wait_ge(sem("rot_step"), l * 48 + 48)
                s5_rotate_in(0)
                s5_rotate_in(1)
                s5_scan(0)
                s5_rotate_in(2)
                s5_scan(1)
                s5_rotate_in(3)
                s5_scan(2)
                v.wait_ge(sem("gate_spread"), l * 6 + 4)
                v.wait_ge(sem("ln_f_ready"), l + 1)
                lf, bsum, gmx = (work[3][0:H, k, 0:T] for k in (1, 2, 3))
                v.scalar_tensor_tensor(lf, rows[:, 1, :], 0.0, lf, ALU.min, ALU.subtract).then_inc(sem("lf_ready"), 1)
                s5_scan(3)
                v.wait_ge(sem("lf_ready"), l + 1)
                v.tensor_tensor_scan(bsum, ones[0:H, 0:1].to_broadcast([H, T]), lf, 0.0, ALU.mult, ALU.add
                                     ).then_inc(sem("bsum_ready"), 1)
                v.wait_ge(sem("bsum_ready"), l + 1)
                v.tensor_tensor(rows[:, 2, :], rows[:, 0, :], bsum, ALU.subtract).then_inc(sem("r_row_ready"), 1)
                v.wait_ge(sem("r_row_ready"), l + 1)
                v.tensor_tensor_scan(gmx, ones[0:H, 0:1].to_broadcast([H, T]), rows[:, 2, :], 0.0, ALU.mult, ALU.max
                                     ).then_inc(sem("gmx_ready"), 1)
                v.wait_ge(sem("gmx_ready"), l + 1)
                v.tensor_scalar(rows[:, 1, :], gmx, -1.0, None, ALU.mult).then_inc(sem("rows_ready"), 1)
                v.scalar_tensor_tensor(rows[:, 3, :], bsum, -1.0, gmx, ALU.mult, ALU.subtract).then_inc(sem("rows_ready"), 1)

                v.wait_ge(sem("idx_read"), l + 1)
                for h in range(H):
                    if h:
                        v.wait_ge(sem("idx_sum"), l * 8 + 2 * h)
                    for tt, cols in ((0, slice(0, P)), (1, slice(P, 384))):
                        w = tokv[:, tt, 192 + h:193 + h]
                        src = work[0][:, h, cols]
                        if h == 0:
                            v.tensor_scalar(sc[:, cols], src, w, None, ALU.mult).then_inc(sem("idx_sum"), 1)
                        else:
                            v.scalar_tensor_tensor(sc[:, cols], src, w, sc[:, cols], ALU.mult, ALU.add
                                                   ).then_inc(sem("idx_sum"), 1)
                v.wait_ge(sem("idx_sum"), l * 8 + 8)
                v.scalar_tensor_tensor(sc[:, :], sc[:, :], IDX_SCALE, mask_b[:, :], ALU.mult, ALU.add
                                       ).then_inc(sem("idx_score"), 1)
                settle(v)
                v.wait_ge(sem("idx_score"), l + 1)
                for k in range(TOPK // 8):
                    for tt, cols in ((0, slice(0, P)), (1, slice(P, 384))):
                        if k:
                            settle(v)
                            v.wait_ge(sem("top_taken"), l * 16 + (2 * (k - 1) + tt + 1))
                        v.max(m8[:, tt, :], sc[:, cols]).then_inc(sem("top_found"), 1)
                    for tt, cols in ((0, slice(0, P)), (1, slice(P, 384))):
                        v.wait_ge(sem("top_found"), l * 16 + (2 * k + tt + 1))
                        waited(v)
                        v.match_replace(sc[:, cols], m8[:, tt, :], sc[:, cols], TAKEN).then_inc(sem("top_taken"), 1)
                    if k % 2:
                        s5_rotate_out(k // 2)
                v.wait_ge(sem("top_taken"), l * 16 + 16)
                v.tensor_scalar(sc[:, :], sc[:, :], TAKEN / 2, NEG, ALU.is_gt, ALU.mult).then_inc(sem("sel_step"), 1)
                v.wait_ge(sem("sel_step"), l * 2 + 1)
                v.tensor_tensor(sc[:, :], sc[:, :], mask_b[:, :], ALU.add).then_inc(sem("sel_step"), 1)
                v.wait_ge(sem("sel_step"), l * 2 + 2)
                for h in range(H):
                    v.scalar_tensor_tensor(work[1][:, h, :], dist[:, :], -SLOPES_B[h], sc[:, :], ALU.mult, ALU.add
                                           ).then_inc(sem("bias_b"), 1)

                def logits(bias, dst, ready, read, mx, nmx, name, sink):
                    v.wait_ge(sem(ready), l + 1)
                    v.scalar_tensor_tensor(dst[:, :, :], PS[:, 0:4, 0:384], HD ** -0.5, bias[:, :, :], ALU.mult, ALU.add
                                           ).then_inc(sem(read), 1)
                    v.wait_ge(sem(read), l + 1)
                    for tt, cols in ((0, slice(0, P)), (1, slice(P, 384))):
                        v.tensor_reduce(heads(mx)[:, tt, :], dst[:, :, cols], AX, ALU.max).then_inc(sem(name + "_max"), 1)
                    v.wait_ge(sem(name + "_max"), l * 2 + 2)
                    if sink is not None:
                        v.tensor_tensor(mx, mx, sink, ALU.max).then_inc(sem(name + "_smax"), 1)
                        v.wait_ge(sem(name + "_smax"), l + 1)
                    v.tensor_scalar(nmx, mx, -1.0, None, ALU.mult).then_inc(sem(name + "_nmax"), 1)

                v.wait_ge(sem("bias_b"), l * 4 + 4)
                logits(work[1], work[0], "sb_ready", "sb_read", mx_b, nmx_b, "b", None)

                v.wait_ge(sem("z_read"), l * NZ + 16)
                for j in range(3, -1, -1):
                    lag = 3 - j
                    for t in range(4):
                        w = col(R_CW, 4 * j + t)
                        if lag == 0:
                            v.tensor_scalar(qkT[:, t, :], qk_raw[:, t, :], w, col(R_CB, t), ALU.mult, ALU.add
                                            ).then_inc(sem("conv_step"), 1)
                        else:
                            v.wait_ge(sem("conv_step"), l * 16 + (4 * (lag - 1) + t + 1))
                            v.scalar_tensor_tensor(qkT[:, t, lag:T], qk_raw[:, t, 0:T - lag], w, qkT[:, t, lag:T],
                                                   ALU.mult, ALU.add).then_inc(sem("conv_step"), 1)

                v.wait_ge(sem("b_exp"), l * 8 + 8)
                v.reciprocal(ri_b, rs_b).then_inc(sem("rib_ready"), 1)

                sk = sinks_sb[:, :, :].rearrange("p t h -> p (t h)")
                v.wait_ge(sem("bias_a_ready"), 4)
                logits(bias_a, work[2], "sa_ready", "sa_read", mx_a, nmx_a, "a", sk)
                v.tensor_tensor(ds_a, sk, mx_a, ALU.subtract).then_inc(sem("sink_arg"), 1)

                v.wait_ge(sem("yd_ready"), l + 1)
                v.wait_ge(sem("rotated_out"), l * 8 + 8)
                for t in range(2):
                    v.scalar_tensor_tensor(tmp[0][:, t * T:(t + 1) * T], udT[:, t, :], col(R_DS, t), PS[:, 7, t * T:(t + 1) * T],
                                           ALU.mult, ALU.add).then_inc(sem("yd_read"), 1)
                v.wait_ge(sem("conv_tanh"), l + 1)
                v.scalar_tensor_tensor(qkT[:, :, :].rearrange("p a b -> p (a b)"), qk_tanh, 1.0,
                                       qkT[:, :, :].rearrange("p a b -> p (a b)"), ALU.add, ALU.mult).then_inc(sem("qk_ready"), 1)
                v.wait_ge(sem("gelu_sq"), l + 1)
                v.tensor_scalar(tmp[1], tmp[1], GELU_C, 1.0, ALU.mult, ALU.add).then_inc(sem("gelu_step"), 1)
                v.wait_ge(sem("gelu_step"), l * 2 + 1)
                v.tensor_tensor(tmp[1], tmp[1], tmp[0], ALU.mult).then_inc(sem("gelu_step"), 1)
                v.wait_ge(sem("a_exp"), l * 9 + 9)
                v.tensor_tensor(rs_a, rs_a, es_a, ALU.add).then_inc(sem("rsa_sum"), 1)
                v.wait_ge(sem("rsa_sum"), l + 1)
                v.reciprocal(ri_a, rs_a).then_inc(sem("ria_ready"), 1)
                v.wait_ge(sem("gelu_tanh"), l + 1)
                v.scalar_tensor_tensor(tmp[3], tmp[1], 1.0, tmp[0], ALU.add, ALU.mult).then_inc(sem("yg_ready"), 1)
                v.wait_ge(sem("glu_tanh"), l + 1)
                v.scalar_tensor_tensor(tmp[0], tmp[2], 1.0, tmp[3], ALU.add, ALU.mult).then_inc(sem("od_step"), 1)
                v.wait_ge(sem("od_step"), l + 1)
                v.tensor_scalar(oT[:, 6:8, :].rearrange("p a b -> p (a b)"), tmp[0], 0.25, None, ALU.mult
                                ).then_inc(sem("od_ready"), 1)

                v.wait_ge(sem("cols_turned"), l + 1)
                v.tensor_copy(rcol, PS[:, 6, 0:8]).then_inc(sem("cols_ready"), 1)
                v.tensor_copy(nmcol, PS[:, 6, 8:16]).then_inc(sem("cols_ready"), 1)
                v.wait_ge(sem("cols_ready"), l * 2 + 2)
                v.wait_ge(sem("g_spread"), l + 1)
                for h in range(H):
                    g = PS[:, 4 + h // 2, (h % 2) * T:(h % 2 + 1) * T]
                    v.scalar_tensor_tensor(work[0][:, h, 0:T], g, heads(rcol)[:, 0, h:h + 1], mask_c[:, :], ALU.add, ALU.add)
                    ins = v.scalar_tensor_tensor(work[0][:, h, T:384], g[:, P:T], heads(rcol)[:, 1, h:h + 1], mask_c[:, 0:P],
                                                 ALU.add, ALU.add)
                ins.then_inc(sem("w_args_ready"), 1)
                v.wait_ge(sem("st_ready"), l + 1)
                v.wait_ge(sem("w_exp"), l + 1)
                v.scalar_tensor_tensor(work[0][:, :, :], PS[:, 4:8, 0:384], HD ** -0.5 / 4, work[0][:, :, :], ALU.mult, ALU.mult
                                       ).then_inc(sem("pc_ready"), 1)
                v.wait_ge(sem("num_ready"), l + 1)
                num = PS[:, 4:6, 0:260].rearrange("p t (h e) -> p t h e", h=H)
                v.wait_ge(sem("den_ready"), l + 1)
                v.tensor_tensor(dmx, den, enm, ALU.max).then_inc(sem("den_step"), 1)
                v.wait_ge(sem("den_step"), l * 2 + 1)
                v.reciprocal(rden_c, dmx).then_inc(sem("den_step"), 1)
                v.wait_ge(sem("den_step"), l * 2 + 2)

                def over_e(ap):
                    return ap.unsqueeze(2).to_broadcast([P, 8, HD])

                for tt in range(2):
                    v.tensor_tensor(hs[:, tt, :, :], num[:, tt, :, 0:HD],
                                    heads(rden_c)[:, tt, :].unsqueeze(2).to_broadcast([P, H, HD]), ALU.mult
                                    ).then_inc(sem("hs_ready"), 1)
                hs8 = hs[:, :, :, :].rearrange("p t h e -> p (t h) e")
                hn8 = hn[:, :, :, :].rearrange("p t h e -> p (t h) e")
                v.wait_ge(sem("hs_ready"), l * 2 + 2)
                v.tensor_reduce(s1, hs8, AX, ALU.add).then_inc(sem("hn_step"), 1)
                v.wait_ge(sem("hn_step"), l * 5 + 1)
                v.tensor_scalar(mu, s1, 1.0 / HD, None, ALU.mult).then_inc(sem("hn_step"), 1)
                v.wait_ge(sem("hn_step"), l * 5 + 2)
                v.tensor_tensor(hs8, hs8, over_e(mu), ALU.subtract).then_inc(sem("hn_step"), 1)
                v.wait_ge(sem("hn_step"), l * 5 + 3)
                v.tensor_tensor(hn8, hs8, hs8, ALU.mult).then_inc(sem("hn_step"), 1)
                v.wait_ge(sem("hn_step"), l * 5 + 4)
                v.tensor_reduce(s2, hn8, AX, ALU.add).then_inc(sem("hn_step"), 1)
                v.wait_ge(sem("hn_step"), l * 5 + 5)
                v.tensor_scalar(var_c, s2, 1.0 / HD, LN_EPS, ALU.mult, ALU.add).then_inc(sem("varc_ready"), 1)
                v.wait_ge(sem("rstdc_ready"), l + 1)
                v.tensor_tensor(hn8, hs8, over_e(rstd_c), ALU.mult).then_inc(sem("hn_ready"), 1)
                v.wait_ge(sem("hn_turned"), l + 1)
                v.wait_ge(sem("sig_ready"), l + 1)
                for t in range(2):
                    v.scalar_tensor_tensor(oT[:, 4 + t, :], PS[:, 6, t * T:(t + 1) * T], col(R_MHG, t), sig_o[:, t, :],
                                           ALU.mult, ALU.mult).then_inc(sem("oc_ready"), 1)
                deepnorm(l, 1)
                evac_uT(2, l * 24 + 16, l * 3 + 3)

                with v.Fori(0, PAIRS) as it:
                    for j in range(2):
                        ffn_tile(0, l * 44 + it * 4 + (22 + 2 * j))
                        ada_chunk(j, 32 * (ada_use(l, 24, it) + 1), l * 36 + it * 2 + (36 + j))
                        ffn_tile(1, l * 44 + it * 4 + (22 + 2 * j))
                    mod_cols(bass.ds(it * 4, 4), 4, l * 36 + it * 2 + 38)
                gate_diag(2, l * 3 + 2)
                for ft in range(2):
                    ffn_tile(ft, l * 44 + 42)
                    ada_chunk(ft, 32 * (ada_use(l, 34 + ft) + 1), l * 36 + (46 + ft))
                mod_cols(slice(20, 24), 4, l * 36 + 48)
                mod_ab(0, 2, l * 3 + 3, l * 12 + 15)
                deepnorm(l, 2)
                evac_uT(0, l * 24 + 24, l * 3 + 4)

        @block.scalar
        def _(a):
            a.wait_ge(sem("c_loaded"), 16)
            a.activation(cs[:, :], c_sb[:, :], ACT.Silu).then_inc(sem("cs_ready"), 1)

            def evac_uT(s, turned, ab):
                a.wait_ge(sem("mod_step"), ab * 3)
                for j in range(4):
                    if j % 2 == 0:
                        a.wait_ge(sem("x_turned"), turned + (TURN_ORDER.index(j + 1) + 1))
                    a.activation(uT[:, j, :], PS[:, 4 + j // 2, (j % 2) * T:(j % 2 + 1) * T], ACT.Identity, bias=mod_b[:, s, j:j + 1],
                                 scale=mod_a[:, s, j:j + 1]).then_inc(sem("uT_act"), 1)

            def copy_gate(n, factor):
                for hf in range(2):
                    a.wait_ge(sem("gate_spread"), n * 2 + (hf + 1))
                    a.activation(gate_bc[:, hf * 512:(hf + 1) * 512], PS[:, 7, :], ACT.Copy, scale=factor
                                 ).then_inc(sem("gate_ready"), 1)

            def silu_tile(ft, tile):
                a.wait_ge(sem("ag_ready"), tile + (ft + 1))
                a.wait_ge(sem("h_done"), tile + (ft + 1))
                a.activation(silu_ring[:, ft, :], PS[:, 4 + ft, 0:T], ACT.Silu).then_inc(sem("silu_ready"), 1)

            evac_uT(0, 0, 1)
            with a.Fori(0, DEPTH) as l:
                a.wait_ge(sem("prm_ready"), l + 1)
                a.activation(S5["dt"], log_dt[:, :], ACT.Exp).then_inc(sem("dt_ready"), 1)
                a.wait_ge(sem("lrdt_ready"), l + 1)
                a.activation(S5["rho"], S5["lrdt"], ACT.Exp)
                a.wait_ge(sem("angle_ready"), l + 1)
                a.activation(S5["sin"], S5["r0"], ACT.Sin)
                a.activation(S5["sinh"], S5["r0"], ACT.Sin, scale=0.5).then_inc(sem("sin_ready"), 1)
                with a.Fori(0, PAIRS) as it:
                    for j in range(2):
                        for ft in range(2):
                            silu_tile(ft, l * 44 + it * 4 + 2 * j)
                copy_gate(l * 3, 0.5)
                for ft in range(2):
                    silu_tile(ft, l * 44 + 20)
                evac_uT(1, l * 24 + 8, l * 3 + 2)

                copy_gate(l * 3 + 1, 1.0)

                def z_in(n):
                    a.wait_ge(sem("z_ready"), l * NZ + (n + 1))
                    return PS[:, 4 + n % 4, 0:T]

                def z_copy(n, dst, w=T):
                    a.activation(dst, z_in(n)[:, 0:w], ACT.Copy).then_inc(sem("z_read"), 1)

                z_copy(0, udT[:, 0, :])
                z_copy(1, udT[:, 1, :])
                z_copy(2, kiT[:, :])
                z_copy(3, cqT[:, :])
                z_copy(4, tokv[:, 0, :], 196)
                z_copy(5, tokv[:, 1, :], 196)
                z_copy(6, kbT[:, :])
                a.wait_ge(sem("ln_bc_used"), l * 3 + 2)
                for n in (7, 8):
                    a.activation(rows[:, n - 7, :], z_in(n)[0:H, :], ACT.Identity, bias=gate_bias[:, n - 7:n - 6]
                                 ).then_inc(sem("z_read"), 1)
                z_copy(9, qiT[:, :])
                z_copy(10, qbT[:, 0, :])
                z_copy(11, qbT[:, 1, :])
                e_row, ln_row = work[3][0:H, 0, 0:T], work[3][0:H, 1, 0:T]
                a.wait_ge(sem("z_read"), l * NZ + 12)
                a.activation(e_row, rows[:, 1, :], ACT.Abs).then_inc(sem("f_step"), 1)
                a.wait_ge(sem("f_step"), l * 2 + 1)
                a.activation(e_row, e_row, ACT.Exp, scale=-1.0).then_inc(sem("f_step"), 1)
                a.wait_ge(sem("f_step"), l * 2 + 2)
                a.activation(ln_row, e_row, ACT.Ln, bias=1.0).then_inc(sem("ln_f_ready"), 1)
                z_copy(12, qk_raw[:, 0, :])
                z_copy(13, qk_raw[:, 1, :])
                a.wait_ge(sem("idx_ready"), l + 1)
                a.activation(work[0][:, :, :], PS[:, 0:4, 0:384], ACT.Relu).then_inc(sem("idx_read"), 1)
                z_copy(14, qk_raw[:, 2, :])
                z_copy(15, qk_raw[:, 3, :])
                for n in range(16, 18):
                    z_copy(n, qaT[:, n - 16, :])
                for n in range(18, 20):
                    z_copy(n, kaT[:, n - 18, :])
                a.wait_ge(sem("vaug_ones"), 1)
                for n in (20, 21):
                    a.activation(vaug[:, n - 20, :, 0:HD], z_in(n).rearrange("p (h e) -> p h e", h=H), ACT.Copy
                                 ).then_inc(sem("z_read"), 1)
                for n in (22, 23):
                    a.activation(sig_o[:, n - 22, :], z_in(n), ACT.Tanh, scale=0.5).then_inc(sem("z_read"), 1)

                def exps(p, nmx, rs, name, ready):
                    a.wait_ge(sem(ready), l + 1)
                    for tt, cols in ((0, slice(0, P)), (1, slice(P, 384))):
                        for h in range(H):
                            a.activation(p[:, h, cols], p[:, h, cols], ACT.Exp, bias=heads(nmx)[:, tt, h:h + 1],
                                         accum_out=heads(rs)[:, tt, h:h + 1]).then_inc(sem(name), 1)

                exps(work[0], nmx_b, rs_b, "b_exp", "b_nmax")
                a.wait_ge(sem("conv_step"), l * 16 + 16)
                a.wait_ge(sem("sb_read"), l + 1)
                a.activation(qk_tanh, qkT[:, :, :].rearrange("p a b -> p (a b)"), ACT.Tanh, scale=0.5).then_inc(sem("conv_tanh"), 1)
                exps(work[2], nmx_a, rs_a, "a_exp", "a_nmax")
                a.wait_ge(sem("sink_arg"), l + 1)
                a.activation(es_a, ds_a, ACT.Exp).then_inc(sem("a_exp"), 1)
                a.wait_ge(sem("yd_read"), l * 2 + 2)
                a.activation(tmp[1], tmp[0], ACT.Square).then_inc(sem("gelu_sq"), 1)
                a.wait_ge(sem("qk_ready"), l + 1)
                ptb = work[1][:, :, :].rearrange("p h n -> p (h n)")
                pta = work[3][:, :, :].rearrange("p h n -> p (h n)")
                for b in range(3):
                    a.wait_ge(sem("ptb_turned"), l * 3 + (b + 1))
                    a.activation(ptb[:, b * 512:(b + 1) * 512], PS[:, 4 + b, :], ACT.Copy).then_inc(sem("ptb_ready"), 1)
                a.wait_ge(sem("gelu_step"), l * 2 + 2)
                a.activation(tmp[1], tmp[1], ACT.Tanh, scale=GELU_S).then_inc(sem("gelu_tanh"), 1)
                a.wait_ge(sem("ob_ready"), l + 1)
                a.activation(oT[:, 2:4, :].rearrange("p a b -> p (a b)"), PS[:, 4, :], ACT.Copy).then_inc(sem("ob_read"), 1)
                a.wait_ge(sem("rows_ready"), l * 2 + 2)
                for b in range(3):
                    a.wait_ge(sem("pta_turned"), l * 3 + (b + 1))
                    a.activation(pta[:, b * 512:(b + 1) * 512], PS[:, 4 + b, :], ACT.Copy).then_inc(sem("pta_ready"), 1)
                a.wait_ge(sem("gb_half_ready"), l + 1)
                a.wait_ge(sem("glu_ready"), l + 1)
                for t in range(2):
                    ins = a.activation(tmp[2][:, t * T:(t + 1) * T], PS[:, 7, t * T:(t + 1) * T], ACT.Tanh, scale=0.25,
                                       bias=gb_half[:, t:t + 1])
                ins.then_inc(sem("glu_tanh"), 1)
                a.wait_ge(sem("oa_ready"), l + 1)
                a.activation(oT[:, 0:2, :].rearrange("p a b -> p (a b)"), PS[:, 4, :], ACT.Copy).then_inc(sem("oa_read"), 1)
                a.wait_ge(sem("cols_ready"), l * 2 + 2)
                a.activation(enm, nmcol, ACT.Exp)
                a.wait_ge(sem("w_args_ready"), l + 1)
                a.activation(work[0][:, :, :], work[0][:, :, :], ACT.Exp).then_inc(sem("w_exp"), 1)
                a.wait_ge(sem("num_ready"), l + 1)
                a.activation(heads(den), PS[:, 4:6, 0:260].rearrange("p t (h e) -> p t h e", h=H)[:, :, :, 64], ACT.Abs
                             ).then_inc(sem("den_ready"), 1)
                evac_uT(2, l * 24 + 16, l * 3 + 3)

                with a.Fori(0, PAIRS) as it:
                    for j in range(2):
                        for ft in range(2):
                            silu_tile(ft, l * 44 + it * 4 + (22 + 2 * j))
                copy_gate(l * 3 + 2, 0.5)
                for ft in range(2):
                    silu_tile(ft, l * 44 + 42)
                evac_uT(0, l * 24 + 24, l * 3 + 4)

        @block.gpsimd
        def _(g):
            for s in range(2):
                g.memset(ada_ring[s][:, 8, :], 0.0).then_inc(sem("pad_zeroed"), 1)
            g.memset(ident[:, :], 0.0).then_inc(sem("const_step"), 1)
            g.memset(ones[:, :], 1.0).then_inc(sem("const_step"), 1)
            g.memset(neg_half[:, :], -0.5).then_inc(sem("const_step"), 1)
            g.memset(zeros_bf[:, :], 0.0).then_inc(sem("const_step"), 1)
            g.memset(mask_c[:, :], 0.0).then_inc(sem("const_step"), 1)
            bm = work[0][:, 0, 0:P].rearrange("p (q two c) -> p q two c", two=2, c=16)
            g.memset(work[0][:, 0, 0:P], 0.0).then_inc(sem("const_step"), 1)
            g.wait_ge(sem("const_step"), 6)
            g.memset(bm[0:64, :, 0, :], 1.0).then_inc(sem("const_step"), 1)
            g.memset(bm[64:128, :, 1, :], 1.0).then_inc(sem("const_step"), 1)
            g.wait_ge(sem("const_step"), 8)
            g.affine_select(out=ident[:, :], in_=ident[:, :], compare_op=ALU.not_equal, fill=1.0, base=0,
                            pattern=[[-1, P]], channel_multiplier=1).then_inc(sem("const_step"), 1)
            g.affine_select(out=mask_c[:, :], in_=mask_c[:, :], compare_op=ALU.is_ge, fill=NEG, base=0,
                            pattern=[[1, T]], channel_multiplier=-1).then_inc(sem("const_step"), 1)
            g.iota(dist[:, 0:P], pattern=[[1, P]], base=0, channel_multiplier=-1,
                   allow_small_or_imprecise_dtypes=True).then_inc(sem("const_step"), 1)
            g.iota(dist[:, P:384], pattern=[[1, T]], base=-P, channel_multiplier=-1,
                   allow_small_or_imprecise_dtypes=True).then_inc(sem("const_step"), 1)
            for m in (mask_a, mask_b[:, :]):
                g.memset(m, 0.0).then_inc(sem("const_step"), 1)
            g.wait_ge(sem("const_step"), 14)
            for m in (mask_a, mask_b[:, :]):
                g.memset(m[0:64, 64:128], NEG).then_inc(sem("const_step"), 1)
                g.memset(m[0:64, P + 192:P + 256], NEG).then_inc(sem("const_step"), 1)
            g.memset(mask_a[64:128, P:P + 64], NEG).then_inc(sem("const_step"), 1)
            g.wait_ge(sem("const_step"), 19)
            g.sem_inc(sem("ln_bc_used"), 1)
            g.wait_ge(sem("x_loaded"), 32)
            g.sem_inc(sem("x_ready"), 2)

            def residual(l, s):
                n = l * 3 + s
                for tt in range(2):
                    g.wait_ge(sem("var_ready"), n * 2 + (tt + 1))
                    g.tensor_tensor(rstd[:, tt:tt + 1], var_eps[:, tt:tt + 1], neg_half[:, 0:1], ALU.pow
                                    ).then_inc(sem("rstd_ready"), 1)
                g.wait_ge(sem("ln_bc_loaded"), (n + 1) * 32)
                for tt in range(2):
                    g.wait_ge(sem("xn_ready"), n * 2 + (tt + 1))
                    g.tensor_tensor(x_sb[:, tt, :], xn[:, tt, :], ln_bc[:, 0, :], ALU.mult).then_inc(sem("x_step"), 1)
                    g.wait_ge(sem("x_step"), n * 2 + (tt + 1))
                    g.tensor_tensor(x_sb[:, tt, :], x_sb[:, tt, :], ln_bc[:, 1, :], ALU.add).then_inc(sem("x_ready"), 1)
                g.wait_ge(sem("x_ready"), n * 2 + 4)
                g.sem_inc(sem("ln_bc_used"), 1)

            with g.Fori(0, DEPTH) as l:
                g.wait_ge(sem("rot_start"), l * 2 + 4)
                m = 1
                k = 0
                while m < T:
                    w = min(m, T - 1 - m)
                    lo = slice(1, 1 + w)
                    hi = slice(m + 1, m + 1 + w)
                    t4 = [work_flat[:, 1024 * q:1024 * q + 8 * w].rearrange("p (i n) -> p i n", i=8) for q in range(4)]
                    cm = cos_t[:, :, m:m + 1].to_broadcast([P, 8, w])
                    sm = sin_t[:, :, m:m + 1].to_broadcast([P, 8, w])
                    if k:
                        g.wait_ge(sem("rot_step"), l * 48 + 6 * k)
                    g.tensor_tensor(t4[0], cos_t[:, :, lo], cm, ALU.mult).then_inc(sem("rot_step"), 1)
                    g.tensor_tensor(t4[1], sin_t[:, :, lo], sm, ALU.mult).then_inc(sem("rot_step"), 1)
                    g.tensor_tensor(t4[2], sin_t[:, :, lo], cm, ALU.mult).then_inc(sem("rot_step"), 1)
                    g.tensor_tensor(t4[3], cos_t[:, :, lo], sm, ALU.mult).then_inc(sem("rot_step"), 1)
                    g.wait_ge(sem("rot_step"), l * 48 + (6 * k + 4))
                    g.tensor_tensor(cos_t[:, :, hi], t4[0], t4[1], ALU.subtract).then_inc(sem("rot_step"), 1)
                    g.tensor_tensor(sin_t[:, :, hi], t4[2], t4[3], ALU.add).then_inc(sem("rot_step"), 1)
                    k += 1
                    m *= 2
                residual(l, 0)
                for b in range(4):
                    tl = slice(2 * b, 2 * b + 2)
                    g.wait_ge(sem("bu_read"), l * 4 + (b + 1))
                    t_re, t_im = (tmp[2 * (b % 2) + q].rearrange("p (a b) -> p a b", a=2) for q in range(2))
                    g.tensor_tensor(st_re[:, tl, :], st_re[:, tl, :], t_re, ALU.add).then_inc(sem("rotated_in"), 1)
                    g.tensor_tensor(st_im[:, tl, :], st_im[:, tl, :], t_im, ALU.subtract).then_inc(sem("rotated_in"), 1)
                for b in range(4):
                    tl = slice(2 * b, 2 * b + 2)
                    g.wait_ge(sem("rotating_out"), l * 4 + (b + 1))
                    t4 = [tmp[q].rearrange("p (a b) -> p a b", a=2) for q in range(4)]
                    g.tensor_tensor(st_re[:, tl, :], t4[0], t4[1], ALU.subtract).then_inc(sem("rotated_out"), 1)
                    g.tensor_tensor(st_im[:, tl, :], t4[2], t4[3], ALU.add).then_inc(sem("rotated_out"), 1)
                g.tensor_scalar(gb_half[:, 0:2], prm[:, R_GB:R_GB + 2], 0.5, 0.0, ALU.mult, ALU.add).then_inc(sem("gb_half_ready"), 1)

                def normalise(p, ri, ready, signal):
                    g.wait_ge(sem(ready), l + 1)
                    for tt, c0, w in ((0, 0, P), (1, P, T)):
                        g.tensor_tensor(p[:, :, c0:c0 + w], p[:, :, c0:c0 + w],
                                        heads(ri)[:, tt, :].unsqueeze(2).to_broadcast([P, H, w]), ALU.mult
                                        ).then_inc(sem(signal), 1)

                normalise(work[0], ri_b, "rib_ready", "pb_ready")
                g.wait_ge(sem("z_read"), l * NZ + NZ)
                waited(g)
                g.tensor_scalar(sig_o[:, :, :], sig_o[:, :, :], 0.5, 0.5, ALU.mult, ALU.add).then_inc(sem("sig_ready"), 1)
                normalise(work[2], ri_a, "ria_ready", "pa_ready")
                g.wait_ge(sem("varc_ready"), l + 1)
                g.tensor_tensor(rstd_c, var_c, neg_half[:, :], ALU.pow).then_inc(sem("rstdc_ready"), 1)
                settle(g)
                g.wait_ge(sem("od_ready"), l + 1)
                for s in range(2):
                    g.memset(ada_ring[s][:, 8, :], 0.0).then_inc(sem("pad_zeroed"), 1)
                residual(l, 1)
                residual(l, 2)


_INS = ["x", "c", "ada_w", "ada_b", "ln_g", "ln_b", "ffn_w13", "ffn_w2", "w_in", "w_out", "sinks", "w_uq", "w_iq",
        "conv_w", "conv_b", "ig_b", "fg_b", "mh_norm_g", "lam_re", "lam_im", "log_step", "b_re", "b_im", "c_re",
        "c_im", "d_skip", "glu_w", "glu_b"]


def kernel(**inputs):
    import numpy as _np
    import concourse.bacc as _bacc
    from concourse import mybir as _mybir
    from concourse.bass_utils import run_bass_kernel_spmd as _run

    nc = _bacc.Bacc("TRN2", target_bir_lowering=False, num_devices=1)
    arrays, args = {}, []
    for name in _INS:
        a = _np.ascontiguousarray(inputs[name])
        arrays[f"in_{name}_dram"] = a
        args.append(nc.dram_tensor(f"in_{name}_dram", a.shape, _mybir.dt.from_np(a.dtype), kind="ExternalInput").ap())
    args.append(nc.dram_tensor("out_0_dram", (1, T, D), _mybir.dt.from_np(_np.dtype("float32")), kind="ExternalOutput").ap())
    trunk(nc, *args)
    r = _run(nc, [arrays], core_ids=[0])
    return r.results[0]["out_0_dram"]
```

```python
from contextlib import ExitStack

import concourse.bass as bass
from concourse import mybir

F32 = mybir.dt.float32
F32R = mybir.dt.float32r
BF16 = mybir.dt.bfloat16
ALU = mybir.AluOpType
ACT = mybir.ActivationFunctionType
AX = mybir.AxisListType.X

P = 128
D = 1024
KT = D // P
T = 256
DEPTH = 2
D_FF = 2816
CW = 256
CHUNKS = D_FF // CW
PAIRS = CHUNKS // 2
MIX_CHUNKS = 6
GPL = 2 * CHUNKS + MIX_CHUNKS
G_MIX = CHUNKS
G_FFN2 = CHUNKS + MIX_CHUNKS
HD = 64
H = 4
N_SUB = 3
ALPHA = (2 * DEPTH) ** 0.25
LN_EPS = 1e-5
NEG = -1e30
TAKEN = -3e38
TOPK = 64
IDX_SCALE = (32 * 4) ** -0.5
SLOPES = [2.0 ** -(i + 1) for i in range(8)]
SLOPES_A, SLOPES_B = SLOPES[0::2], SLOPES[1::2]
MAGIC = 1.5 * 2.0 ** 23
INV_2PI = 0.15915494309189535
TWO_PI_1, TWO_PI_2, TWO_PI_3 = 6.28125, 1.9350051879882812e-3, 3.0198289163009303e-07
PI_BELOW = 3.1415925
GELU_C, GELU_S = 0.044715, 0.7978845608028654

C_QA, C_KA, C_VA, C_CQ, C_KB, C_VB, C_KI, C_WI, C_QK, C_VC, C_IG, C_FG, C_OC, C_UD = (
    0, 256, 384, 512, 640, 704, 768, 800, 804, 1316, 1572, 1576, 1580, 1836)
MIX_PIECES = [
    [(0, C_UD, 256), (256, C_KI, 32), (288, C_KI, 32), (320, C_KI, 32), (352, C_KI, 32), (384, C_CQ, 128)],
    [(0, C_VB, 64), (64, C_VA, 128), (192, C_WI, 4), (196, C_KB, 64), (260, C_KB, 64), (324, C_IG, 4), (328, C_FG, 4)],
    [(0, C_QK, 512)],
    [(0, C_QA, 256), (256, C_KA, 64), (320, C_KA, 64), (384, C_KA + 64, 64), (448, C_KA + 64, 64)],
    [(0, C_VC, 256)],
    [(0, C_OC, 256)],
]
OUT_TILES = [[6, 7], [2, 3], [0], [1], [4], [5]]
LOADS = [2] * CHUNKS + [len(p) for p in MIX_PIECES] + [2] * CHUNKS
LOADS_PER_LAYER = [sum(LOADS[s::2]) for s in range(2)]
LOADS_BEFORE = [sum(LOADS[g % 2:g:2]) for g in range(GPL)]

R_LNG, R_LNB, R_CW, R_CB, R_MHG, R_DS, R_GB, R_LR, R_LI, ROWS = 0, 24, 48, 64, 68, 70, 72, 74, 82, 90
PARAM_DMAS = 24

ADA_FIRST = 12
ADA_PER_LAYER = 36
ADA_FFN1 = 20
MODS = 9
TURN_ORDER = [0, 1, 4, 5, 2, 3, 6, 7]
ROT_STEPS = 54
NZ = 24


def trunk(nc, x, c, ada_w, ada_b, ln_g, ln_b, ffn_w13, ffn_w2, w_in, w_out, sinks, w_uq, w_iq,
          conv_w, conv_b, ig_b, fg_b, mh_norm_g, lam_re, lam_im, log_step, b_re, b_im, c_re, c_im,
          d_skip, glu_w, glu_b, out):
    ctx = ExitStack()
    with ctx:
        def sb(name, shape, dt=F32):
            offset[name] = (nc.sbuf_base + 31) // 32 * 32
            return ctx.enter_context(nc.sbuf_tensor(name, shape, dt))

        def over(name, of, shape, skip=0):
            return nc.alloc_sbuf_tensor_at(name, shape, F32R, offset=offset[of] + 4 * skip)

        sems, offset = {}, {}

        def sem(name):
            if name not in sems:
                sems[name] = ctx.enter_context(nc.semaphore(name))
            return sems[name]

        w_in_ring = [sb(f"w_in_ring{s}", [P, KT, 512]) for s in range(2)]
        w_out_ring = [sb(f"w_out_ring{s}", [P, 2, D]) for s in range(2)]
        arena = sb("arena", [P, 6144])
        ada_ring = [arena[:, s * 2304:(s + 1) * 2304].rearrange("p (t n) -> p t n", n=CW) for s in range(2)]
        h_ring = arena[:, 4608:5632].rearrange("p (s n) -> p s n", n=T)
        silu_ring = arena[:, 5632:6144].rearrange("p (s n) -> p s n", n=T)
        st_re = arena[:, 0:2048].rearrange("p (i n) -> p i n", n=T)
        st_im = arena[:, 2048:4096].rearrange("p (i n) -> p i n", n=T)
        tmp = [arena[:, 4096 + 512 * k:4608 + 512 * k] for k in range(4)]

        x_sb = sb("x_sb", [P, 2, D])
        xn = sb("xn", [P, 2, D])
        uT = sb("uT", [P, KT, T])
        oT = uT
        gate_bc = sb("gate_bc", [P, D])
        ln_bc = sb("ln_bc", [P, 2, D])
        qk_raw = ln_bc[:, 0, :].rearrange("p (t n) -> p t n", n=T)
        rows = ln_bc[0:H, 1, :].rearrange("p (t n) -> p t n", n=T)
        acc = [sb(f"acc{s}", [P, CW]) for s in range(2)]
        cos_t = sb("cos_t", [P, 8, T])
        sin_t = sb("sin_t", [P, 8, T])
        bias_a = sb("bias_a", [P, H, 384])
        dist = sb("dist", [P, 384])
        mask_b = sb("mask_b", [P, 384])
        mask_c = sb("mask_c", [P, T])
        ident = sb("ident", [P, P])
        ones = sb("ones", [P, P])
        block_mask = sb("block_mask", [P, P])
        zeros_bf = sb("zeros_bf", [1, 512], BF16)
        neg_half = sb("neg_half", [P, 8])
        c_sb = sb("c_sb", [P, 8])
        cs = sb("cs", [P, 8])
        mod = sb("mod", [P, 9 * 8])
        mod_a = sb("mod_a", [P, N_SUB, 8])
        mod_b = sb("mod_b", [P, N_SUB, 8])
        stats = sb("stats", [P, 2, 2, 6])
        mv = sb("mv", [P, 2, 2])
        var_eps = sb("var_eps", [P, 2])
        rstd = sb("rstd", [P, 2])
        nmr = sb("nmr", [P, 2])
        prow = sb("prow", [ROWS, P])
        prm = sb("prm", [P, ROWS])
        log_dt = sb("log_dt", [P, 8])
        b_raw = sb("b_raw", [P, 2, 8, 16])
        b_blk = sb("b_blk", [P, 2, 8, 32])
        c_blk = sb("c_blk", [P, 2, 2, P])
        bbT = sb("bbT", [P, 2, 2, P])
        cT = sb("cT", [P, 2, 2, P])
        glu_sb = sb("glu_sb", [P, 2, 256])
        uq_sb = sb("uq_sb", [P, 256])
        iq_sb = sb("iq_sb", [P, P])
        sinks_sb = sb("sinks_sb", [P, 2, H])
        gate_bias = sb("gate_bias", [H, 2])
        s5p = sb("s5p", [P, 24, 8])
        uT_lo = sb("uT_lo", [P, KT, T])
        udT, qbT = uT_lo[:, 0:2, :], uT_lo[:, 2:4, :]
        kiT, cqT, kbT, qiT = (uT_lo[:, 4 + k, :] for k in range(4))
        rot_flat = sb("rot_flat", [P, 8 * T])
        qaT, kaT, qkT = (rot_flat[:, a * T:b * T].rearrange("p (t n) -> p t n", n=T) for a, b in ((0, 2), (2, 4), (4, 8)))
        tokv = sb("tokv", [P, 2, 196])
        vaug = sb("vaug", [P, 2, H, 65])
        sig_o = sb("sig_o", [P, 2, T])
        work_flat = sb("work_flat", [P, 4 * H * 384])
        w_in_hi = [over(f"w_in_hi{ft}", "work_flat", [P, KT, 2, P], 2048 * ft) for ft in range(2)]
        w_out_hi = [over(f"w_out_hi{ft}", "work_flat", [P, D], 4096 + D * ft) for ft in range(2)]
        w_in_lo = [over(f"w_in_lo{s}", f"w_in_ring{s}", [P, KT, 512]) for s in range(2)]
        w_out_lo = [over(f"w_out_lo{s}", f"w_out_ring{s}", [P, 2, D]) for s in range(2)]
        h_parts = over("h_parts", "arena", [P, 4, T], 4608)
        u_hi, u_lo = over("u_hi", "uT", [P, KT, T]), over("u_lo", "uT_lo", [P, KT, T])
        work = [work_flat[:, k * 1536:(k + 1) * 1536].rearrange("p (h n) -> p h n", h=H) for k in range(4)]
        mask_a = work_flat[:, 1536:1920]
        qk_tanh = work_flat[:, 1536:2560]
        hs, hn = (work_flat[:, 1536 + 512 * k:2048 + 512 * k].rearrange("p (t h e) -> p t h e", t=2, h=H) for k in range(2))
        sc = sb("sc", [P, 384])
        m8 = sb("m8", [P, 2, 8])
        small = sb("small", [P, 32, 8])
        diag = sig_o[:, :, :].rearrange("p t n -> p (t n)")
        PS = ctx.enter_context(nc.psum_tensor("PS", [P, 8, 512], F32))

        S5 = {n: s5p[:, k, :] for k, n in enumerate(
            ["dt", "th", "lrdt", "rho", "n", "r", "sin", "sinh", "sh2", "cos", "a_re", "a_im", "am1", "t1", "t2",
             "den", "rden", "k1", "k2", "k_re", "k3", "k4", "k_im", "r0"])}
        mx_b, nmx_b, rs_b, ri_b, mx_a, nmx_a, rs_a, ri_a, es_a, ds_a, rcol, nmcol, enm, den, dmx, rden_c, \
            s1, mu, s2, var_c, rstd_c, gb_half, t8 = (small[:, k, :] for k in range(23))

        def heads(ap):
            return ap.rearrange("p (t h) -> p t h", t=2)

        def col(r, k=0):
            return prm[:, r + k:r + k + 1]

        block = ctx.enter_context(nc.Block())

        def settle(eng):
            eng.wait_ge(sem("const_step"), 1)

        def waited(eng):
            eng.sem_inc(sem("waits_passed"), 1)

        def w_in_tile(ring, slot, ft):
            return ring[slot][:, :, :].rearrange("p k (h f c) -> p k h f c", h=2, f=2)[:, :, :, ft, :]

        def ff_tile(l, f, it, j):
            return l * 44 + it * 4 + (22 * f + 2 * j)

        def in_loads(l, f, it, j):
            g = (0, G_FFN2)[f] + j % 2
            return 16 * (l * LOADS_PER_LAYER[g % 2] + it * 2 + (LOADS_BEFORE[g] + 2 + 2 * (j // 2)))

        def ring_use(l, g, it=0):
            return l * (GPL // 2) + (g // 2 + it)

        def ada_use(l, n, it_uses=0):
            return l * (ADA_PER_LAYER // 2) + (ADA_FIRST // 2 + n // 2) + it_uses

        @block.sync
        def _(sp):
            sp.dma_start(c_sb[:, :], c.rearrange("o (p t) -> p (o t)", t=8)).then_inc(sem("c_loaded"), 16)
            sp.wait_ge(sem("pad_zeroed"), 2)

            def load_ada(l, slot, layer, column, use, wait):
                if wait:
                    settle(sp)
                    sp.wait_ge(sem("acc_step"), use * 16 + (8 * slot - 8))
                sp.dma_start(ada_ring[slot][:, 0:8, :],
                             ada_w[layer, :, column].rearrange("o (p t) n -> p (o t) n", t=8)
                             ).then_inc(sem(f"ada_loaded{slot}"), 16)
                sp.dma_start(ada_ring[slot][0:1, 8, :], ada_b[layer, column]
                             ).then_inc(sem(f"ada_loaded{slot}"), 16)

            for n in range(ADA_FIRST):
                load_ada(0, n % 2, slice(0, 1), slice(n * CW, (n + 1) * CW), n // 2, n >= 2)
                if n == 1:
                    for tt in range(2):
                        sp.dma_start(x_sb[:, tt, :], x[0, tt * P:(tt + 1) * P, :]).then_inc(sem("x_loaded"), 16)

            def load_ffn_in(l, f, slot, column, use):
                sp.wait_ge(sem(f"w_in_used{slot}"), use + 1)
                waited(sp)
                for half, off in ((0, 0), (1, D_FF)):
                    cols = bass.ds(column + off, CW)
                    sp.dma_start(w_in_ring[slot][:, :, half * CW:(half + 1) * CW],
                                 ffn_w13[bass.ds(l, 1), f, :, cols].rearrange("o (t p) n -> p (o t) n", p=P)
                                 ).then_inc(sem(f"w_in_loaded{slot}"), 16)

            def load_ffn_out(l, f, slot, column, use):
                sp.wait_ge(sem(f"w_out_used{slot}"), use + 1)
                waited(sp)
                sp.dma_start(w_out_ring[slot][:, :, :],
                             ffn_w2[bass.ds(l, 1), f, bass.ds(column, CW), :].rearrange("o (t p) n -> p (o t) n", p=P)
                             ).then_inc(sem(f"w_out_loaded{slot}"), 16)

            def load_ln(l, s):
                for k, src in enumerate((ln_g, ln_b)):
                    sp.dma_start(ln_bc[:, k, :], src[bass.ds(l, 1), s, :].to_broadcast([P, D])
                                 ).then_inc(sem("ln_bc_loaded"), 16)

            with sp.Fori(0, DEPTH) as l:
                L = bass.ds(l, 1)
                settle(sp)
                sp.wait_ge(sem("mixer_params_used"), l + 1)
                pl = sem("params_loaded")
                for r, src in ((R_LNG, ln_g), (R_LNB, ln_b)):
                    sp.dma_start(prow[r:r + 24, :], src[L].rearrange("o s (j p) -> (o s j) p", p=P)).then_inc(pl, 16)
                sp.dma_start(prow[R_CW:R_CW + 16, :], conv_w[L].rearrange("o s (j p) -> (o s j) p", p=P)).then_inc(pl, 16)
                for r, n, src in ((R_CB, 4, conv_b), (R_MHG, 2, mh_norm_g), (R_DS, 2, d_skip), (R_GB, 2, glu_b)):
                    sp.dma_start(prow[r:r + n, :], src[L].rearrange("o (j p) -> (o j) p", p=P)).then_inc(pl, 16)
                for r, src in ((R_LR, lam_re), (R_LI, lam_im)):
                    sp.dma_start(prow[r:r + 8, :], src[L].rearrange("o (i two) p -> (o i) (two p)", two=2)).then_inc(pl, 16)
                for half in range(2):
                    sp.dma_start(log_dt[64 * half:64 * half + 64, :],
                                 log_step[L].rearrange("o (i two) -> two (o i)", two=2)[half:half + 1].to_broadcast([64, 8]),
                                 allow_slow_non_contiguous=True).then_inc(pl, 16)
                for k, src in enumerate((b_re, b_im)):
                    sp.dma_start(b_raw[:, k, :, :], src[L].rearrange("o (i two) p c -> (two p) (o i) c", two=2)).then_inc(pl, 16)
                for k, src in enumerate((c_re, c_im)):
                    for rep in range(2):
                        sp.dma_start(c_blk[:, k, :, rep * 64:(rep + 1) * 64],
                                     src[L].rearrange("o (t g) c p -> (g c) (o t) p", t=2)).then_inc(pl, 16)
                sp.dma_start(glu_sb[:, :, :], glu_w[L].rearrange("o (t p) n -> p (o t) n", p=P)).then_inc(pl, 16)
                sp.dma_start(uq_sb[:, :], w_uq[bass.ds(l, 1)].rearrange("o p n -> p (o n)")).then_inc(pl, 16)
                sp.dma_start(iq_sb[:, :], w_iq[bass.ds(l, 1)].rearrange("o p n -> p (o n)")).then_inc(pl, 16)
                for k in range(2):
                    sp.dma_start(sinks_sb[:, k, :], sinks[L].to_broadcast([P, H])).then_inc(pl, 16)
                for k, src in enumerate((ig_b, fg_b)):
                    sp.dma_start(gate_bias[:, k:k + 1], src[L].rearrange("o h -> h o")).then_inc(pl, 16)
                load_ffn_in(l, 0, 0, 0, ring_use(l, 0))
                load_ffn_out(l, 0, 0, 0, ring_use(l, 0))
                with sp.Fori(0, PAIRS) as it:
                    for j in range(2):
                        for a in range(2):
                            load_ada(l, a, L, bass.ds(3 * D + it * D + (2 * j + a) * CW, CW),
                                     ada_use(l, 0, it * 2 + j), True)
                        load_ffn_in(l, 0, 1 - j, it * 2 * CW + (j + 1) * CW, ring_use(l, j + 1, it))
                        load_ffn_out(l, 0, 1 - j, it * 2 * CW + (j + 1) * CW, ring_use(l, j + 1, it))
                sp.wait_ge(sem("ln_bc_used"), l * 3 + 1)
                waited(sp)
                load_ln(l, 0)
                def load_mix_in(m):
                    g = G_MIX + m
                    slot = g % 2
                    sp.wait_ge(sem(f"w_in_used{slot}"), ring_use(l, g) + 1)
                    waited(sp)
                    for dst, src, w in MIX_PIECES[m]:
                        sp.dma_start(w_in_ring[slot][:, :, dst:dst + w],
                                     w_in[L, :, src:src + w].rearrange("o (t p) n -> p (o t) n", p=P)
                                     ).then_inc(sem(f"w_in_loaded{slot}"), 16)

                def load_mix_out(m):
                    g = G_MIX + m
                    slot = g % 2
                    sp.wait_ge(sem(f"w_out_used{slot}"), ring_use(l, g) + 1)
                    waited(sp)
                    t0, tn = OUT_TILES[m][0], len(OUT_TILES[m])
                    sp.dma_start(w_out_ring[slot][:, 0:tn, :],
                                 w_out[L, t0 * P:(t0 + tn) * P, :].rearrange("o (t p) n -> p (o t) n", p=P)
                                 ).then_inc(sem(f"w_out_loaded{slot}"), 16)

                for m in range(2):
                    load_mix_in(m)
                for m in range(2):
                    load_mix_out(m)
                for m in range(2, MIX_CHUNKS):
                    load_mix_in(m)
                slot2 = G_FFN2 % 2
                load_ffn_in(l, 1, slot2, 0, ring_use(l, G_FFN2))
                for m in range(2, MIX_CHUNKS):
                    load_mix_out(m)
                sp.wait_ge(sem("cols_turned"), l + 1)
                waited(sp)
                sp.wait_ge(sem("g_spread"), l + 1)
                waited(sp)
                sp.wait_ge(sem("conv_step"), l * 16 + 16)
                waited(sp)
                load_ln(l, 1)
                load_ffn_out(l, 1, slot2, 0, ring_use(l, G_FFN2))
                sp.wait_ge(sem("pad_zeroed"), l * 2 + 4)
                waited(sp)

                def load_pair(it, ada):
                    for j in range(2):
                        if ada is not None:
                            layer, column, use = ada
                            for a in range(2):
                                load_ada(l, a, layer, bass.ds(column + (2 * j + a) * CW, CW), use(j), True)
                        g = G_FFN2 + j + 1
                        load_ffn_in(l, 1, g % 2, it * 2 * CW + (j + 1) * CW, ring_use(l, g, it))
                        load_ffn_out(l, 1, g % 2, it * 2 * CW + (j + 1) * CW, ring_use(l, g, it))

                load_pair(0, (L, 8 * D, lambda j: ada_use(l, ADA_FFN1 + 2 * j)))
                with sp.Fori(0, 3) as it:
                    load_pair(it + 1, (slice(DEPTH - 1, DEPTH), it * D, lambda j: ada_use(l, ADA_FFN1 + 4 + 2 * j, it * 2)))
                load_pair(4, None)
                sp.wait_ge(sem("ln_bc_used"), l * 3 + 3)
                waited(sp)
                load_ln(l, 2)
            for tt in range(2):
                sp.wait_ge(sem("x_ready"), 2 * N_SUB * DEPTH + 1 + tt)
                sp.dma_start(out[0, tt * P:(tt + 1) * P, :], x_sb[:, tt, :]).then_inc(sem("out_stored"), 16)
            sp.wait_ge(sem("out_stored"), 32)

        @block.tensor
        def _(pe):
            for s in range(2):
                pe.sem_inc(sem(f"w_in_used{s}"), 1)
                pe.sem_inc(sem(f"w_out_used{s}"), 1)
            pe.sem_inc(sem("mixer_params_used"), 1)
            pe.sem_inc(sem("ag_ready"), 2)
            pe.wait_ge(sem("const_step"), 10)

            pe.transpose(PS[:, 4, 0:P], work[0][:, 0, 0:P], ident[:, :]).then_inc(sem("mask_turned"), 1)

            def ada_cols(chunk, base):
                for a in range(2):
                    mm = pe.matmul(PS[:, 6, 2 * base + a:2 * base + a + 1], acc[chunk][:, a * P:(a + 1) * P],
                                   ones[:, 0:1], start=True, stop=True)
                mm.then_inc(sem("ada_summed"), 1)

            def turn(src, l, s):
                for tt in range(2):
                    if s is not None:
                        pe.wait_ge(sem("xn_ready"), l * 6 + (2 * s + tt + 1))
                    for j in TURN_ORDER:
                        mm = pe.transpose(PS[:, 4 + j // 2, (j % 2) * T + tt * P:(j % 2) * T + (tt + 1) * P],
                                          src[:, tt, j * P:(j + 1) * P], ident[:, :])
                        if tt == 1:
                            mm.then_inc(sem("x_turned"), 1)

            def spread_gate(n):
                for hf in range(2):
                    pe.wait_ge(sem("diag_ready"), n * 2 + (hf + 1))
                    if hf == 1:
                        pe.wait_ge(sem("gate_ready"), n * 2 + hf)
                    pe.matmul(PS[:, 7, :], ones[:, :], diag, start=True, stop=True).then_inc(sem("gate_spread"), 1)

            def seed_y():
                for b in range(4):
                    pe.matmul(PS[:, b, :], zeros_bf[0:1, 0:P], zeros_bf[0:1, :], start=True, stop=False)

            def ffn_chunk(slot, tile, last):
                for ft in range(2):
                    pe.wait_ge(sem("w_in_split"), tile + (ft + 1))
                    pe.wait_ge(sem("h_done"), tile + (ft + 1))
                    lo = w_in_tile(w_in_lo, slot, ft)
                    for half in range(2):
                        for kt in range(KT):
                            hi = w_in_hi[ft][:, kt, half, :]
                            y = PS[:, 4 + ft, half * T:(half + 1) * T]
                            pe.matmul(y, hi, u_hi[:, kt, :], start=(kt == 0), stop=False)
                            pe.matmul(y, hi, u_lo[:, kt, :], start=False, stop=False)
                            mm = pe.matmul(y, lo[:, kt, half, :], u_hi[:, kt, :], start=False, stop=(kt == KT - 1))
                    mm.then_inc(sem("ag_ready"), 1)
                for ft in range(2):
                    pe.wait_ge(sem("w_out_split"), tile + (ft + 1))
                    pe.wait_ge(sem("h_done"), tile + (ft + 3))
                    for tt in range(2):
                        for hf in range(2):
                            tok, cols = slice(tt * P, (tt + 1) * P), slice(hf * 512, (hf + 1) * 512)
                            h_hi, h_lo = h_parts[:, 2 + ft, tok], h_parts[:, ft, tok]
                            y = PS[:, 2 * tt + hf, :]
                            mm = pe.matmul(y, h_hi, w_out_hi[ft][:, cols], start=False, stop=False)
                            if (ft, tt, hf) == (0, 0, 0):
                                mm.then_inc(sem(f"w_in_used{slot}"), 1)
                            pe.matmul(y, h_hi, w_out_lo[slot][:, ft, cols], start=False, stop=False)
                            mm = pe.matmul(y, h_lo, w_out_hi[ft][:, cols], start=False, stop=(last and ft == 1))
                            if last and ft == 1:
                                mm.then_inc(sem("y_ready"), 1)
                            elif (ft, tt, hf) == (1, 1, 1):
                                mm.then_inc(sem(f"w_out_used{slot}"), 1)

            def release_out(slot):
                pe.drain().then_inc(sem(f"w_out_used{slot}"), 1)

            def ada_sum(before, n, groups):
                pe.wait_ge(sem("acc_step"), before * 8 + 8)
                if n == 0 and groups is not None:
                    pe.wait_ge(sem("mod_ready"), groups)
                ada_cols(n % 2, n)

            for gr in range(3):
                for n in range(4):
                    ada_sum(4 * gr + n, n, gr or None)
            pe.wait_ge(sem("x_loaded"), 32)
            pe.wait_ge(sem("block_mask_ready"), 1)
            pe.wait_ge(sem("mod_ready"), 3)
            turn(x_sb, 0, None)

            with pe.Fori(0, DEPTH) as l:
                pe.wait_ge(sem("params_loaded"), (l + 1) * (16 * PARAM_DMAS))
                pe.wait_ge(sem("uT_act"), l * 12 + 4)
                pe.wait_ge(sem("uT_dve"), l * 12 + 4)
                pe.transpose(PS[:, 4, 0:ROWS], prow[:, :], ident[0:ROWS, 0:ROWS]).then_inc(sem("prm_turned"), 1)
                pe.wait_ge(sem("prm_ready"), l + 1)
                pe.wait_ge(sem("y_read"), l * 12 + 4)
                pe.wait_ge(sem("uT_split"), l * 8 + 4)
                seed_y()
                with pe.Fori(0, PAIRS) as it:
                    for j in range(2):
                        ffn_chunk(j, ff_tile(l, 0, it, j), False)
                        for n in (2 * j, 2 * j + 1):
                            ada_sum(l * 36 + it * 4 + (12 + n), n, l * MODS + it + 3)
                spread_gate(l * 3)
                pe.wait_ge(sem("b_blk_ready"), l * 4 + 4)
                pe.wait_ge(sem("gate_ready"), l * 6 + 2)
                for k in range(2):
                    for t in range(2):
                        mm = pe.transpose(PS[:, 7, (2 * k + t) * P:(2 * k + t + 1) * P],
                                          b_blk[:, k, 4 * t:4 * t + 4, :].rearrange("p a b -> p (a b)"), ident[:, :])
                mm.then_inc(sem("bb_turned"), 1)
                pe.wait_ge(sem("c_blk_ready"), l * 2 + 2)
                pe.wait_ge(sem("bbT_ready"), l + 1)
                for k in range(2):
                    for t in range(2):
                        mm = pe.transpose(PS[:, 7, (2 * k + t) * P:(2 * k + t + 1) * P], c_blk[:, k, t, :], ident[:, :])
                mm.then_inc(sem("c_turned"), 1)
                ffn_chunk(0, ff_tile(l, 0, PAIRS, 0), True)
                release_out(0)
                pe.wait_ge(sem("mod_ready"), l * MODS + 8)
                pe.wait_ge(sem("h_done"), l * 44 + 24)
                pe.wait_ge(sem("cT_ready"), l + 1)
                turn(xn, l, 0)

                pe.wait_ge(sem("uT_act"), l * 12 + 8)
                pe.wait_ge(sem("uT_dve"), l * 12 + 8)
                pe.wait_ge(sem("y_read"), l * 12 + 8)
                spread_gate(l * 3 + 1)

                def z_out(n):
                    if n == 3:
                        pe.wait_ge(sem("gate_ready"), l * 6 + 4)
                    if n >= 4:
                        pe.wait_ge(sem("z_read"), l * NZ + (n - 3))
                    return PS[:, 4 + n % 4, 0:T]

                def z_feature(n, slot, c0, m=P):
                    o = z_out(n)
                    for kt in range(KT):
                        mm = pe.matmul(o[0:m, :], w_in_ring[slot][:, kt, c0:c0 + m], uT[:, kt, :],
                                       start=(kt == 0), stop=(kt == KT - 1))
                    mm.then_inc(sem("z_ready"), 1)

                def z_token(n, slot, c0, w, tt):
                    o = z_out(n)
                    for kt in range(KT):
                        mm = pe.matmul(o[:, 0:w], uT[:, kt, tt * P:(tt + 1) * P], w_in_ring[slot][:, kt, c0:c0 + w],
                                       start=(kt == 0), stop=(kt == KT - 1))
                    mm.then_inc(sem("z_ready"), 1)

                def chunk_in(m):
                    g = G_MIX + m
                    pe.wait_ge(sem(f"w_in_loaded{g % 2}"), 16 * (l * LOADS_PER_LAYER[g % 2] + LOADS_BEFORE[g] + LOADS[g]))

                def chunk_done(m):
                    pe.drain().then_inc(sem(f"w_in_used{(G_MIX + m) % 2}"), 1)

                def s5_inputs(b):
                    if b >= 2:
                        pe.wait_ge(sem("bu_read"), l * 4 + (b - 1))
                    for k in range(2):
                        i = 2 * b + k
                        q, t = i % 4, i // 4
                        for ri in range(2):
                            mm = pe.matmul(PS[:, 2 * (b % 2) + k, ri * T:(ri + 1) * T],
                                           bbT[32 * q:32 * q + 32, ri, t, :], udT[32 * q:32 * q + 32, t, :],
                                           start=True, stop=True)
                    mm.then_inc(sem("bu_ready"), 1)

                def scores(q_of, k_of, rows_of, signal):
                    for h in range(H):
                        r = rows_of(h)
                        for tt, w in ((0, P), (1, T)):
                            mm = pe.matmul(PS[:, h, (0, P)[tt]:(0, P)[tt] + w], q_of(h)[r, tt * P:(tt + 1) * P],
                                           k_of(h)[r, 0:w], start=True, stop=True)
                    mm.then_inc(sem(signal), 1)

                def half(h):
                    return slice(64 * (h % 2), 64 * (h % 2) + 64)

                chunk_in(0)
                s0, s1_ = G_MIX % 2, (G_MIX + 1) % 2
                z_feature(0, s0, 0)
                z_feature(1, s0, 128)
                pe.wait_ge(sem("z_read"), l * NZ + 2)
                s5_inputs(0)
                s5_inputs(1)
                z_feature(2, s0, 256)
                z_feature(3, s0, 384)
                chunk_done(0)
                chunk_in(1)
                for tt in range(2):
                    z_token(4 + tt, s1_, 0, 196, tt)
                z_feature(6, s1_, 196)
                z_feature(7, s1_, 324, H)
                z_feature(8, s1_, 328, H)
                chunk_done(1)
                s5_inputs(2)
                for n, w in ((9, iq_sb[:, :]), (10, uq_sb[:, 0:P]), (11, uq_sb[:, P:2 * P])):
                    pe.matmul(z_out(n), w, cqT[:, :], start=True, stop=True).then_inc(sem("z_ready"), 1)
                s5_inputs(3)
                chunk_in(2)
                for t in range(2):
                    z_feature(12 + t, s0, t * P)
                pe.wait_ge(sem("z_read"), l * NZ + 12)
                pe.wait_ge(sem("bu_read"), l * 4 + 4)
                scores(lambda h: qiT, lambda h: kiT, lambda h: slice(32 * h, 32 * h + 32), "idx_ready")
                for t in range(2, 4):
                    z_feature(12 + t, s0, t * P)
                chunk_done(2)
                pe.wait_ge(sem("idx_read"), l + 1)
                scores(lambda h: qbT[:, h // 2, :], lambda h: kbT, half, "sb_ready")
                chunk_in(3)
                for t in range(4):
                    z_feature(16 + t, s1_, t * P)
                chunk_done(3)
                chunk_in(4)
                for tt in range(2):
                    z_token(20 + tt, s0, 0, T, tt)
                chunk_done(4)
                pe.wait_ge(sem("sb_read"), l + 1)
                pe.wait_ge(sem("z_read"), l * NZ + 20)
                scores(lambda h: qaT[:, h // 2, :], lambda h: kaT[:, h // 2, :], half, "sa_ready")
                chunk_in(5)
                for t in range(2):
                    z_feature(22 + t, s1_, t * P)
                chunk_done(5)
                pe.wait_ge(sem("z_read"), l * NZ + NZ)

                def turn_probs(src, signal):
                    for b, c0 in enumerate((0, P, 2 * P)):
                        for h in range(H):
                            mm = pe.transpose(PS[:, 4 + b, h * P:(h + 1) * P], src[:, h, c0:c0 + P], ident[:, :])
                        mm.then_inc(sem(signal), 1)

                def mix_values(pt, v_of, bank):
                    for h in range(H):
                        o = PS[half(h), bank, (h // 2) * T:(h // 2 + 1) * T]
                        ptv = pt[:, :, :].rearrange("p h n -> p (h n)")
                        mm = pe.matmul(o[:, 0:P], v_of(0, h), ptv[:, h * P:(h + 1) * P], start=True, stop=True)
                        for kt in range(2):
                            mm = pe.matmul(o[:, P:T], v_of(kt, h), ptv[:, 512 * (kt + 1) + h * P:512 * (kt + 1) + (h + 1) * P],
                                           start=(kt == 0), stop=(kt == 1))
                    return mm

                pe.wait_ge(sem("rotated_out"), l * 8 + 8)
                for i in range(8):
                    q, t = i % 4, i // 4
                    for ri, st in ((0, st_re), (1, st_im)):
                        mm = pe.matmul(PS[32 * q:32 * q + 32, 7, t * T:(t + 1) * T], cT[:, ri, t, 32 * q:32 * q + 32],
                                       st[:, i, :], start=(ri == 0), stop=(ri == 1))
                mm.then_inc(sem("yd_ready"), 1)
                pe.wait_ge(sem("pb_ready"), l * 2 + 2)
                turn_probs(work[0], "ptb_turned")
                pe.wait_ge(sem("ptb_ready"), l * 3 + 3)
                mix_values(work[1], lambda kt, h: tokv[:, kt, 0:64], 4).then_inc(sem("ob_ready"), 1)
                pe.wait_ge(sem("pa_ready"), l * 2 + 2)
                pe.wait_ge(sem("ob_read"), l + 1)
                turn_probs(work[2], "pta_turned")
                pe.wait_ge(sem("yg_ready"), l + 1)
                for t in range(2):
                    for kt in range(2):
                        mm = pe.matmul(PS[:, 7, t * T:(t + 1) * T], glu_sb[:, kt, t * P:(t + 1) * P],
                                       tmp[3][:, kt * T:(kt + 1) * T], start=(kt == 0), stop=(kt == 1))
                mm.then_inc(sem("glu_ready"), 1)
                pe.wait_ge(sem("pta_ready"), l * 3 + 3)
                mix_values(work[3], lambda kt, h: tokv[:, kt, 64 + 64 * (h // 2):128 + 64 * (h // 2)], 4
                           ).then_inc(sem("oa_ready"), 1)
                settle(pe)
                pe.wait_ge(sem("rows_ready"), l * 2 + 2)
                for k in range(2):
                    for tt in range(2):
                        mm = pe.transpose(PS[:, 6, (2 * k + tt) * 4:(2 * k + tt) * 4 + 4],
                                          rows[:, (2, 3)[k], tt * P:(tt + 1) * P], ident[0:H, 0:H])
                mm.then_inc(sem("cols_turned"), 1)
                pe.wait_ge(sem("oa_read"), l + 1)
                for h in range(H):
                    mm = pe.matmul(PS[:, 4 + h // 2, (h % 2) * T:(h % 2 + 1) * T], ident[0:H, h:h + 1].to_broadcast([H, P]),
                                   rows[:, 1, :], start=True, stop=True)
                mm.then_inc(sem("g_spread"), 1)

                def y_chunk(m):
                    g = G_MIX + m
                    pe.wait_ge(sem(f"w_out_loaded{g % 2}"), ring_use(l, g) * 16 + 16)
                    for k, kt in enumerate(OUT_TILES[m]):
                        for b in range(4):
                            tt, hf = b // 2, b % 2
                            mm = pe.matmul(PS[:, b, :], oT[:, kt, tt * P:(tt + 1) * P],
                                           w_out_ring[g % 2][:, k, hf * 512:(hf + 1) * 512],
                                           start=False, stop=(m == 5))
                            if m == 5:
                                mm.then_inc(sem("y_ready"), 1)
                    pe.drain().then_inc(sem(f"w_out_used{g % 2}"), 1)

                pe.wait_ge(sem("sa_read"), l + 1)
                seed_y()
                pe.wait_ge(sem("od_ready"), l + 1)
                y_chunk(0)
                pe.wait_ge(sem("w_args_ready"), l + 1)
                pe.wait_ge(sem("cols_ready"), l * 2 + 2)
                pe.wait_ge(sem("qk_ready"), l + 1)
                for h in range(H):
                    for s_t, w in ((0, T), (1, P)):
                        mm = pe.matmul(PS[:, 4 + h, (0, T)[s_t]:(0, T)[s_t] + w],
                                       qkT[half(h), 2 + h // 2, s_t * P:(s_t + 1) * P], qkT[half(h), h // 2, T - w:T],
                                       start=True, stop=True)
                mm.then_inc(sem("st_ready"), 1)
                y_chunk(1)
                pe.wait_ge(sem("pc_ready"), l + 1)
                for tt in range(2):
                    for h in range(H):
                        o = PS[:, 4 + tt, h * 65:(h + 1) * 65]
                        mm = pe.matmul(o, work[0][:, h, tt * P:(tt + 1) * P], vaug[:, 0, h, :], start=True, stop=(tt == 0))
                        if tt == 1:
                            mm = pe.matmul(o, work[0][:, h, T:T + P], vaug[:, 1, h, :], start=False, stop=True)
                mm.then_inc(sem("num_ready"), 1)
                y_chunk(2)
                y_chunk(3)
                pe.wait_ge(sem("hn_ready"), l + 1)
                for pr in range(2):
                    for tt in range(2):
                        mm = pe.transpose(PS[:, 6, pr * T + tt * P:pr * T + (tt + 1) * P],
                                          hn[:, tt, 2 * pr:2 * pr + 2, :].rearrange("p h e -> p (h e)"), ident[:, :])
                mm.then_inc(sem("hn_turned"), 1)
                pe.wait_ge(sem("oc_ready"), l * 2 + 2)
                y_chunk(4)
                y_chunk(5)
                pe.drain().then_inc(sem("mixer_params_used"), 1)
                turn(xn, l, 1)

                pe.wait_ge(sem("uT_act"), l * 12 + 12)
                pe.wait_ge(sem("uT_dve"), l * 12 + 12)
                pe.wait_ge(sem("y_read"), l * 12 + 12)
                seed_y()
                pe.wait_ge(sem("uT_split"), l * 8 + 8)

                def ffn_pair(it, group):
                    for j in range(2):
                        ffn_chunk((G_FFN2 + j) % 2, ff_tile(l, 1, it, j), False)
                        if group is not None:
                            for n in (2 * j, 2 * j + 1):
                                ada_sum(l * 36 + group * 4 + (12 + ADA_FFN1 + n), n, l * MODS + group + 8)

                ffn_pair(0, 0)
                with pe.Fori(0, 3) as it:
                    ffn_pair(it + 1, it + 1)
                ffn_pair(4, None)
                spread_gate(l * 3 + 2)
                ffn_chunk(1, ff_tile(l, 1, PAIRS, 0), True)
                release_out(1)
                pe.wait_ge(sem("mod_ready"), l * MODS + 12)
                pe.wait_ge(sem("h_done"), l * 44 + 46)
                pe.wait_ge(sem("gate_ready"), l * 6 + 6)
                turn(xn, l, 2)

        @block.vector
        def _(v):
            v.sem_inc(sem("h_done"), 2)
            v.wait_ge(sem("const_step"), 19)
            v.scalar_tensor_tensor(dist[:, :], dist[:, :], -1.0, dist[:, :], ALU.mult, ALU.max).then_inc(sem("dist_ready"), 1)
            v.wait_ge(sem("dist_ready"), 1)
            for h in range(H):
                v.scalar_tensor_tensor(bias_a[:, h, :], dist[:, :], -SLOPES_A[h], mask_a, ALU.mult, ALU.add
                                       ).then_inc(sem("bias_a_ready"), 1)
            v.wait_ge(sem("mask_turned"), 1)
            v.tensor_copy(block_mask[:, :], PS[:, 4, 0:P]).then_inc(sem("block_mask_ready"), 1)
            v.memset(b_blk[:, :, :, :], 0.0)
            v.memset(cos_t[:, :, 0:1], 1.0).then_inc(sem("rot_start"), 1)
            v.memset(sin_t[:, :, 0:1], 0.0).then_inc(sem("rot_start"), 1)
            v.memset(vaug[:, :, :, 64:65], 1.0).then_inc(sem("vaug_ones"), 1)

            def ada_chunk(slot, loaded, n, first=False):
                v.wait_ge(sem(f"ada_loaded{slot}"), loaded)
                if not first:
                    v.wait_ge(sem("ada_summed"), n - 1)
                w = ada_ring[slot]
                for t in range(8):
                    if t:
                        v.wait_ge(sem("acc_step"), n * 8 + t)
                    ins = v.scalar_tensor_tensor(acc[slot][:, :], w[:, t, :], cs[:, t:t + 1],
                                                 w[:, 8, :] if t == 0 else acc[slot][:, :], ALU.mult, ALU.add)
                    ins.then_inc(sem("acc_step"), 1)

            def mod_cols(dst, width, summed):
                v.wait_ge(sem("ada_summed"), summed)
                v.tensor_copy(mod[:, dst], PS[:, 6, 0:width]).then_inc(sem("mod_ready"), 1)

            def mod_ab(s, lng, n, mods):
                v.wait_ge(sem("mod_ready"), mods)
                sh, scl = mod[:, 24 * s:24 * s + 8], mod[:, 24 * s + 8:24 * s + 16]
                if lng is None:
                    v.tensor_scalar(mod_a[:, s, :], scl, 1.0, None, ALU.add).then_inc(sem("mod_step"), 1)
                    v.tensor_copy(mod_b[:, s, :], sh).then_inc(sem("mod_step"), 1)
                    v.tensor_copy(t8, sh).then_inc(sem("mod_step"), 1)
                else:
                    g, b = prm[:, R_LNG + 8 * lng:R_LNG + 8 * lng + 8], prm[:, R_LNB + 8 * lng:R_LNB + 8 * lng + 8]
                    v.scalar_tensor_tensor(mod_a[:, s, :], scl, 1.0, g, ALU.add, ALU.mult).then_inc(sem("mod_step"), 1)
                    v.wait_ge(sem("mod_step"), n * 3)
                    v.scalar_tensor_tensor(t8, scl, 1.0, b, ALU.add, ALU.mult).then_inc(sem("mod_step"), 1)
                    v.wait_ge(sem("mod_step"), n * 3 + 2)
                    v.tensor_tensor(mod_b[:, s, :], t8, sh, ALU.add).then_inc(sem("mod_step"), 1)

            def evac_uT(s, turned, ab, split=None):
                dst = uT if split is None else uT_lo
                v.wait_ge(sem("mod_step"), ab * 3)
                for j in range(4, KT):
                    if j % 2 == 0:
                        v.wait_ge(sem("x_turned"), turned + (TURN_ORDER.index(j + 1) + 1))
                    v.tensor_scalar(dst[:, j, :], PS[:, 4 + j // 2, (j % 2) * T:(j % 2 + 1) * T], mod_a[:, s, j:j + 1], mod_b[:, s, j:j + 1],
                                    ALU.mult, ALU.add).then_inc(sem("uT_dve"), 1)
                if split is None:
                    return
                v.wait_ge(sem("uT_dve"), turned // 2 + 4)
                for k in (2, 3):
                    two = slice(2 * k, 2 * k + 2)
                    v.tensor_copy(u_hi[:, two, :], uT_lo[:, two, :]).then_inc(sem("uT_high_dve"), 1)
                for k in (0, 2, 1, 3):
                    two = slice(2 * k, 2 * k + 2)
                    if k < 2:
                        v.wait_ge(sem("uT_high_act"), split * 2 + (k + 1))
                    else:
                        v.wait_ge(sem("uT_high_dve"), split * 2 + (k - 1))
                    v.tensor_tensor(u_lo[:, two, :], uT_lo[:, two, :], u_hi[:, two, :].bitcast(F32), ALU.subtract
                                    ).then_inc(sem("uT_split"), 1)

            def gate_diag(s, n, mods):
                v.wait_ge(sem("mod_ready"), mods)
                for hf in range(2):
                    if hf:
                        v.wait_ge(sem("gate_spread"), n * 2 + 1)
                    k = 24 * s + 16 + 4 * hf
                    v.tensor_tensor(diag.rearrange("p (a b) -> p a b", a=4), ident[:, :].unsqueeze(1).to_broadcast([P, 4, P]),
                                    mod[:, k:k + 4].unsqueeze(2).to_broadcast([P, 4, P]), ALU.mult
                                    ).then_inc(sem("diag_ready"), 1)

            def ffn_tile(ft, tile):
                v.wait_ge(sem("silu_ready"), tile + (ft + 1))
                v.tensor_tensor(h_ring[:, ft, :], silu_ring[:, ft, :], PS[:, 4 + ft, T:2 * T], ALU.mult
                                ).then_inc(sem("h_step"), 1)
                v.wait_ge(sem("h_step"), tile * 2 + (2 * ft + 1))
                v.tensor_copy(h_parts[:, 2 + ft, :], h_ring[:, ft, :]).then_inc(sem("h_step"), 1)
                v.wait_ge(sem("h_step"), tile * 2 + (2 * ft + 2))
                v.tensor_tensor(h_parts[:, ft, :], h_ring[:, ft, :], h_parts[:, 2 + ft, :].bitcast(F32), ALU.subtract
                                ).then_inc(sem("h_done"), 1)

            def w_in_low(slot, ft, tile):
                v.wait_ge(sem("w_in_high"), tile + 1)
                v.tensor_tensor(w_in_tile(w_in_lo, slot, ft), w_in_tile(w_in_ring, slot, ft), w_in_hi[ft][:, :, :, :].bitcast(F32),
                                ALU.subtract).then_inc(sem("w_in_split"), 1)

            def w_out_low(slot, ft, tile):
                v.wait_ge(sem("w_out_high"), tile + 1)
                v.tensor_tensor(w_out_lo[slot][:, ft, :], w_out_ring[slot][:, ft, :], w_out_hi[ft][:, :].bitcast(F32), ALU.subtract
                                ).then_inc(sem("w_out_split"), 1)

            def ffn_chunk(slot, tile, ada, more):
                for ft in range(2):
                    w_out_low(slot, ft, tile + ft)
                for ft in range(2):
                    if ada is not None:
                        n, use = ada
                        ada_chunk(ft, 32 * (use + 1), n + ft)
                    ffn_tile(ft, tile)
                    if more:
                        w_in_low(1 - slot, ft, tile + (2 + ft))

            def deepnorm(l, s):
                n = l * 3 + s
                v.wait_ge(sem("gate_ready"), n * 2 + 2)
                v.wait_ge(sem("x_ready"), n * 2 + 2)
                for tt in range(2):
                    for hf in range(2):
                        b = 2 * tt + hf
                        v.wait_ge(sem("y_ready"), n * 4 + (b + 1))
                        v.tensor_tensor(xn[:, tt, hf * 512:(hf + 1) * 512], PS[:, b, :], gate_bc[:, hf * 512:(hf + 1) * 512],
                                        ALU.mult).then_inc(sem("y_read"), 1)
                    for hf in range(2):
                        b = 2 * tt + hf
                        v.wait_ge(sem("y_read"), n * 4 + (b + 5))
                        v.scalar_tensor_tensor(xn[:, tt, hf * 512:(hf + 1) * 512], x_sb[:, tt, hf * 512:(hf + 1) * 512], ALPHA,
                                               xn[:, tt, hf * 512:(hf + 1) * 512], ALU.mult, ALU.add
                                               ).then_inc(sem("r_ready"), 1)
                    for hf in range(2):
                        v.wait_ge(sem("r_ready"), n * 4 + (2 * tt + hf + 1))
                        v.bn_stats(stats[:, tt, hf, :], xn[:, tt, hf * 512:(hf + 1) * 512]).then_inc(sem("stats_ready"), 1)
                    settle(v)
                    v.wait_ge(sem("stats_ready"), n * 4 + (2 * tt + 2))
                    v.bn_aggr(mv[:, tt, :], stats[:, tt, :, :].rearrange("p a b -> p (a b)")).then_inc(sem("mv_ready"), 1)
                    v.wait_ge(sem("mv_ready"), n * 2 + (tt + 1))
                    v.tensor_scalar(var_eps[:, tt:tt + 1], mv[:, tt, 1:2], LN_EPS, None, ALU.add).then_inc(sem("var_ready"), 1)
                for tt in range(2):
                    v.wait_ge(sem("rstd_ready"), n * 2 + (tt + 1))
                    v.tensor_scalar(nmr[:, tt:tt + 1], mv[:, tt, 0:1], rstd[:, tt:tt + 1], -1.0, ALU.mult, ALU.mult
                                    ).then_inc(sem("nmr_ready"), 1)
                    v.wait_ge(sem("nmr_ready"), n * 2 + (tt + 1))
                    v.tensor_scalar(xn[:, tt, :], xn[:, tt, :], rstd[:, tt:tt + 1], nmr[:, tt:tt + 1], ALU.mult, ALU.add
                                    ).then_inc(sem("xn_ready"), 1)

            v.sem_inc(sem("y_read"), 4)
            v.wait_ge(sem("cs_ready"), 1)
            for gr in range(3):
                for n in range(4):
                    k = 4 * gr + n
                    ada_chunk(n % 2, 32 * (k // 2 + 1), k, first=k < 2)
                mod_cols(slice(8 * gr, 8 * gr + 8), 8, 4 * gr + 4)
            mod_ab(0, None, 0, 3)
            evac_uT(0, 0, 1, 0)

            with v.Fori(0, DEPTH) as l:
                for ft in range(2):
                    w_in_low(0, ft, ff_tile(l, 0, 0, 0) + ft)
                v.wait_ge(sem("prm_turned"), l + 1)
                v.tensor_copy(prm[:, :], PS[:, 4, 0:ROWS]).then_inc(sem("prm_ready"), 1)
                v.wait_ge(sem("prm_ready"), l + 1)
                step = [0]
                STEPS = 27

                def s5(ins):
                    ins.then_inc(sem("s5_step"), 1)
                    step[0] += 1
                    v.wait_ge(sem("s5_step"), l * STEPS + step[0])

                lr, li = prm[:, R_LR:R_LR + 8], prm[:, R_LI:R_LI + 8]
                v.wait_ge(sem("dt_ready"), l + 1)
                v.tensor_tensor(S5["lrdt"], lr, S5["dt"], ALU.mult).then_inc(sem("lrdt_ready"), 1)
                s5(v.tensor_tensor(S5["th"], li, S5["dt"], ALU.mult))
                s5(v.tensor_scalar(S5["n"], S5["th"], INV_2PI, MAGIC, ALU.mult, ALU.add))
                s5(v.tensor_scalar(S5["n"], S5["n"], MAGIC, None, ALU.subtract))
                s5(v.scalar_tensor_tensor(S5["r"], S5["n"], -TWO_PI_1, S5["th"], ALU.mult, ALU.add))
                s5(v.scalar_tensor_tensor(S5["r"], S5["n"], -TWO_PI_2, S5["r"], ALU.mult, ALU.add))
                s5(v.scalar_tensor_tensor(S5["r"], S5["n"], -TWO_PI_3, S5["r"], ALU.mult, ALU.add))
                v.tensor_scalar(S5["r0"], S5["r"], PI_BELOW, -PI_BELOW, ALU.min, ALU.max).then_inc(sem("angle_ready"), 1)
                v.wait_ge(sem("sin_ready"), l + 1)
                s5(v.tensor_tensor(S5["sh2"], S5["sinh"], S5["sinh"], ALU.mult))
                s5(v.tensor_scalar(S5["cos"], S5["sh2"], -2.0, 1.0, ALU.mult, ALU.add))
                v.tensor_copy(cos_t[:, :, 1:2], S5["cos"].unsqueeze(2)).then_inc(sem("rot_start"), 1)
                v.tensor_copy(sin_t[:, :, 1:2], S5["sin"].unsqueeze(2)).then_inc(sem("rot_start"), 1)
                s5(v.tensor_tensor(S5["a_re"], S5["rho"], S5["cos"], ALU.mult))
                s5(v.tensor_tensor(S5["a_im"], S5["rho"], S5["sin"], ALU.mult))
                s5(v.tensor_scalar(S5["am1"], S5["a_re"], 1.0, None, ALU.subtract))
                s5(v.tensor_tensor(S5["t1"], lr, lr, ALU.mult))
                s5(v.tensor_tensor(S5["t2"], li, li, ALU.mult))
                s5(v.tensor_tensor(S5["den"], S5["t1"], S5["t2"], ALU.add))
                s5(v.reciprocal(S5["rden"], S5["den"]))
                s5(v.tensor_tensor(S5["k1"], S5["am1"], lr, ALU.mult))
                s5(v.tensor_tensor(S5["k2"], S5["a_im"], li, ALU.mult))
                s5(v.tensor_tensor(S5["k1"], S5["k1"], S5["k2"], ALU.add))
                s5(v.tensor_tensor(S5["k_re"], S5["k1"], S5["rden"], ALU.mult))
                s5(v.tensor_tensor(S5["k3"], S5["a_im"], lr, ALU.mult))
                s5(v.tensor_tensor(S5["k4"], S5["am1"], li, ALU.mult))
                s5(v.tensor_tensor(S5["k3"], S5["k3"], S5["k4"], ALU.subtract))
                s5(v.tensor_tensor(S5["k_im"], S5["k3"], S5["rden"], ALU.mult))
                kre = S5["k_re"].unsqueeze(2).to_broadcast([P, 8, 16])
                kim = S5["k_im"].unsqueeze(2).to_broadcast([P, 8, 16])
                bt = [diag[:, k * P:(k + 1) * P].rearrange("p (i c) -> p i c", c=16) for k in range(4)]
                s5(v.tensor_tensor(bt[0], b_raw[:, 0, :, :], kre, ALU.mult))
                s5(v.tensor_tensor(bt[1], b_raw[:, 1, :, :], kim, ALU.mult))
                s5(v.tensor_tensor(bt[2], b_raw[:, 1, :, :], kre, ALU.mult))
                s5(v.tensor_tensor(bt[3], b_raw[:, 0, :, :], kim, ALU.mult))
                for two_ in range(2):
                    ph = slice(64 * two_, 64 * two_ + 64)
                    v.tensor_tensor(b_blk[ph, 0, :, 16 * two_:16 * two_ + 16], bt[0][ph], bt[1][ph], ALU.subtract
                                    ).then_inc(sem("b_blk_ready"), 1)
                    v.tensor_tensor(b_blk[ph, 1, :, 16 * two_:16 * two_ + 16], bt[2][ph], bt[3][ph], ALU.add
                                    ).then_inc(sem("b_blk_ready"), 1)
                for k, sign in ((0, 1.0), (1, -1.0)):
                    v.scalar_tensor_tensor(c_blk[:, k, :, :], c_blk[:, k, :, :], sign,
                                           block_mask[:, :].unsqueeze(1).to_broadcast([P, 2, P]), ALU.mult, ALU.mult
                                           ).then_inc(sem("c_blk_ready"), 1)
                assert step[0] == STEPS

                with v.Fori(0, PAIRS) as it:
                    for j in range(2):
                        ffn_chunk(j, ff_tile(l, 0, it, j),
                                  (l * 36 + it * 4 + (12 + 2 * j), ada_use(l, 0, it * 2 + j)), True)
                    mod_cols(bass.ds(24 + it * 8, 8), 8, l * 36 + it * 4 + 16)
                gate_diag(0, l * 3, l * MODS + 3)
                v.wait_ge(sem("bb_turned"), l + 1)
                v.tensor_copy(bbT[:, :, :, :].rearrange("p a b c -> p (a b c)"), PS[:, 7, :]).then_inc(sem("bbT_ready"), 1)
                v.wait_ge(sem("c_turned"), l + 1)
                v.tensor_copy(cT[:, :, :, :].rearrange("p a b c -> p (a b c)"), PS[:, 7, :]).then_inc(sem("cT_ready"), 1)
                ffn_chunk(0, ff_tile(l, 0, PAIRS, 0), None, False)
                mod_ab(1, 0, l * 3 + 1, l * MODS + 8)
                mod_ab(2, 1, l * 3 + 2, l * MODS + 8)
                deepnorm(l, 0)
                evac_uT(1, l * 24 + 8, l * 3 + 2)

                gate_diag(1, l * 3 + 1, l * MODS + 6)

                def tiles2(ap):
                    return ap.rearrange("p (a b) -> p a b", a=2)

                def s5_rotate_in(b):
                    v.wait_ge(sem("bu_ready"), l * 4 + (b + 1))
                    if b >= 2:
                        v.wait_ge(sem("rotated_in"), l * 8 + 2 * (b - 1))
                    tl = slice(2 * b, 2 * b + 2)
                    bk = 2 * (b % 2)
                    re, im = PS[:, bk:bk + 2, 0:T], PS[:, bk:bk + 2, T:2 * T]
                    v.tensor_tensor(st_re[:, tl, :], re, cos_t[:, tl, :], ALU.mult)
                    v.tensor_tensor(tiles2(tmp[2 * (b % 2)]), im, sin_t[:, tl, :], ALU.mult)
                    v.tensor_tensor(st_im[:, tl, :], im, cos_t[:, tl, :], ALU.mult)
                    v.tensor_tensor(tiles2(tmp[2 * (b % 2) + 1]), re, sin_t[:, tl, :], ALU.mult).then_inc(sem("bu_read"), 1)

                def s5_scan(b):
                    v.wait_ge(sem("rotated_in"), l * 8 + 2 * (b + 1))
                    for i in (2 * b, 2 * b + 1):
                        for st in (st_re, st_im):
                            ins = v.tensor_tensor_scan(st[:, i, :], S5["rho"][:, i:i + 1].to_broadcast([P, T]), st[:, i, :],
                                                       0.0, ALU.mult, ALU.add)
                    ins.then_inc(sem("scanned"), 1)

                def s5_rotate_out(b):
                    v.wait_ge(sem("scanned"), l * 4 + (b + 1))
                    v.wait_ge(sem("rotated_in"), l * 8 + 8)
                    if b:
                        v.wait_ge(sem("rotated_out"), l * 8 + 2 * b)
                    tl = slice(2 * b, 2 * b + 2)
                    v.tensor_tensor(tiles2(tmp[0]), st_re[:, tl, :], cos_t[:, tl, :], ALU.mult)
                    v.tensor_tensor(tiles2(tmp[1]), st_im[:, tl, :], sin_t[:, tl, :], ALU.mult)
                    v.tensor_tensor(tiles2(tmp[2]), st_re[:, tl, :], sin_t[:, tl, :], ALU.mult)
                    v.tensor_tensor(tiles2(tmp[3]), st_im[:, tl, :], cos_t[:, tl, :], ALU.mult).then_inc(sem("rotating_out"), 1)

                v.wait_ge(sem("rot_step"), (l + 1) * ROT_STEPS)
                s5_rotate_in(0)
                s5_rotate_in(1)
                s5_scan(0)
                s5_rotate_in(2)
                s5_scan(1)
                s5_rotate_in(3)
                s5_scan(2)
                v.wait_ge(sem("ln_f_ready"), l + 1)
                lf, bsum, gmx = (work[3][0:H, k, 0:T] for k in (1, 2, 3))
                v.scalar_tensor_tensor(lf, rows[:, 1, :], 0.0, lf, ALU.min, ALU.subtract).then_inc(sem("lf_ready"), 1)
                s5_scan(3)
                v.wait_ge(sem("lf_ready"), l + 1)
                v.tensor_tensor_scan(bsum, ones[0:H, 0:1].to_broadcast([H, T]), lf, 0.0, ALU.mult, ALU.add
                                     ).then_inc(sem("bsum_ready"), 1)
                v.wait_ge(sem("bsum_ready"), l + 1)
                v.tensor_tensor(rows[:, 2, :], rows[:, 0, :], bsum, ALU.subtract).then_inc(sem("r_row_ready"), 1)
                v.wait_ge(sem("r_row_ready"), l + 1)
                v.tensor_tensor_scan(gmx, ones[0:H, 0:1].to_broadcast([H, T]), rows[:, 2, :], 0.0, ALU.mult, ALU.max
                                     ).then_inc(sem("gmx_ready"), 1)
                v.wait_ge(sem("gmx_ready"), l + 1)
                v.tensor_scalar(rows[:, 1, :], gmx, -1.0, None, ALU.mult).then_inc(sem("rows_ready"), 1)
                v.scalar_tensor_tensor(rows[:, 3, :], bsum, -1.0, gmx, ALU.mult, ALU.subtract).then_inc(sem("rows_ready"), 1)

                v.wait_ge(sem("idx_read"), l + 1)
                for h in range(H):
                    if h:
                        v.wait_ge(sem("idx_sum"), l * 8 + 2 * h)
                    for tt, cols in ((0, slice(0, P)), (1, slice(P, 384))):
                        w = tokv[:, tt, 192 + h:193 + h]
                        src = work[0][:, h, cols]
                        if h == 0:
                            v.tensor_scalar(sc[:, cols], src, w, None, ALU.mult).then_inc(sem("idx_sum"), 1)
                        else:
                            v.scalar_tensor_tensor(sc[:, cols], src, w, sc[:, cols], ALU.mult, ALU.add
                                                   ).then_inc(sem("idx_sum"), 1)
                v.wait_ge(sem("idx_sum"), l * 8 + 8)
                v.scalar_tensor_tensor(sc[:, :], sc[:, :], IDX_SCALE, mask_b[:, :], ALU.mult, ALU.add
                                       ).then_inc(sem("idx_score"), 1)
                settle(v)
                v.wait_ge(sem("idx_score"), l + 1)
                for k in range(TOPK // 8):
                    for tt, cols in ((0, slice(0, P)), (1, slice(P, 384))):
                        if k:
                            settle(v)
                            v.wait_ge(sem("top_taken"), l * 16 + (2 * (k - 1) + tt + 1))
                        v.max(m8[:, tt, :], sc[:, cols]).then_inc(sem("top_found"), 1)
                    for tt, cols in ((0, slice(0, P)), (1, slice(P, 384))):
                        v.wait_ge(sem("top_found"), l * 16 + (2 * k + tt + 1))
                        waited(v)
                        v.match_replace(sc[:, cols], m8[:, tt, :], sc[:, cols], TAKEN).then_inc(sem("top_taken"), 1)
                    if k % 2:
                        s5_rotate_out(k // 2)
                v.wait_ge(sem("top_taken"), l * 16 + 16)
                v.tensor_scalar(sc[:, :], sc[:, :], TAKEN / 2, NEG, ALU.is_gt, ALU.mult).then_inc(sem("sel_step"), 1)
                v.wait_ge(sem("sel_step"), l * 2 + 1)
                v.tensor_tensor(sc[:, :], sc[:, :], mask_b[:, :], ALU.add).then_inc(sem("sel_step"), 1)
                v.wait_ge(sem("sel_step"), l * 2 + 2)
                for h in range(H):
                    v.scalar_tensor_tensor(work[1][:, h, :], dist[:, :], -SLOPES_B[h], sc[:, :], ALU.mult, ALU.add
                                           ).then_inc(sem("bias_b"), 1)

                def logits(bias, dst, ready, read, mx, nmx, name, sink):
                    v.wait_ge(sem(ready), l + 1)
                    v.scalar_tensor_tensor(dst[:, :, :], PS[:, 0:4, 0:384], HD ** -0.5, bias[:, :, :], ALU.mult, ALU.add
                                           ).then_inc(sem(read), 1)
                    v.wait_ge(sem(read), l + 1)
                    for tt, cols in ((0, slice(0, P)), (1, slice(P, 384))):
                        v.tensor_reduce(heads(mx)[:, tt, :], dst[:, :, cols], AX, ALU.max).then_inc(sem(name + "_max"), 1)
                    v.wait_ge(sem(name + "_max"), l * 2 + 2)
                    if sink is not None:
                        v.tensor_tensor(mx, mx, sink, ALU.max).then_inc(sem(name + "_smax"), 1)
                        v.wait_ge(sem(name + "_smax"), l + 1)
                    v.tensor_scalar(nmx, mx, -1.0, None, ALU.mult).then_inc(sem(name + "_nmax"), 1)

                v.wait_ge(sem("bias_b"), l * 4 + 4)
                logits(work[1], work[0], "sb_ready", "sb_read", mx_b, nmx_b, "b", None)

                v.wait_ge(sem("z_read"), l * NZ + 16)
                for j in range(3, -1, -1):
                    lag = 3 - j
                    for t in range(4):
                        w = col(R_CW, 4 * j + t)
                        if lag == 0:
                            v.tensor_scalar(qkT[:, t, :], qk_raw[:, t, :], w, col(R_CB, t), ALU.mult, ALU.add
                                            ).then_inc(sem("conv_step"), 1)
                        else:
                            v.wait_ge(sem("conv_step"), l * 16 + (4 * (lag - 1) + t + 1))
                            v.scalar_tensor_tensor(qkT[:, t, lag:T], qk_raw[:, t, 0:T - lag], w, qkT[:, t, lag:T],
                                                   ALU.mult, ALU.add).then_inc(sem("conv_step"), 1)

                v.wait_ge(sem("b_exp"), l * 8 + 8)
                v.reciprocal(ri_b, rs_b).then_inc(sem("rib_ready"), 1)

                sk = sinks_sb[:, :, :].rearrange("p t h -> p (t h)")
                v.wait_ge(sem("bias_a_ready"), 4)
                logits(bias_a, work[2], "sa_ready", "sa_read", mx_a, nmx_a, "a", sk)
                v.tensor_tensor(ds_a, sk, mx_a, ALU.subtract).then_inc(sem("sink_arg"), 1)

                v.wait_ge(sem("yd_ready"), l + 1)
                v.wait_ge(sem("rotated_out"), l * 8 + 8)
                for t in range(2):
                    v.scalar_tensor_tensor(tmp[0][:, t * T:(t + 1) * T], udT[:, t, :], col(R_DS, t), PS[:, 7, t * T:(t + 1) * T],
                                           ALU.mult, ALU.add).then_inc(sem("yd_read"), 1)
                v.wait_ge(sem("conv_tanh"), l + 1)
                v.scalar_tensor_tensor(qkT[:, :, :].rearrange("p a b -> p (a b)"), qk_tanh, 1.0,
                                       qkT[:, :, :].rearrange("p a b -> p (a b)"), ALU.add, ALU.mult).then_inc(sem("qk_ready"), 1)
                v.wait_ge(sem("gelu_sq"), l + 1)
                v.tensor_scalar(tmp[1], tmp[1], GELU_C, 1.0, ALU.mult, ALU.add).then_inc(sem("gelu_step"), 1)
                v.wait_ge(sem("gelu_step"), l * 2 + 1)
                v.tensor_tensor(tmp[1], tmp[1], tmp[0], ALU.mult).then_inc(sem("gelu_step"), 1)
                v.wait_ge(sem("a_exp"), l * 9 + 9)
                v.tensor_tensor(rs_a, rs_a, es_a, ALU.add).then_inc(sem("rsa_sum"), 1)
                v.wait_ge(sem("rsa_sum"), l + 1)
                v.reciprocal(ri_a, rs_a).then_inc(sem("ria_ready"), 1)
                v.wait_ge(sem("gelu_tanh"), l + 1)
                v.scalar_tensor_tensor(tmp[3], tmp[1], 1.0, tmp[0], ALU.add, ALU.mult).then_inc(sem("yg_ready"), 1)
                v.wait_ge(sem("glu_tanh"), l + 1)
                v.scalar_tensor_tensor(tmp[0], tmp[2], 1.0, tmp[3], ALU.add, ALU.mult).then_inc(sem("od_step"), 1)
                v.wait_ge(sem("od_step"), l + 1)
                v.tensor_scalar(oT[:, 6:8, :].rearrange("p a b -> p (a b)"), tmp[0], 0.25, None, ALU.mult
                                ).then_inc(sem("od_ready"), 1)

                v.wait_ge(sem("cols_turned"), l + 1)
                v.tensor_copy(rcol, PS[:, 6, 0:8]).then_inc(sem("cols_ready"), 1)
                v.tensor_copy(nmcol, PS[:, 6, 8:16]).then_inc(sem("cols_ready"), 1)
                v.wait_ge(sem("cols_ready"), l * 2 + 2)
                v.wait_ge(sem("g_spread"), l + 1)
                for h in range(H):
                    g = PS[:, 4 + h // 2, (h % 2) * T:(h % 2 + 1) * T]
                    v.scalar_tensor_tensor(work[0][:, h, 0:T], g, heads(rcol)[:, 0, h:h + 1], mask_c[:, :], ALU.add, ALU.add)
                    ins = v.scalar_tensor_tensor(work[0][:, h, T:384], g[:, P:T], heads(rcol)[:, 1, h:h + 1], mask_c[:, 0:P],
                                                 ALU.add, ALU.add)
                ins.then_inc(sem("w_args_ready"), 1)
                v.wait_ge(sem("st_ready"), l + 1)
                v.wait_ge(sem("w_exp"), l + 1)
                v.scalar_tensor_tensor(work[0][:, :, :], PS[:, 4:8, 0:384], HD ** -0.5 / 4, work[0][:, :, :], ALU.mult, ALU.mult
                                       ).then_inc(sem("pc_ready"), 1)
                v.wait_ge(sem("num_ready"), l + 1)
                num = PS[:, 4:6, 0:260].rearrange("p t (h e) -> p t h e", h=H)
                v.wait_ge(sem("den_ready"), l + 1)
                v.tensor_tensor(dmx, den, enm, ALU.max).then_inc(sem("den_step"), 1)
                v.wait_ge(sem("den_step"), l * 2 + 1)
                v.reciprocal(rden_c, dmx).then_inc(sem("den_step"), 1)
                v.wait_ge(sem("den_step"), l * 2 + 2)

                def over_e(ap):
                    return ap.unsqueeze(2).to_broadcast([P, 8, HD])

                for tt in range(2):
                    v.tensor_tensor(hs[:, tt, :, :], num[:, tt, :, 0:HD],
                                    heads(rden_c)[:, tt, :].unsqueeze(2).to_broadcast([P, H, HD]), ALU.mult
                                    ).then_inc(sem("hs_ready"), 1)
                hs8 = hs[:, :, :, :].rearrange("p t h e -> p (t h) e")
                hn8 = hn[:, :, :, :].rearrange("p t h e -> p (t h) e")
                v.wait_ge(sem("hs_ready"), l * 2 + 2)
                v.tensor_reduce(s1, hs8, AX, ALU.add).then_inc(sem("hn_step"), 1)
                v.wait_ge(sem("hn_step"), l * 5 + 1)
                v.tensor_scalar(mu, s1, 1.0 / HD, None, ALU.mult).then_inc(sem("hn_step"), 1)
                v.wait_ge(sem("hn_step"), l * 5 + 2)
                v.tensor_tensor(hs8, hs8, over_e(mu), ALU.subtract).then_inc(sem("hn_step"), 1)
                v.wait_ge(sem("hn_step"), l * 5 + 3)
                v.tensor_tensor(hn8, hs8, hs8, ALU.mult).then_inc(sem("hn_step"), 1)
                v.wait_ge(sem("hn_step"), l * 5 + 4)
                v.tensor_reduce(s2, hn8, AX, ALU.add).then_inc(sem("hn_step"), 1)
                v.wait_ge(sem("hn_step"), l * 5 + 5)
                v.tensor_scalar(var_c, s2, 1.0 / HD, LN_EPS, ALU.mult, ALU.add).then_inc(sem("varc_ready"), 1)
                v.wait_ge(sem("rstdc_ready"), l + 1)
                v.tensor_tensor(hn8, hs8, over_e(rstd_c), ALU.mult).then_inc(sem("hn_ready"), 1)
                v.wait_ge(sem("hn_turned"), l + 1)
                v.wait_ge(sem("sig_ready"), l + 1)
                for t in range(2):
                    v.scalar_tensor_tensor(oT[:, 4 + t, :], PS[:, 6, t * T:(t + 1) * T], col(R_MHG, t), sig_o[:, t, :],
                                           ALU.mult, ALU.mult).then_inc(sem("oc_ready"), 1)
                for ft in range(2):
                    w_in_low(G_FFN2 % 2, ft, ff_tile(l, 1, 0, 0) + ft)
                deepnorm(l, 1)
                evac_uT(2, l * 24 + 16, l * 3 + 3, l * 2 + 1)

                def ffn_pair(it, group):
                    for j in range(2):
                        ffn_chunk((G_FFN2 + j) % 2, ff_tile(l, 1, it, j), None if group is None else
                                  (l * 36 + group * 4 + (12 + ADA_FFN1 + 2 * j), ada_use(l, ADA_FFN1 + 2 * j, group * 2)), True)

                ffn_pair(0, 0)
                mod_cols(slice(64, 72), 8, l * 36 + (16 + ADA_FFN1))
                with v.Fori(0, 3) as it:
                    ffn_pair(it + 1, it + 1)
                    mod_cols(bass.ds(it * 8, 8), 8, l * 36 + it * 4 + (20 + ADA_FFN1))
                ffn_pair(4, None)
                gate_diag(2, l * 3 + 2, l * MODS + 9)
                ffn_chunk(1, ff_tile(l, 1, PAIRS, 0), None, False)
                mod_ab(0, 2, l * 3 + 3, l * MODS + 12)
                deepnorm(l, 2)
                evac_uT(0, l * 24 + 24, l * 3 + 4, l * 2 + 2)

        @block.scalar
        def _(a):
            a.wait_ge(sem("c_loaded"), 16)
            a.activation(cs[:, :], c_sb[:, :], ACT.Silu).then_inc(sem("cs_ready"), 1)

            def evac_uT(s, turned, ab, split=None):
                dst = uT if split is None else uT_lo
                a.wait_ge(sem("mod_step"), ab * 3)
                for j in range(4):
                    if j % 2 == 0:
                        a.wait_ge(sem("x_turned"), turned + (TURN_ORDER.index(j + 1) + 1))
                    a.activation(dst[:, j, :], PS[:, 4 + j // 2, (j % 2) * T:(j % 2 + 1) * T], ACT.Identity, bias=mod_b[:, s, j:j + 1],
                                 scale=mod_a[:, s, j:j + 1]).then_inc(sem("uT_act"), 1)
                if split is None:
                    return
                for k in (0, 1):
                    two = slice(2 * k, 2 * k + 2)
                    a.wait_ge(sem("uT_act"), turned // 2 + (2 * k + 2))
                    a.activation(u_hi[:, two, :], uT_lo[:, two, :], ACT.Copy).then_inc(sem("uT_high_act"), 1)

            def copy_gate(n, factor):
                for hf in range(2):
                    a.wait_ge(sem("gate_spread"), n * 2 + (hf + 1))
                    a.activation(gate_bc[:, hf * 512:(hf + 1) * 512], PS[:, 7, :], ACT.Copy, scale=factor
                                 ).then_inc(sem("gate_ready"), 1)

            def silu_tile(ft, tile):
                a.wait_ge(sem("ag_ready"), tile + (ft + 3))
                a.wait_ge(sem("h_done"), tile + (ft + 1))
                a.activation(silu_ring[:, ft, :], PS[:, 4 + ft, 0:T], ACT.Silu).then_inc(sem("silu_ready"), 1)

            def w_in_high(slot, ft, tile):
                a.wait_ge(sem("ag_ready"), tile + 1)
                a.activation(w_in_hi[ft][:, :, :, :], w_in_tile(w_in_ring, slot, ft), ACT.Copy).then_inc(sem("w_in_high"), 1)

            def ffn_chunk(l, f, it, j, more):
                g = (0, G_FFN2)[f] + j
                slot = g % 2
                tile = ff_tile(l, f, it, j)
                a.wait_ge(sem(f"w_out_loaded{slot}"), ring_use(l, g, it) * 16 + 16)
                a.wait_ge(sem(f"w_out_used{1 - slot}"), ring_use(l, g - 1, it) + 2)
                for ft in range(2):
                    a.activation(w_out_hi[ft][:, :], w_out_ring[slot][:, ft, :], ACT.Copy).then_inc(sem("w_out_high"), 1)
                for ft in range(2):
                    silu_tile(ft, tile)
                    if more:
                        if ft == 0:
                            a.wait_ge(sem(f"w_in_loaded{1 - slot}"), in_loads(l, f, it, j + 1))
                        w_in_high(1 - slot, ft, tile + (2 + ft))

            a.wait_ge(sem("bias_a_ready"), 4)
            a.wait_ge(sem("block_mask_ready"), 1)
            evac_uT(0, 0, 1, 0)
            with a.Fori(0, DEPTH) as l:
                a.wait_ge(sem("w_in_loaded0"), in_loads(l, 0, 0, 0))
                for ft in range(2):
                    w_in_high(0, ft, ff_tile(l, 0, 0, 0) + ft)
                a.wait_ge(sem("prm_ready"), l + 1)
                a.activation(S5["dt"], log_dt[:, :], ACT.Exp).then_inc(sem("dt_ready"), 1)
                a.wait_ge(sem("lrdt_ready"), l + 1)
                a.activation(S5["rho"], S5["lrdt"], ACT.Exp)
                a.wait_ge(sem("angle_ready"), l + 1)
                a.activation(S5["sin"], S5["r0"], ACT.Sin)
                a.activation(S5["sinh"], S5["r0"], ACT.Sin, scale=0.5).then_inc(sem("sin_ready"), 1)
                with a.Fori(0, PAIRS) as it:
                    for j in range(2):
                        ffn_chunk(l, 0, it, j, True)
                copy_gate(l * 3, 0.5)
                ffn_chunk(l, 0, PAIRS, 0, False)
                evac_uT(1, l * 24 + 8, l * 3 + 2)

                copy_gate(l * 3 + 1, 1.0)

                def z_in(n):
                    a.wait_ge(sem("z_ready"), l * NZ + (n + 1))
                    return PS[:, 4 + n % 4, 0:T]

                def z_copy(n, dst, w=T):
                    a.activation(dst, z_in(n)[:, 0:w], ACT.Copy).then_inc(sem("z_read"), 1)

                z_copy(0, udT[:, 0, :])
                z_copy(1, udT[:, 1, :])
                z_copy(2, kiT[:, :])
                z_copy(3, cqT[:, :])
                z_copy(4, tokv[:, 0, :], 196)
                z_copy(5, tokv[:, 1, :], 196)
                z_copy(6, kbT[:, :])
                a.wait_ge(sem("ln_bc_used"), l * 3 + 2)
                for n in (7, 8):
                    a.activation(rows[:, n - 7, :], z_in(n)[0:H, :], ACT.Identity, bias=gate_bias[:, n - 7:n - 6]
                                 ).then_inc(sem("z_read"), 1)
                z_copy(9, qiT[:, :])
                z_copy(10, qbT[:, 0, :])
                z_copy(11, qbT[:, 1, :])
                e_row, ln_row = work[3][0:H, 0, 0:T], work[3][0:H, 1, 0:T]
                a.wait_ge(sem("z_read"), l * NZ + 12)
                a.activation(e_row, rows[:, 1, :], ACT.Abs).then_inc(sem("f_step"), 1)
                a.wait_ge(sem("f_step"), l * 2 + 1)
                a.activation(e_row, e_row, ACT.Exp, scale=-1.0).then_inc(sem("f_step"), 1)
                a.wait_ge(sem("f_step"), l * 2 + 2)
                a.activation(ln_row, e_row, ACT.Ln, bias=1.0).then_inc(sem("ln_f_ready"), 1)
                z_copy(12, qk_raw[:, 0, :])
                z_copy(13, qk_raw[:, 1, :])
                a.wait_ge(sem("idx_ready"), l + 1)
                a.activation(work[0][:, :, :], PS[:, 0:4, 0:384], ACT.Relu).then_inc(sem("idx_read"), 1)
                z_copy(14, qk_raw[:, 2, :])
                z_copy(15, qk_raw[:, 3, :])
                for n in range(16, 18):
                    z_copy(n, qaT[:, n - 16, :])
                for n in range(18, 20):
                    z_copy(n, kaT[:, n - 18, :])
                a.wait_ge(sem("vaug_ones"), 1)
                for n in (20, 21):
                    a.activation(vaug[:, n - 20, :, 0:HD], z_in(n).rearrange("p (h e) -> p h e", h=H), ACT.Copy
                                 ).then_inc(sem("z_read"), 1)
                for n in (22, 23):
                    a.activation(sig_o[:, n - 22, :], z_in(n), ACT.Tanh, scale=0.5).then_inc(sem("z_read"), 1)

                def exps(p, nmx, rs, name, ready):
                    a.wait_ge(sem(ready), l + 1)
                    for tt, cols in ((0, slice(0, P)), (1, slice(P, 384))):
                        for h in range(H):
                            a.activation(p[:, h, cols], p[:, h, cols], ACT.Exp, bias=heads(nmx)[:, tt, h:h + 1],
                                         accum_out=heads(rs)[:, tt, h:h + 1]).then_inc(sem(name), 1)

                exps(work[0], nmx_b, rs_b, "b_exp", "b_nmax")
                a.wait_ge(sem("conv_step"), l * 16 + 16)
                a.wait_ge(sem("sb_read"), l + 1)
                a.activation(qk_tanh, qkT[:, :, :].rearrange("p a b -> p (a b)"), ACT.Tanh, scale=0.5).then_inc(sem("conv_tanh"), 1)
                exps(work[2], nmx_a, rs_a, "a_exp", "a_nmax")
                a.wait_ge(sem("sink_arg"), l + 1)
                a.activation(es_a, ds_a, ACT.Exp).then_inc(sem("a_exp"), 1)
                a.wait_ge(sem("yd_read"), l * 2 + 2)
                a.activation(tmp[1], tmp[0], ACT.Square).then_inc(sem("gelu_sq"), 1)
                a.wait_ge(sem("qk_ready"), l + 1)
                ptb = work[1][:, :, :].rearrange("p h n -> p (h n)")
                pta = work[3][:, :, :].rearrange("p h n -> p (h n)")
                for b in range(3):
                    a.wait_ge(sem("ptb_turned"), l * 3 + (b + 1))
                    a.activation(ptb[:, b * 512:(b + 1) * 512], PS[:, 4 + b, :], ACT.Copy).then_inc(sem("ptb_ready"), 1)
                a.wait_ge(sem("gelu_step"), l * 2 + 2)
                a.activation(tmp[1], tmp[1], ACT.Tanh, scale=GELU_S).then_inc(sem("gelu_tanh"), 1)
                a.wait_ge(sem("ob_ready"), l + 1)
                a.activation(oT[:, 2:4, :].rearrange("p a b -> p (a b)"), PS[:, 4, :], ACT.Copy).then_inc(sem("ob_read"), 1)
                a.wait_ge(sem("rows_ready"), l * 2 + 2)
                for b in range(3):
                    a.wait_ge(sem("pta_turned"), l * 3 + (b + 1))
                    a.activation(pta[:, b * 512:(b + 1) * 512], PS[:, 4 + b, :], ACT.Copy).then_inc(sem("pta_ready"), 1)
                a.wait_ge(sem("gb_half_ready"), l + 1)
                a.wait_ge(sem("glu_ready"), l + 1)
                for t in range(2):
                    ins = a.activation(tmp[2][:, t * T:(t + 1) * T], PS[:, 7, t * T:(t + 1) * T], ACT.Tanh, scale=0.25,
                                       bias=gb_half[:, t:t + 1])
                ins.then_inc(sem("glu_tanh"), 1)
                a.wait_ge(sem("oa_ready"), l + 1)
                a.activation(oT[:, 0:2, :].rearrange("p a b -> p (a b)"), PS[:, 4, :], ACT.Copy).then_inc(sem("oa_read"), 1)
                a.wait_ge(sem("cols_ready"), l * 2 + 2)
                a.activation(enm, nmcol, ACT.Exp)
                a.wait_ge(sem("w_args_ready"), l + 1)
                a.activation(work[0][:, :, :], work[0][:, :, :], ACT.Exp).then_inc(sem("w_exp"), 1)
                a.wait_ge(sem("num_ready"), l + 1)
                a.activation(heads(den), PS[:, 4:6, 0:260].rearrange("p t (h e) -> p t h e", h=H)[:, :, :, 64], ACT.Abs
                             ).then_inc(sem("den_ready"), 1)
                a.wait_ge(sem("hn_turned"), l + 1)
                a.wait_ge(sem(f"w_in_loaded{G_FFN2 % 2}"), in_loads(l, 1, 0, 0))
                for ft in range(2):
                    w_in_high(G_FFN2 % 2, ft, ff_tile(l, 1, 0, 0) + ft)
                evac_uT(2, l * 24 + 16, l * 3 + 3, l * 2 + 1)

                with a.Fori(0, PAIRS) as it:
                    for j in range(2):
                        ffn_chunk(l, 1, it, j, True)
                copy_gate(l * 3 + 2, 0.5)
                ffn_chunk(l, 1, PAIRS, 0, False)
                evac_uT(0, l * 24 + 24, l * 3 + 4, l * 2 + 2)

        @block.gpsimd
        def _(g):
            for s in range(2):
                g.memset(ada_ring[s][:, 8, :], 0.0).then_inc(sem("pad_zeroed"), 1)
            g.memset(ident[:, :], 0.0).then_inc(sem("const_step"), 1)
            g.memset(ones[:, :], 1.0).then_inc(sem("const_step"), 1)
            g.memset(neg_half[:, :], -0.5).then_inc(sem("const_step"), 1)
            g.memset(zeros_bf[:, :], 0.0).then_inc(sem("const_step"), 1)
            g.memset(mask_c[:, :], 0.0).then_inc(sem("const_step"), 1)
            bm = work[0][:, 0, 0:P].rearrange("p (q two c) -> p q two c", two=2, c=16)
            g.memset(work[0][:, 0, 0:P], 0.0).then_inc(sem("const_step"), 1)
            g.wait_ge(sem("const_step"), 6)
            g.memset(bm[0:64, :, 0, :], 1.0).then_inc(sem("const_step"), 1)
            g.memset(bm[64:128, :, 1, :], 1.0).then_inc(sem("const_step"), 1)
            g.wait_ge(sem("const_step"), 8)
            g.affine_select(out=ident[:, :], in_=ident[:, :], compare_op=ALU.not_equal, fill=1.0, base=0,
                            pattern=[[-1, P]], channel_multiplier=1).then_inc(sem("const_step"), 1)
            g.affine_select(out=mask_c[:, :], in_=mask_c[:, :], compare_op=ALU.is_ge, fill=NEG, base=0,
                            pattern=[[1, T]], channel_multiplier=-1).then_inc(sem("const_step"), 1)
            g.iota(dist[:, 0:P], pattern=[[1, P]], base=0, channel_multiplier=-1,
                   allow_small_or_imprecise_dtypes=True).then_inc(sem("const_step"), 1)
            g.iota(dist[:, P:384], pattern=[[1, T]], base=-P, channel_multiplier=-1,
                   allow_small_or_imprecise_dtypes=True).then_inc(sem("const_step"), 1)
            for m in (mask_a, mask_b[:, :]):
                g.memset(m, 0.0).then_inc(sem("const_step"), 1)
            g.wait_ge(sem("const_step"), 14)
            for m in (mask_a, mask_b[:, :]):
                g.memset(m[0:64, 64:128], NEG).then_inc(sem("const_step"), 1)
                g.memset(m[0:64, P + 192:P + 256], NEG).then_inc(sem("const_step"), 1)
            g.memset(mask_a[64:128, P:P + 64], NEG).then_inc(sem("const_step"), 1)
            g.wait_ge(sem("const_step"), 19)
            g.sem_inc(sem("ln_bc_used"), 1)
            g.wait_ge(sem("x_loaded"), 32)
            g.sem_inc(sem("x_ready"), 2)

            def residual(l, s):
                n = l * 3 + s
                for tt in range(2):
                    g.wait_ge(sem("var_ready"), n * 2 + (tt + 1))
                    g.tensor_tensor(rstd[:, tt:tt + 1], var_eps[:, tt:tt + 1], neg_half[:, 0:1], ALU.pow
                                    ).then_inc(sem("rstd_ready"), 1)
                g.wait_ge(sem("ln_bc_loaded"), (n + 1) * 32)
                for tt in range(2):
                    g.wait_ge(sem("xn_ready"), n * 2 + (tt + 1))
                    g.tensor_tensor(x_sb[:, tt, :], xn[:, tt, :], ln_bc[:, 0, :], ALU.mult).then_inc(sem("x_step"), 1)
                    g.wait_ge(sem("x_step"), n * 2 + (tt + 1))
                    g.tensor_tensor(x_sb[:, tt, :], x_sb[:, tt, :], ln_bc[:, 1, :], ALU.add).then_inc(sem("x_ready"), 1)
                g.wait_ge(sem("x_ready"), n * 2 + 4)
                g.sem_inc(sem("ln_bc_used"), 1)

            with g.Fori(0, DEPTH) as l:
                g.wait_ge(sem("rot_start"), l * 2 + 4)
                steps = [(m, 1, m) for m in (1, 2, 4, 8, 16, 32, 64)] + [(P, 1, 64), (P, 65, 63)]
                for k, (m, first, w) in enumerate(steps):
                    lo = slice(first, first + w)
                    hi = slice(m + first, m + first + w)
                    t4 = [rot_flat[:, 512 * q:512 * q + 8 * w].rearrange("p (i n) -> p i n", i=8) for q in range(4)]
                    cm = cos_t[:, :, m:m + 1].to_broadcast([P, 8, w])
                    sm = sin_t[:, :, m:m + 1].to_broadcast([P, 8, w])
                    if k:
                        g.wait_ge(sem("rot_step"), l * ROT_STEPS + 6 * k)
                    g.tensor_tensor(t4[0], cos_t[:, :, lo], cm, ALU.mult).then_inc(sem("rot_step"), 1)
                    g.tensor_tensor(t4[1], sin_t[:, :, lo], sm, ALU.mult).then_inc(sem("rot_step"), 1)
                    g.tensor_tensor(t4[2], sin_t[:, :, lo], cm, ALU.mult).then_inc(sem("rot_step"), 1)
                    g.tensor_tensor(t4[3], cos_t[:, :, lo], sm, ALU.mult).then_inc(sem("rot_step"), 1)
                    g.wait_ge(sem("rot_step"), l * ROT_STEPS + (6 * k + 4))
                    g.tensor_tensor(cos_t[:, :, hi], t4[0], t4[1], ALU.subtract).then_inc(sem("rot_step"), 1)
                    g.tensor_tensor(sin_t[:, :, hi], t4[2], t4[3], ALU.add).then_inc(sem("rot_step"), 1)
                residual(l, 0)
                for b in range(4):
                    tl = slice(2 * b, 2 * b + 2)
                    g.wait_ge(sem("bu_read"), l * 4 + (b + 1))
                    t_re, t_im = (tmp[2 * (b % 2) + q].rearrange("p (a b) -> p a b", a=2) for q in range(2))
                    g.tensor_tensor(st_re[:, tl, :], st_re[:, tl, :], t_re, ALU.add).then_inc(sem("rotated_in"), 1)
                    g.tensor_tensor(st_im[:, tl, :], st_im[:, tl, :], t_im, ALU.subtract).then_inc(sem("rotated_in"), 1)
                for b in range(4):
                    tl = slice(2 * b, 2 * b + 2)
                    g.wait_ge(sem("rotating_out"), l * 4 + (b + 1))
                    t4 = [tmp[q].rearrange("p (a b) -> p a b", a=2) for q in range(4)]
                    g.tensor_tensor(st_re[:, tl, :], t4[0], t4[1], ALU.subtract).then_inc(sem("rotated_out"), 1)
                    g.tensor_tensor(st_im[:, tl, :], t4[2], t4[3], ALU.add).then_inc(sem("rotated_out"), 1)
                g.tensor_scalar(gb_half[:, 0:2], prm[:, R_GB:R_GB + 2], 0.5, 0.0, ALU.mult, ALU.add).then_inc(sem("gb_half_ready"), 1)

                def normalise(p, ri, ready, signal):
                    g.wait_ge(sem(ready), l + 1)
                    for tt, c0, w in ((0, 0, P), (1, P, T)):
                        g.tensor_tensor(p[:, :, c0:c0 + w], p[:, :, c0:c0 + w],
                                        heads(ri)[:, tt, :].unsqueeze(2).to_broadcast([P, H, w]), ALU.mult
                                        ).then_inc(sem(signal), 1)

                normalise(work[0], ri_b, "rib_ready", "pb_ready")
                g.wait_ge(sem("z_read"), l * NZ + NZ)
                waited(g)
                g.tensor_scalar(sig_o[:, :, :], sig_o[:, :, :], 0.5, 0.5, ALU.mult, ALU.add).then_inc(sem("sig_ready"), 1)
                normalise(work[2], ri_a, "ria_ready", "pa_ready")
                g.wait_ge(sem("varc_ready"), l + 1)
                g.tensor_tensor(rstd_c, var_c, neg_half[:, :], ALU.pow).then_inc(sem("rstdc_ready"), 1)
                settle(g)
                g.wait_ge(sem("od_ready"), l + 1)
                for s in range(2):
                    g.memset(ada_ring[s][:, 8, :], 0.0).then_inc(sem("pad_zeroed"), 1)
                residual(l, 1)
                residual(l, 2)


_INS = ["x", "c", "ada_w", "ada_b", "ln_g", "ln_b", "ffn_w13", "ffn_w2", "w_in", "w_out", "sinks", "w_uq", "w_iq",
        "conv_w", "conv_b", "ig_b", "fg_b", "mh_norm_g", "lam_re", "lam_im", "log_step", "b_re", "b_im", "c_re",
        "c_im", "d_skip", "glu_w", "glu_b"]


def kernel(**inputs):
    import numpy as _np
    import concourse.bacc as _bacc
    from concourse import mybir as _mybir
    from concourse.bass_utils import run_bass_kernel_spmd as _run

    nc = _bacc.Bacc("TRN2", target_bir_lowering=False, num_devices=1)
    arrays, args = {}, []
    for name in _INS:
        a = _np.ascontiguousarray(inputs[name])
        arrays[f"in_{name}_dram"] = a
        args.append(nc.dram_tensor(f"in_{name}_dram", a.shape, _mybir.dt.from_np(a.dtype), kind="ExternalInput").ap())
    args.append(nc.dram_tensor("out_0_dram", (1, T, D), _mybir.dt.from_np(_np.dtype("float32")), kind="ExternalOutput").ap())
    trunk(nc, *args)
    r = _run(nc, [arrays], core_ids=[0])
    return r.results[0]["out_0_dram"]
```

```python
from contextlib import ExitStack

import concourse.bass as bass
from concourse import mybir

F32 = mybir.dt.float32
F32R = mybir.dt.float32r
BF16 = mybir.dt.bfloat16
ALU = mybir.AluOpType
ACT = mybir.ActivationFunctionType
AX = mybir.AxisListType.X

P = 128
D = 1024
KT = D // P
T = 256
DEPTH = 2
D_FF = 2816
CW = 256
CHUNKS = D_FF // CW
MIX_CHUNKS = 6
GPL = 2 * CHUNKS + MIX_CHUNKS
G_MIX = CHUNKS
G_FFN2 = CHUNKS + MIX_CHUNKS
HD = 64
H = 4
N_SUB = 3
ALPHA = (2 * DEPTH) ** 0.25
LN_EPS = 1e-5
NEG = -1e30
TAKEN = -3e38
TOPK = 64
IDX_SCALE = (32 * 4) ** -0.5
SLOPES = [2.0 ** -(i + 1) for i in range(8)]
SLOPES_A, SLOPES_B = SLOPES[0::2], SLOPES[1::2]
MAGIC = 1.5 * 2.0 ** 23
INV_2PI = 0.15915494309189535
TWO_PI_1, TWO_PI_2, TWO_PI_3 = 6.28125, 1.9350051879882812e-3, 3.0198289163009303e-07
PI_BELOW = 3.1415925
GELU_C, GELU_S = 0.044715, 0.7978845608028654

C_QA, C_KA, C_VA, C_CQ, C_KB, C_VB, C_KI, C_WI, C_QK, C_VC, C_IG, C_FG, C_OC, C_UD = (
    0, 256, 384, 512, 640, 704, 768, 800, 804, 1316, 1572, 1576, 1580, 1836)
MIX_PIECES = [
    [(0, C_UD, 256), (256, C_KI, 32), (288, C_KI, 32), (320, C_KI, 32), (352, C_KI, 32), (384, C_CQ, 128)],
    [(0, C_VB, 64), (64, C_VA, 128), (192, C_WI, 4), (196, C_KB, 64), (260, C_KB, 64), (324, C_IG, 4), (328, C_FG, 4)],
    [(0, C_QK, 512)],
    [(0, C_QA, 256), (256, C_KA, 64), (320, C_KA, 64), (384, C_KA + 64, 64), (448, C_KA + 64, 64)],
    [(0, C_VC, 256)],
    [(0, C_OC, 256)],
]
OUT_TILES = [[6, 7], [2, 3], [0], [1], [4], [5]]
LOADS = [2] * CHUNKS + [len(p) for p in MIX_PIECES] + [2] * CHUNKS
LOADS_PER_LAYER = [sum(LOADS[s::2]) for s in range(2)]
LOADS_BEFORE = [sum(LOADS[g % 2:g:2]) for g in range(GPL)]

R_LNG, R_LNB, R_CW, R_CB, R_MHG, R_DS, R_GB, R_LR, R_LI, ROWS = 0, 24, 48, 64, 68, 70, 72, 74, 82, 90
PARAM_DMAS = 24

AW = 512
ADA_FIRST = 6
ADA_BLOCKS = (10, 8)
ADA_PER_LAYER = sum(ADA_BLOCKS)
TRIPS = tuple((n - 2) // 2 for n in ADA_BLOCKS)
MODS = 3
TURN_ORDER = [0, 1, 4, 5, 2, 3, 6, 7]
ROT_STEPS = 54
NZ = 24


def trunk(nc, x, c, ada_w, ada_b, ln_g, ln_b, ffn_w13, ffn_w2, w_in, w_out, sinks, w_uq, w_iq,
          conv_w, conv_b, ig_b, fg_b, mh_norm_g, lam_re, lam_im, log_step, b_re, b_im, c_re, c_im,
          d_skip, glu_w, glu_b, out):
    ctx = ExitStack()
    with ctx:
        def sb(name, shape, dt=F32):
            offset[name] = (nc.sbuf_base + 31) // 32 * 32
            return ctx.enter_context(nc.sbuf_tensor(name, shape, dt))

        def over(name, of, shape, skip=0):
            return nc.alloc_sbuf_tensor_at(name, shape, F32R, offset=offset[of] + 4 * skip)

        sems, offset = {}, {}

        def sem(name):
            if name not in sems:
                sems[name] = ctx.enter_context(nc.semaphore(name))
            return sems[name]

        w_in_ring = [sb(f"w_in_ring{s}", [P, KT, 512]) for s in range(2)]
        w_out_ring = [sb(f"w_out_ring{s}", [P, 2, D]) for s in range(2)]
        arena = sb("arena", [P, 6144])
        ada_w_sb = arena[:, 0:9 * AW].rearrange("p (t n) -> p t n", n=AW)
        h_ring = arena[:, 4608:5632].rearrange("p (s n) -> p s n", n=T)
        silu_ring = arena[:, 5632:6144].rearrange("p (s n) -> p s n", n=T)
        st_re = arena[:, 0:2048].rearrange("p (i n) -> p i n", n=T)
        st_im = arena[:, 2048:4096].rearrange("p (i n) -> p i n", n=T)
        tmp = [arena[:, 4096 + 512 * k:4608 + 512 * k] for k in range(4)]

        x_sb = sb("x_sb", [P, 2, D])
        xn = sb("xn", [P, 2, D])
        uT = sb("uT", [P, KT, T])
        oT = uT
        gate_bc = sb("gate_bc", [P, D])
        ln_bc = sb("ln_bc", [P, 2, D])
        qk_raw = ln_bc[:, 0, :].rearrange("p (t n) -> p t n", n=T)
        rows = ln_bc[0:H, 1, :].rearrange("p (t n) -> p t n", n=T)
        acc = sb("acc", [P, AW])
        cos_t = sb("cos_t", [P, 8, T])
        sin_t = sb("sin_t", [P, 8, T])
        bias_a = sb("bias_a", [P, H, 384])
        dist = sb("dist", [P, 384])
        mask_b = sb("mask_b", [P, 384])
        mask_c = sb("mask_c", [P, T])
        ident = sb("ident", [P, P])
        ones = sb("ones", [P, P])
        block_mask = sb("block_mask", [P, P])
        zeros_bf = sb("zeros_bf", [1, 512], BF16)
        neg_half = sb("neg_half", [P, 8])
        c_sb = sb("c_sb", [P, 8])
        cs = sb("cs", [P, 8])
        mod = sb("mod", [P, 9 * 8])
        mod_a = sb("mod_a", [P, N_SUB, 8])
        mod_b = sb("mod_b", [P, N_SUB, 8])
        stats = sb("stats", [P, 2, 2, 6])
        mv = sb("mv", [P, 2, 2])
        var_eps = sb("var_eps", [P, 2])
        rstd = sb("rstd", [P, 2])
        nmr = sb("nmr", [P, 2])
        prow = sb("prow", [ROWS, P])
        prm = sb("prm", [P, ROWS])
        log_dt = sb("log_dt", [P, 8])
        b_raw = sb("b_raw", [P, 2, 8, 16])
        b_blk = sb("b_blk", [P, 2, 8, 32])
        c_blk = sb("c_blk", [P, 2, 2, P])
        bbT = sb("bbT", [P, 2, 2, P])
        cT = sb("cT", [P, 2, 2, P])
        glu_sb = sb("glu_sb", [P, 2, 256])
        uq_sb = sb("uq_sb", [P, 256])
        iq_sb = sb("iq_sb", [P, P])
        sinks_sb = sb("sinks_sb", [P, 2, H])
        gate_bias = sb("gate_bias", [H, 2])
        s5p = sb("s5p", [P, 24, 8])
        uT_lo = sb("uT_lo", [P, KT, T])
        udT, qbT = uT_lo[:, 0:2, :], uT_lo[:, 2:4, :]
        kiT, cqT, kbT, qiT = (uT_lo[:, 4 + k, :] for k in range(4))
        rot_flat = sb("rot_flat", [P, 8 * T])
        qaT, kaT, qkT = (rot_flat[:, a * T:b * T].rearrange("p (t n) -> p t n", n=T) for a, b in ((0, 2), (2, 4), (4, 8)))
        tokv = sb("tokv", [P, 2, 196])
        vaug = sb("vaug", [P, 2, H, 65])
        sig_o = sb("sig_o", [P, 2, T])
        work_flat = sb("work_flat", [P, 4 * H * 384])
        w_in_hi = [over(f"w_in_hi{ft}", "work_flat", [P, KT, 2, P], 2048 * ft) for ft in range(2)]
        w_out_hi = [over(f"w_out_hi{ft}", "work_flat", [P, D], 4096 + D * ft) for ft in range(2)]
        w_in_lo = [over(f"w_in_lo{s}", f"w_in_ring{s}", [P, KT, 512]) for s in range(2)]
        w_out_lo = [over(f"w_out_lo{s}", f"w_out_ring{s}", [P, 2, D]) for s in range(2)]
        h_parts = over("h_parts", "arena", [P, 4, T], 4608)
        u_hi, u_lo = over("u_hi", "uT", [P, KT, T]), over("u_lo", "uT_lo", [P, KT, T])
        work = [work_flat[:, k * 1536:(k + 1) * 1536].rearrange("p (h n) -> p h n", h=H) for k in range(4)]
        ada_w_2 = work_flat[:, 0:9 * AW].rearrange("p (t n) -> p t n", n=AW)
        mask_a = rot_flat[:, 0:384]
        acc_2 = rot_flat[:, 512:512 + AW]
        qk_tanh = work_flat[:, 1536:2560]
        hs, hn = (work_flat[:, 1536 + 512 * k:2048 + 512 * k].rearrange("p (t h e) -> p t h e", t=2, h=H) for k in range(2))
        sc = sb("sc", [P, 384])
        m8 = sb("m8", [P, 2, 8])
        small = sb("small", [P, 32, 8])
        diag = sig_o[:, :, :].rearrange("p t n -> p (t n)")
        PS = ctx.enter_context(nc.psum_tensor("PS", [P, 8, 512], F32))

        S5 = {n: s5p[:, k, :] for k, n in enumerate(
            ["dt", "th", "lrdt", "rho", "n", "r", "sin", "sinh", "sh2", "cos", "a_re", "a_im", "am1", "t1", "t2",
             "den", "rden", "k1", "k2", "k_re", "k3", "k4", "k_im", "r0"])}
        mx_b, nmx_b, rs_b, ri_b, mx_a, nmx_a, rs_a, ri_a, es_a, ds_a, rcol, nmcol, enm, den, dmx, rden_c, \
            s1, mu, s2, var_c, rstd_c, gb_half, t8 = (small[:, k, :] for k in range(23))

        def heads(ap):
            return ap.rearrange("p (t h) -> p t h", t=2)

        def col(r, k=0):
            return prm[:, r + k:r + k + 1]

        block = ctx.enter_context(nc.Block())

        def settle(eng):
            eng.wait_ge(sem("const_step"), 1)

        def waited(eng):
            eng.sem_inc(sem("waits_passed"), 1)

        def w_in_tile(ring, slot, ft):
            return ring[slot][:, :, :].rearrange("p k (h f c) -> p k h f c", h=2, f=2)[:, :, :, ft, :]

        def ff_tile(l, f, it, j):
            return l * 44 + it * 4 + (22 * f + 2 * j)

        def in_loads(l, f, it, j):
            g = (0, G_FFN2)[f] + j % 2
            return 16 * (l * LOADS_PER_LAYER[g % 2] + it * 2 + (LOADS_BEFORE[g] + 2 + 2 * (j // 2)))

        def ada_before(l, f, it, j):
            return l * ADA_PER_LAYER + it * 2 + (ADA_FIRST + (0, ADA_BLOCKS[0])[f] + j)

        def ring_use(l, g, it=0):
            return l * (GPL // 2) + (g // 2 + it)

        @block.sync
        def _(sp):
            sp.dma_start(c_sb[:, :], c.rearrange("o (p t) -> p (o t)", t=8)).then_inc(sem("c_loaded"), 16)
            sp.wait_ge(sem("pad_zeroed"), 2)

            def load_ada(dst, layer, column, done, loaded):
                if done is not None:
                    sp.wait_ge(sem("acc_step"), done * 8)
                    waited(sp)
                sp.dma_start(dst[:, 0:8, :], ada_w[layer, :, column].rearrange("o (p t) n -> p (o t) n", t=8)
                             ).then_inc(sem(loaded), 16)
                sp.dma_start(dst[0:1, 8, :], ada_b[layer, column]).then_inc(sem(loaded), 16)

            for n in range(ADA_FIRST):
                load_ada((ada_w_sb, ada_w_2)[n % 2], slice(0, 1), slice(n * AW, (n + 1) * AW),
                         None if n < 2 else n - 1, f"ada_loaded{n % 2}")
                if n == 1:
                    for tt in range(2):
                        sp.dma_start(x_sb[:, tt, :], x[0, tt * P:(tt + 1) * P, :]).then_inc(sem("x_loaded"), 16)

            def load_ffn_in(l, f, slot, column, use):
                sp.wait_ge(sem(f"w_in_used{slot}"), use + 1)
                waited(sp)
                for half, off in ((0, 0), (1, D_FF)):
                    cols = bass.ds(column + off, CW)
                    sp.dma_start(w_in_ring[slot][:, :, half * CW:(half + 1) * CW],
                                 ffn_w13[bass.ds(l, 1), f, :, cols].rearrange("o (t p) n -> p (o t) n", p=P)
                                 ).then_inc(sem(f"w_in_loaded{slot}"), 16)

            def load_ffn_out(l, f, slot, column, use):
                sp.wait_ge(sem(f"w_out_used{slot}"), use + 1)
                waited(sp)
                sp.dma_start(w_out_ring[slot][:, :, :],
                             ffn_w2[bass.ds(l, 1), f, bass.ds(column, CW), :].rearrange("o (t p) n -> p (o t) n", p=P)
                             ).then_inc(sem(f"w_out_loaded{slot}"), 16)

            def load_ln(l, s):
                for k, src in enumerate((ln_g, ln_b)):
                    sp.dma_start(ln_bc[:, k, :], src[bass.ds(l, 1), s, :].to_broadcast([P, D])
                                 ).then_inc(sem("ln_bc_loaded"), 16)

            with sp.Fori(0, DEPTH) as l:
                L = bass.ds(l, 1)
                load_ffn_in(l, 0, 0, 0, ring_use(l, 0))
                load_ffn_out(l, 0, 0, 0, ring_use(l, 0))
                sp.wait_ge(sem("mixer_params_used"), l + 1)
                waited(sp)
                pl = sem("params_loaded")
                for r, src in ((R_LNG, ln_g), (R_LNB, ln_b)):
                    sp.dma_start(prow[r:r + 24, :], src[L].rearrange("o s (j p) -> (o s j) p", p=P)).then_inc(pl, 16)
                sp.dma_start(prow[R_CW:R_CW + 16, :], conv_w[L].rearrange("o s (j p) -> (o s j) p", p=P)).then_inc(pl, 16)
                for r, n, src in ((R_CB, 4, conv_b), (R_MHG, 2, mh_norm_g), (R_DS, 2, d_skip), (R_GB, 2, glu_b)):
                    sp.dma_start(prow[r:r + n, :], src[L].rearrange("o (j p) -> (o j) p", p=P)).then_inc(pl, 16)
                for r, src in ((R_LR, lam_re), (R_LI, lam_im)):
                    sp.dma_start(prow[r:r + 8, :], src[L].rearrange("o (i two) p -> (o i) (two p)", two=2)).then_inc(pl, 16)
                for half in range(2):
                    sp.dma_start(log_dt[64 * half:64 * half + 64, :],
                                 log_step[L].rearrange("o (i two) -> two (o i)", two=2)[half:half + 1].to_broadcast([64, 8]),
                                 allow_slow_non_contiguous=True).then_inc(pl, 16)
                for k, src in enumerate((b_re, b_im)):
                    sp.dma_start(b_raw[:, k, :, :], src[L].rearrange("o (i two) p c -> (two p) (o i) c", two=2)).then_inc(pl, 16)
                for k, src in enumerate((c_re, c_im)):
                    for rep in range(2):
                        sp.dma_start(c_blk[:, k, :, rep * 64:(rep + 1) * 64],
                                     src[L].rearrange("o (t g) c p -> (g c) (o t) p", t=2)).then_inc(pl, 16)
                sp.dma_start(glu_sb[:, :, :], glu_w[L].rearrange("o (t p) n -> p (o t) n", p=P)).then_inc(pl, 16)
                sp.dma_start(uq_sb[:, :], w_uq[bass.ds(l, 1)].rearrange("o p n -> p (o n)")).then_inc(pl, 16)
                sp.dma_start(iq_sb[:, :], w_iq[bass.ds(l, 1)].rearrange("o p n -> p (o n)")).then_inc(pl, 16)
                for k in range(2):
                    sp.dma_start(sinks_sb[:, k, :], sinks[L].to_broadcast([P, H])).then_inc(pl, 16)
                for k, src in enumerate((ig_b, fg_b)):
                    sp.dma_start(gate_bias[:, k:k + 1], src[L].rearrange("o h -> h o")).then_inc(pl, 16)
                def load_beside(f, it, j, ada):
                    g = (0, G_FFN2)[f] + j + 1
                    load_ffn_in(l, f, g % 2, it * 2 * CW + (j + 1) * CW, ring_use(l, g, it))
                    load_ffn_out(l, f, g % 2, it * 2 * CW + (j + 1) * CW, ring_use(l, g, it))
                    if ada is not None:
                        load_ada(ada_w_sb, ada[0], bass.ds(ada[1], AW), ada_before(l, f, it, j), "ada_loaded0")

                for j in range(2):
                    load_beside(0, 0, j, (L, 3 * D + j * AW))
                with sp.Fori(0, TRIPS[0]) as it:
                    for j in range(2):
                        load_beside(0, it + 1, j, (L, it * 2 * AW + (3 * D + (2 + j) * AW)))
                sp.wait_ge(sem("ln_bc_used"), l * 3 + 1)
                waited(sp)
                load_ln(l, 0)
                def load_mix_in(m):
                    g = G_MIX + m
                    slot = g % 2
                    sp.wait_ge(sem(f"w_in_used{slot}"), ring_use(l, g) + 1)
                    waited(sp)
                    for dst, src, w in MIX_PIECES[m]:
                        sp.dma_start(w_in_ring[slot][:, :, dst:dst + w],
                                     w_in[L, :, src:src + w].rearrange("o (t p) n -> p (o t) n", p=P)
                                     ).then_inc(sem(f"w_in_loaded{slot}"), 16)

                def load_mix_out(m):
                    g = G_MIX + m
                    slot = g % 2
                    sp.wait_ge(sem(f"w_out_used{slot}"), ring_use(l, g if m < 4 else g - 2) + 1)
                    waited(sp)
                    t0, tn = OUT_TILES[m][0], len(OUT_TILES[m])
                    at = 1 if m >= 4 else 0
                    sp.dma_start(w_out_ring[slot][:, at:at + tn, :],
                                 w_out[L, t0 * P:(t0 + tn) * P, :].rearrange("o (t p) n -> p (o t) n", p=P)
                                 ).then_inc(sem(f"w_out_loaded{slot}"), 16)

                for m in range(2):
                    load_mix_in(m)
                for m in range(2):
                    load_mix_out(m)
                for m in range(2, MIX_CHUNKS):
                    load_mix_in(m)
                slot2 = G_FFN2 % 2
                load_ffn_in(l, 1, slot2, 0, ring_use(l, G_FFN2))
                for m in (2, 4, 3, 5):
                    load_mix_out(m)
                sp.wait_ge(sem("cols_turned"), l + 1)
                waited(sp)
                sp.wait_ge(sem("g_spread"), l + 1)
                waited(sp)
                sp.wait_ge(sem("conv_step"), l * 16 + 16)
                waited(sp)
                load_ln(l, 1)
                load_ffn_out(l, 1, slot2, 0, ring_use(l, G_FFN2))
                sp.wait_ge(sem("pad_zeroed"), l + 3)
                waited(sp)
                for j in range(2):
                    load_beside(1, 0, j, (L, 8 * D + j * AW))
                with sp.Fori(0, TRIPS[1]) as it:
                    for j in range(2):
                        load_beside(1, it + 1, j, (slice(DEPTH - 1, DEPTH), it * 2 * AW + j * AW))
                for k in range(2 * TRIPS[1] + 2, CHUNKS - 1):
                    load_beside(1, k // 2, k % 2, None)
                sp.wait_ge(sem("ln_bc_used"), l * 3 + 3)
                waited(sp)
                load_ln(l, 2)
            for tt in range(2):
                sp.wait_ge(sem("x_ready"), 2 * N_SUB * DEPTH + 1 + tt)
                sp.dma_start(out[0, tt * P:(tt + 1) * P, :], x_sb[:, tt, :]).then_inc(sem("out_stored"), 16)
            sp.wait_ge(sem("out_stored"), 32)

        @block.tensor
        def _(pe):
            for s in range(2):
                pe.sem_inc(sem(f"w_in_used{s}"), 1)
                pe.sem_inc(sem(f"w_out_used{s}"), 1)
            pe.sem_inc(sem("mixer_params_used"), 1)
            pe.sem_inc(sem("ag_ready"), 2)
            pe.wait_ge(sem("const_step"), 10)

            pe.transpose(PS[:, 4, 0:P], rot_flat[:, 384:512], ident[:, :]).then_inc(sem("mask_turned"), 1)

            def turn(src, l, s):
                for tt in range(2):
                    if s is not None:
                        pe.wait_ge(sem("xn_act"), l * 6 + (2 * s + tt + 1))
                        if tt == 1:
                            pe.wait_ge(sem("xn_dve"), l * 3 + (s + 1))
                    for j in TURN_ORDER:
                        mm = pe.transpose(PS[:, 4 + j // 2, (j % 2) * T + tt * P:(j % 2) * T + (tt + 1) * P],
                                          src[:, tt, j * P:(j + 1) * P], ident[:, :])
                        if tt == 1:
                            mm.then_inc(sem("x_turned"), 1)

            def spread_gate(n, hf):
                pe.wait_ge(sem("diag_ready"), n * 2 + (hf + 1))
                if hf == 1:
                    pe.wait_ge(sem("gate_ready"), n * 2 + hf)
                pe.matmul(PS[:, 7, :], ones[:, :], diag, start=True, stop=True).then_inc(sem("gate_spread"), 1)

            def seed_y():
                for b in range(4):
                    pe.matmul(PS[:, b, :], zeros_bf[0:1, 0:P], zeros_bf[0:1, :], start=True, stop=False)

            def ada_sum(n, base, mods, acc=acc):
                pe.wait_ge(sem("acc_step"), n * 8 + 8)
                if mods is not None:
                    pe.wait_ge(sem("mod_ready"), mods)
                for a in range(AW // P):
                    mm = pe.matmul(PS[:, 6, bass.ds(base + a, 1)], acc[:, a * P:(a + 1) * P], ones[:, 0:1], start=True, stop=True)
                mm.then_inc(sem("ada_summed"), 1)

            def ffn_chunk(l, f, it, j):
                slot = ((0, G_FFN2)[f] + j) % 2
                tile = ff_tile(l, f, it, j)
                first, c = isinstance(it, int) and it == 0 and j == 0, it * 2 + j if isinstance(it, int) else None
                last = c == CHUNKS - 1
                for ft in range(2):
                    pe.wait_ge(sem("w_in_split"), tile + (ft + 1))
                    pe.wait_ge(sem("h_done"), tile + (ft + 1))
                    lo = w_in_tile(w_in_lo, slot, ft)
                    for half in range(2):
                        for i, kt in enumerate(TURN_ORDER):
                            if first and ft == 0 and half == 0 and i % 2 == 0:
                                pe.wait_ge(sem("uT_split"), l * 8 + (4 * f + i // 2 + 1))
                            hi = w_in_hi[ft][:, kt, half, :]
                            y = PS[:, 4 + ft, half * T:(half + 1) * T]
                            pe.matmul(y, hi, u_hi[:, kt, :], start=(i == 0), stop=False)
                            pe.matmul(y, hi, u_lo[:, kt, :], start=False, stop=False)
                            mm = pe.matmul(y, lo[:, kt, half, :], u_hi[:, kt, :], start=False, stop=(i == KT - 1))
                    mm.then_inc(sem("ag_ready"), 1)
                if not first and (c is None or c - 1 < ADA_BLOCKS[f]):
                    ada_sum(ada_before(l, f, it, j - 1), it * 8 + (4 * j - 4), l * MODS + (1 + f))
                for k, (tt, ft) in enumerate(((0, 0), (0, 1), (1, 0), (1, 1)) if last else ((0, 0), (1, 0), (0, 1), (1, 1))):
                    if tt == 0:
                        pe.wait_ge(sem("w_out_split"), tile + (ft + 1))
                        pe.wait_ge(sem("h_done"), tile + (ft + 3))
                    for hf in range(2):
                        tok, cols = slice(tt * P, (tt + 1) * P), slice(hf * 512, (hf + 1) * 512)
                        h_hi, h_lo = h_parts[:, 2 + ft, tok], h_parts[:, ft, tok]
                        y = PS[:, 2 * tt + hf, :]
                        mm = pe.matmul(y, h_hi, w_out_hi[ft][:, cols], start=False, stop=False)
                        if k == 0 and hf == 0:
                            mm.then_inc(sem(f"w_in_used{slot}"), 1)
                        pe.matmul(y, h_hi, w_out_lo[slot][:, ft, cols], start=False, stop=False)
                        mm = pe.matmul(y, h_lo, w_out_hi[ft][:, cols], start=False, stop=(last and ft == 1))
                        if last and ft == 1:
                            mm.then_inc(sem("y_ready"), 1)
                        elif k == 3 and hf == 1:
                            mm.then_inc(sem(f"w_out_used{slot}"), 1)

            def release_out(slot):
                pe.drain().then_inc(sem(f"w_out_used{slot}"), 1)

            for n in range(ADA_FIRST):
                ada_sum(n, 4 * n, None, (acc, acc_2)[n % 2])
            pe.wait_ge(sem("x_loaded"), 32)
            pe.wait_ge(sem("block_mask_ready"), 1)
            pe.wait_ge(sem("mod_ready"), 1)
            turn(x_sb, 0, None)

            with pe.Fori(0, DEPTH) as l:
                pe.wait_ge(sem("y_read"), l * 12 + 4)
                seed_y()
                ffn_chunk(l, 0, 0, 0)
                pe.wait_ge(sem("params_loaded"), (l + 1) * (16 * PARAM_DMAS))
                pe.transpose(PS[:, 7, 0:ROWS], prow[:, :], ident[0:ROWS, 0:ROWS]).then_inc(sem("prm_turned"), 1)
                ffn_chunk(l, 0, 0, 1)
                pe.wait_ge(sem("prm_ready"), l + 1)
                spread_gate(l * 3, 0)
                with pe.Fori(0, TRIPS[0]) as it:
                    for j in range(2):
                        ffn_chunk(l, 0, it + 1, j)
                spread_gate(l * 3, 1)
                ffn_chunk(l, 0, 5, 0)
                release_out(0)
                pe.wait_ge(sem("b_blk_ready"), l * 4 + 4)
                pe.wait_ge(sem("gate_ready"), l * 6 + 2)
                for k in range(2):
                    for t in range(2):
                        mm = pe.transpose(PS[:, 7, (2 * k + t) * P:(2 * k + t + 1) * P],
                                          b_blk[:, k, 4 * t:4 * t + 4, :].rearrange("p a b -> p (a b)"), ident[:, :])
                mm.then_inc(sem("bb_turned"), 1)
                pe.wait_ge(sem("c_blk_ready"), l * 2 + 2)
                pe.wait_ge(sem("bbT_ready"), l + 1)
                for k in range(2):
                    for t in range(2):
                        mm = pe.transpose(PS[:, 7, (2 * k + t) * P:(2 * k + t + 1) * P], c_blk[:, k, t, :], ident[:, :])
                mm.then_inc(sem("c_turned"), 1)
                pe.wait_ge(sem("mod_ready"), l * MODS + 2)
                pe.wait_ge(sem("h_done"), l * 44 + 24)
                pe.wait_ge(sem("cT_ready"), l + 1)
                turn(xn, l, 0)

                pe.wait_ge(sem("uT_act"), l * 12 + 8)
                pe.wait_ge(sem("uT_dve"), l * 12 + 8)
                pe.wait_ge(sem("y_read"), l * 12 + 8)
                def z_out(n):
                    if n == 3:
                        pe.wait_ge(sem("gate_ready"), l * 6 + 4)
                    if n >= 4:
                        pe.wait_ge(sem("z_read"), l * NZ + (n - 3))
                    return PS[:, 4 + n % 4, 0:T]

                def z_feature(n, slot, c0, m=P):
                    o = z_out(n)
                    for kt in range(KT):
                        mm = pe.matmul(o[0:m, :], w_in_ring[slot][:, kt, c0:c0 + m], uT[:, kt, :],
                                       start=(kt == 0), stop=(kt == KT - 1))
                    mm.then_inc(sem("z_ready"), 1)

                def z_token(n, slot, c0, w, tt):
                    o = z_out(n)
                    for kt in range(KT):
                        mm = pe.matmul(o[:, 0:w], uT[:, kt, tt * P:(tt + 1) * P], w_in_ring[slot][:, kt, c0:c0 + w],
                                       start=(kt == 0), stop=(kt == KT - 1))
                    mm.then_inc(sem("z_ready"), 1)

                def chunk_in(m):
                    g = G_MIX + m
                    pe.wait_ge(sem(f"w_in_loaded{g % 2}"), 16 * (l * LOADS_PER_LAYER[g % 2] + LOADS_BEFORE[g] + LOADS[g]))

                def chunk_done(m):
                    pe.drain().then_inc(sem(f"w_in_used{(G_MIX + m) % 2}"), 1)

                def s5_inputs(b):
                    if b >= 2:
                        pe.wait_ge(sem("bu_read"), l * 4 + (b - 1))
                    for k in range(2):
                        i = 2 * b + k
                        q, t = i % 4, i // 4
                        for ri in range(2):
                            mm = pe.matmul(PS[:, 2 * (b % 2) + k, ri * T:(ri + 1) * T],
                                           bbT[32 * q:32 * q + 32, ri, t, :], udT[32 * q:32 * q + 32, t, :],
                                           start=True, stop=True)
                    mm.then_inc(sem("bu_ready"), 1)

                def scores(q_of, k_of, rows_of, signal):
                    for h in range(H):
                        r = rows_of(h)
                        for tt, w in ((0, P), (1, T)):
                            mm = pe.matmul(PS[:, h, (0, P)[tt]:(0, P)[tt] + w], q_of(h)[r, tt * P:(tt + 1) * P],
                                           k_of(h)[r, 0:w], start=True, stop=True)
                    mm.then_inc(sem(signal), 1)

                def half(h):
                    return slice(64 * (h % 2), 64 * (h % 2) + 64)

                chunk_in(0)
                s0, s1_ = G_MIX % 2, (G_MIX + 1) % 2
                z_feature(0, s0, 0)
                z_feature(1, s0, 128)
                spread_gate(l * 3 + 1, 0)
                pe.wait_ge(sem("z_read"), l * NZ + 2)
                s5_inputs(0)
                s5_inputs(1)
                spread_gate(l * 3 + 1, 1)
                z_feature(2, s0, 256)
                z_feature(3, s0, 384)
                chunk_done(0)
                chunk_in(1)
                for tt in range(2):
                    z_token(4 + tt, s1_, 0, 196, tt)
                z_feature(6, s1_, 196)
                z_feature(7, s1_, 324, H)
                z_feature(8, s1_, 328, H)
                chunk_done(1)
                s5_inputs(2)
                for n, w in ((9, iq_sb[:, :]), (10, uq_sb[:, 0:P]), (11, uq_sb[:, P:2 * P])):
                    pe.matmul(z_out(n), w, cqT[:, :], start=True, stop=True).then_inc(sem("z_ready"), 1)
                s5_inputs(3)
                chunk_in(2)
                for t in range(2):
                    z_feature(12 + t, s0, t * P)
                pe.wait_ge(sem("z_read"), l * NZ + 12)
                pe.wait_ge(sem("bu_read"), l * 4 + 4)
                scores(lambda h: qiT, lambda h: kiT, lambda h: slice(32 * h, 32 * h + 32), "idx_ready")
                for t in range(2, 4):
                    z_feature(12 + t, s0, t * P)
                chunk_done(2)
                pe.wait_ge(sem("idx_read"), l + 1)
                scores(lambda h: qbT[:, h // 2, :], lambda h: kbT, half, "sb_ready")
                chunk_in(3)
                for t in range(4):
                    z_feature(16 + t, s1_, t * P)
                chunk_done(3)
                chunk_in(4)
                for tt in range(2):
                    z_token(20 + tt, s0, 0, T, tt)
                chunk_done(4)
                pe.wait_ge(sem("sb_read"), l + 1)
                pe.wait_ge(sem("z_read"), l * NZ + 20)
                scores(lambda h: qaT[:, h // 2, :], lambda h: kaT[:, h // 2, :], half, "sa_ready")
                chunk_in(5)
                for t in range(2):
                    z_feature(22 + t, s1_, t * P)
                chunk_done(5)
                pe.wait_ge(sem("z_read"), l * NZ + NZ)

                def turn_probs(src, signal):
                    for b, c0 in enumerate((0, P, 2 * P)):
                        for h in range(H):
                            mm = pe.transpose(PS[:, 4 + b, h * P:(h + 1) * P], src[:, h, c0:c0 + P], ident[:, :])
                        mm.then_inc(sem(signal), 1)

                def mix_values(pt, v_of, bank):
                    for h in range(H):
                        o = PS[half(h), bank, (h // 2) * T:(h // 2 + 1) * T]
                        ptv = pt[:, :, :].rearrange("p h n -> p (h n)")
                        mm = pe.matmul(o[:, 0:P], v_of(0, h), ptv[:, h * P:(h + 1) * P], start=True, stop=True)
                        for kt in range(2):
                            mm = pe.matmul(o[:, P:T], v_of(kt, h), ptv[:, 512 * (kt + 1) + h * P:512 * (kt + 1) + (h + 1) * P],
                                           start=(kt == 0), stop=(kt == 1))
                    return mm

                pe.wait_ge(sem("rotated_out"), l * 8 + 8)
                for i in range(8):
                    q, t = i % 4, i // 4
                    for ri, st in ((0, st_re), (1, st_im)):
                        mm = pe.matmul(PS[32 * q:32 * q + 32, 7, t * T:(t + 1) * T], cT[:, ri, t, 32 * q:32 * q + 32],
                                       st[:, i, :], start=(ri == 0), stop=(ri == 1))
                mm.then_inc(sem("yd_ready"), 1)
                pe.wait_ge(sem("pb_ready"), l * 2 + 2)
                turn_probs(work[0], "ptb_turned")
                pe.wait_ge(sem("ptb_ready"), l * 3 + 3)
                mix_values(work[1], lambda kt, h: tokv[:, kt, 0:64], 4).then_inc(sem("ob_ready"), 1)
                pe.wait_ge(sem("pa_ready"), l * 2 + 2)
                pe.wait_ge(sem("ob_read"), l + 1)
                turn_probs(work[2], "pta_turned")
                pe.wait_ge(sem("yg_ready"), l + 1)
                for t in range(2):
                    for kt in range(2):
                        mm = pe.matmul(PS[:, 7, t * T:(t + 1) * T], glu_sb[:, kt, t * P:(t + 1) * P],
                                       tmp[3][:, kt * T:(kt + 1) * T], start=(kt == 0), stop=(kt == 1))
                mm.then_inc(sem("glu_ready"), 1)
                pe.wait_ge(sem("pta_ready"), l * 3 + 3)
                mix_values(work[3], lambda kt, h: tokv[:, kt, 64 + 64 * (h // 2):128 + 64 * (h // 2)], 4
                           ).then_inc(sem("oa_ready"), 1)
                settle(pe)
                pe.wait_ge(sem("rows_ready"), l * 2 + 2)
                for k in range(2):
                    for tt in range(2):
                        mm = pe.transpose(PS[:, 6, (2 * k + tt) * 4:(2 * k + tt) * 4 + 4],
                                          rows[:, (2, 3)[k], tt * P:(tt + 1) * P], ident[0:H, 0:H])
                mm.then_inc(sem("cols_turned"), 1)
                pe.wait_ge(sem("oa_read"), l + 1)
                for h in range(H):
                    mm = pe.matmul(PS[:, 4 + h // 2, (h % 2) * T:(h % 2 + 1) * T], ident[0:H, h:h + 1].to_broadcast([H, P]),
                                   rows[:, 1, :], start=True, stop=True)
                mm.then_inc(sem("g_spread"), 1)

                def y_chunk(m):
                    g = G_MIX + m
                    pe.wait_ge(sem(f"w_out_loaded{g % 2}"), ring_use(l, g if m < 2 else g + 2) * 16 + 16)
                    for k, kt in enumerate(OUT_TILES[m]):
                        for b in range(4):
                            tt, hf = b // 2, b % 2
                            pe.matmul(PS[:, b, :], oT[:, kt, tt * P:(tt + 1) * P],
                                      w_out_ring[g % 2][:, k, hf * 512:(hf + 1) * 512], start=False, stop=False)
                    pe.drain().then_inc(sem(f"w_out_used{g % 2}"), 1)

                pe.wait_ge(sem("sa_read"), l + 1)
                seed_y()
                pe.wait_ge(sem("od_ready"), l + 1)
                y_chunk(0)
                pe.wait_ge(sem("w_args_ready"), l + 1)
                pe.wait_ge(sem("cols_ready"), l * 2 + 2)
                pe.wait_ge(sem("qk_ready"), l + 1)
                for h in range(H):
                    for s_t, w in ((0, T), (1, P)):
                        mm = pe.matmul(PS[:, 4 + h, (0, T)[s_t]:(0, T)[s_t] + w],
                                       qkT[half(h), 2 + h // 2, s_t * P:(s_t + 1) * P], qkT[half(h), h // 2, T - w:T],
                                       start=True, stop=True)
                mm.then_inc(sem("st_ready"), 1)
                y_chunk(1)
                pe.wait_ge(sem("pc_ready"), l + 1)
                for tt in range(2):
                    for h in range(H):
                        o = PS[:, 4 + tt, h * 65:(h + 1) * 65]
                        mm = pe.matmul(o, work[0][:, h, tt * P:(tt + 1) * P], vaug[:, 0, h, :], start=True, stop=(tt == 0))
                        if tt == 1:
                            mm = pe.matmul(o, work[0][:, h, T:T + P], vaug[:, 1, h, :], start=False, stop=True)
                mm.then_inc(sem("num_ready"), 1)
                y_chunk(2)
                y_chunk(3)
                pe.wait_ge(sem("hn_ready"), l + 1)
                for pr in range(2):
                    for tt in range(2):
                        mm = pe.transpose(PS[:, 6, pr * T + tt * P:pr * T + (tt + 1) * P],
                                          hn[:, tt, 2 * pr:2 * pr + 2, :].rearrange("p h e -> p (h e)"), ident[:, :])
                mm.then_inc(sem("hn_turned"), 1)
                pe.wait_ge(sem("oc_ready"), l * 2 + 2)
                for b in range(4):
                    tt, hf = b // 2, b % 2
                    for m in (4, 5):
                        mm = pe.matmul(PS[:, b, :], oT[:, OUT_TILES[m][0], tt * P:(tt + 1) * P],
                                       w_out_ring[(G_MIX + m) % 2][:, 1, hf * 512:(hf + 1) * 512], start=False, stop=(m == 5))
                    mm.then_inc(sem("y_ready"), 1)
                for m in (4, 5):
                    pe.drain().then_inc(sem(f"w_out_used{(G_MIX + m) % 2}"), 1)
                pe.drain().then_inc(sem("mixer_params_used"), 1)
                turn(xn, l, 1)

                pe.wait_ge(sem("y_read"), l * 12 + 12)
                seed_y()
                for j in range(2):
                    ffn_chunk(l, 1, 0, j)
                with pe.Fori(0, TRIPS[1]) as it:
                    for j in range(2):
                        ffn_chunk(l, 1, it + 1, j)
                ffn_chunk(l, 1, 4, 0)
                spread_gate(l * 3 + 2, 0)
                ffn_chunk(l, 1, 4, 1)
                spread_gate(l * 3 + 2, 1)
                ffn_chunk(l, 1, 5, 0)
                release_out(1)
                pe.wait_ge(sem("mod_ready"), l * MODS + 4)
                pe.wait_ge(sem("h_done"), l * 44 + 46)
                pe.wait_ge(sem("gate_ready"), l * 6 + 6)
                turn(xn, l, 2)

        @block.vector
        def _(v):
            v.sem_inc(sem("h_done"), 2)
            v.wait_ge(sem("const_step"), 19)
            v.scalar_tensor_tensor(dist[:, :], dist[:, :], -1.0, dist[:, :], ALU.mult, ALU.max).then_inc(sem("dist_ready"), 1)
            v.wait_ge(sem("dist_ready"), 1)
            for h in range(H):
                v.scalar_tensor_tensor(bias_a[:, h, :], dist[:, :], -SLOPES_A[h], mask_a, ALU.mult, ALU.add
                                       ).then_inc(sem("bias_a_ready"), 1)
            v.wait_ge(sem("mask_turned"), 1)
            v.tensor_copy(block_mask[:, :], PS[:, 4, 0:P]).then_inc(sem("block_mask_ready"), 1)
            v.memset(b_blk[:, :, :, :], 0.0)
            v.memset(cos_t[:, :, 0:1], 1.0).then_inc(sem("rot_start"), 1)
            v.memset(sin_t[:, :, 0:1], 0.0).then_inc(sem("rot_start"), 1)
            v.memset(vaug[:, :, :, 64:65], 1.0).then_inc(sem("vaug_ones"), 1)

            def ada_block(buf, loaded, sem_name, n, acc=acc, summed=0):
                v.wait_ge(sem(sem_name), loaded)
                if summed is not None:
                    v.wait_ge(sem("ada_summed"), n + summed)
                for t in range(8):
                    if t:
                        v.wait_ge(sem("acc_step"), n * 8 + t)
                    v.scalar_tensor_tensor(acc[:, :], buf[:, t, :], cs[:, t:t + 1], buf[:, 8, :] if t == 0 else acc[:, :],
                                           ALU.mult, ALU.add).then_inc(sem("acc_step"), 1)

            def mod_cols(dst, cols, summed):
                v.wait_ge(sem("ada_summed"), summed)
                v.tensor_copy(mod[:, dst], PS[:, 6, cols]).then_inc(sem("mod_ready"), 1)

            def mod_ab(s, lng, n, mods):
                v.wait_ge(sem("mod_ready"), mods)
                sh, scl = mod[:, 24 * s:24 * s + 8], mod[:, 24 * s + 8:24 * s + 16]
                if lng is None:
                    v.tensor_scalar(mod_a[:, s, :], scl, 1.0, None, ALU.add).then_inc(sem("mod_step"), 1)
                    v.tensor_copy(mod_b[:, s, :], sh).then_inc(sem("mod_step"), 1)
                    v.tensor_copy(t8, sh).then_inc(sem("mod_step"), 1)
                else:
                    g, b = prm[:, R_LNG + 8 * lng:R_LNG + 8 * lng + 8], prm[:, R_LNB + 8 * lng:R_LNB + 8 * lng + 8]
                    v.scalar_tensor_tensor(mod_a[:, s, :], scl, 1.0, g, ALU.add, ALU.mult).then_inc(sem("mod_step"), 1)
                    v.wait_ge(sem("mod_step"), n * 3)
                    v.scalar_tensor_tensor(t8, scl, 1.0, b, ALU.add, ALU.mult).then_inc(sem("mod_step"), 1)
                    v.wait_ge(sem("mod_step"), n * 3 + 2)
                    v.tensor_tensor(mod_b[:, s, :], t8, sh, ALU.add).then_inc(sem("mod_step"), 1)

            def u_low(k, split):
                two = slice(2 * k, 2 * k + 2)
                if k < 2:
                    v.wait_ge(sem("uT_high_act"), split * 2 + (k + 1))
                else:
                    v.wait_ge(sem("uT_high_dve"), split * 2 + (k - 1))
                v.tensor_tensor(u_lo[:, two, :], uT_lo[:, two, :], u_hi[:, two, :].bitcast(F32), ALU.subtract
                                ).then_inc(sem("uT_split"), 1)

            def evac_uT(s, turned, ab, split=None):
                dst = uT if split is None else uT_lo
                v.wait_ge(sem("mod_step"), ab * 3)
                for j in range(4, KT):
                    if j == 6 and split is not None:
                        v.wait_ge(sem("uT_dve"), turned // 2 + 2)
                        v.tensor_copy(u_hi[:, 4:6, :], uT_lo[:, 4:6, :]).then_inc(sem("uT_high_dve"), 1)
                        for k in (0, 2):
                            u_low(k, split)
                    if j % 2 == 0:
                        v.wait_ge(sem("x_turned"), turned + (TURN_ORDER.index(j + 1) + 1))
                    v.tensor_scalar(dst[:, j, :], PS[:, 4 + j // 2, (j % 2) * T:(j % 2 + 1) * T], mod_a[:, s, j:j + 1], mod_b[:, s, j:j + 1],
                                    ALU.mult, ALU.add).then_inc(sem("uT_dve"), 1)
                if split is None:
                    return
                v.wait_ge(sem("uT_dve"), turned // 2 + 4)
                v.tensor_copy(u_hi[:, 6:8, :], uT_lo[:, 6:8, :]).then_inc(sem("uT_high_dve"), 1)
                for k in (1, 3):
                    u_low(k, split)

            def gate_diag(s, n, mods, hf):
                v.wait_ge(sem("mod_ready"), mods)
                if hf:
                    v.wait_ge(sem("gate_spread"), n * 2 + 1)
                k = 24 * s + 16 + 4 * hf
                v.tensor_tensor(diag.rearrange("p (a b) -> p a b", a=4), ident[:, :].unsqueeze(1).to_broadcast([P, 4, P]),
                                mod[:, k:k + 4].unsqueeze(2).to_broadcast([P, 4, P]), ALU.mult
                                ).then_inc(sem("diag_ready"), 1)

            def ffn_tile(ft, tile):
                v.wait_ge(sem("silu_ready"), tile + (ft + 1))
                v.tensor_tensor(h_ring[:, ft, :], silu_ring[:, ft, :], PS[:, 4 + ft, T:2 * T], ALU.mult
                                ).then_inc(sem("h_step"), 1)
                v.wait_ge(sem("h_step"), tile * 2 + (2 * ft + 1))
                v.tensor_copy(h_parts[:, 2 + ft, :], h_ring[:, ft, :]).then_inc(sem("h_step"), 1)
                v.wait_ge(sem("h_step"), tile * 2 + (2 * ft + 2))
                v.tensor_tensor(h_parts[:, ft, :], h_ring[:, ft, :], h_parts[:, 2 + ft, :].bitcast(F32), ALU.subtract
                                ).then_inc(sem("h_done"), 1)

            def w_in_low(slot, ft, tile):
                v.wait_ge(sem("w_in_high"), tile + 1)
                v.tensor_tensor(w_in_tile(w_in_lo, slot, ft), w_in_tile(w_in_ring, slot, ft), w_in_hi[ft][:, :, :, :].bitcast(F32),
                                ALU.subtract).then_inc(sem("w_in_split"), 1)

            def w_out_low(slot, ft, tile):
                v.wait_ge(sem("w_out_high"), tile + 1)
                v.tensor_tensor(w_out_lo[slot][:, ft, :], w_out_ring[slot][:, ft, :], w_out_hi[ft][:, :].bitcast(F32), ALU.subtract
                                ).then_inc(sem("w_out_split"), 1)

            def ffn_chunk(l, f, it, j):
                c = it * 2 + j if isinstance(it, int) else None
                slot = ((0, G_FFN2)[f] + j) % 2
                tile = ff_tile(l, f, it, j)
                for ft in range(2):
                    w_out_low(slot, ft, tile + ft)
                for ft in range(2):
                    ffn_tile(ft, tile)
                    if c != CHUNKS - 1:
                        w_in_low(1 - slot, ft, tile + (2 + ft))
                if c is None or c < ADA_BLOCKS[f]:
                    n = ada_before(l, f, it, j)
                    ada_block(ada_w_sb, (l * ADA_PER_LAYER + it * 2 + (ADA_FIRST // 2 + (0, ADA_BLOCKS[0])[f] + j + 1)) * 32,
                              "ada_loaded0", n)

            def deepnorm(l, s):
                n = l * 3 + s
                v.wait_ge(sem("gate_ready"), n * 2 + 2)
                v.wait_ge(sem("x_ready"), n * 2 + 2)

                def neg_mean(tt):
                    v.wait_ge(sem("rstd_ready"), n * 2 + (tt + 1))
                    v.tensor_scalar(nmr[:, tt:tt + 1], mv[:, tt, 0:1], rstd[:, tt:tt + 1], -1.0, ALU.mult, ALU.mult
                                    ).then_inc(sem("nmr_ready"), 1)

                for tt in range(2):
                    for hf in range(2):
                        b = 2 * tt + hf
                        v.wait_ge(sem("y_ready"), n * 4 + (b + 1))
                        v.tensor_tensor(xn[:, tt, hf * 512:(hf + 1) * 512], PS[:, b, :], gate_bc[:, hf * 512:(hf + 1) * 512],
                                        ALU.mult).then_inc(sem("y_read"), 1)
                    if tt == 1:
                        neg_mean(0)
                    for hf in range(2):
                        b = 2 * tt + hf
                        v.wait_ge(sem("y_read"), n * 4 + (b + 5))
                        v.scalar_tensor_tensor(xn[:, tt, hf * 512:(hf + 1) * 512], x_sb[:, tt, hf * 512:(hf + 1) * 512], ALPHA,
                                               xn[:, tt, hf * 512:(hf + 1) * 512], ALU.mult, ALU.add
                                               ).then_inc(sem("r_ready"), 1)
                    for hf in range(2):
                        v.wait_ge(sem("r_ready"), n * 4 + (2 * tt + hf + 1))
                        v.bn_stats(stats[:, tt, hf, :], xn[:, tt, hf * 512:(hf + 1) * 512]).then_inc(sem("stats_ready"), 1)
                    settle(v)
                    v.wait_ge(sem("stats_ready"), n * 4 + (2 * tt + 2))
                    v.bn_aggr(mv[:, tt, :], stats[:, tt, :, :].rearrange("p a b -> p (a b)")).then_inc(sem("mv_ready"), 1)
                    v.wait_ge(sem("mv_ready"), n * 2 + (tt + 1))
                    v.tensor_scalar(var_eps[:, tt:tt + 1], mv[:, tt, 1:2], LN_EPS, None, ALU.add).then_inc(sem("var_ready"), 1)
                neg_mean(1)
                v.wait_ge(sem("nmr_ready"), n * 2 + 2)
                v.tensor_scalar(xn[:, 1, 0:512], xn[:, 1, 0:512], rstd[:, 1:2], nmr[:, 1:2], ALU.mult, ALU.add
                                ).then_inc(sem("xn_dve"), 1)

            v.sem_inc(sem("y_read"), 4)
            v.wait_ge(sem("cs_ready"), 1)
            for n in range(ADA_FIRST):
                ada_block((ada_w_sb, ada_w_2)[n % 2], 32 * (n // 2 + 1), f"ada_loaded{n % 2}", n,
                          (acc, acc_2)[n % 2], None if n < 2 else -1)
            mod_cols(slice(0, 24), slice(0, 24), ADA_FIRST)
            mod_ab(0, None, 0, 1)
            evac_uT(0, 0, 1, 0)
            for ft in range(2):
                w_in_low(0, ft, ft)

            with v.Fori(0, DEPTH) as l:
                gate_diag(0, l * 3, l * MODS + 1, 0)
                ffn_chunk(l, 0, 0, 0)
                v.wait_ge(sem("prm_turned"), l + 1)
                v.tensor_copy(prm[:, :], PS[:, 7, 0:ROWS]).then_inc(sem("prm_ready"), 1)
                ffn_chunk(l, 0, 0, 1)
                v.wait_ge(sem("prm_ready"), l + 1)
                step = [0]
                STEPS = 27

                def s5(ins):
                    ins.then_inc(sem("s5_step"), 1)
                    step[0] += 1
                    v.wait_ge(sem("s5_step"), l * STEPS + step[0])

                lr, li = prm[:, R_LR:R_LR + 8], prm[:, R_LI:R_LI + 8]
                v.wait_ge(sem("dt_ready"), l + 1)
                v.tensor_tensor(S5["lrdt"], lr, S5["dt"], ALU.mult).then_inc(sem("lrdt_ready"), 1)
                s5(v.tensor_tensor(S5["th"], li, S5["dt"], ALU.mult))
                s5(v.tensor_scalar(S5["n"], S5["th"], INV_2PI, MAGIC, ALU.mult, ALU.add))
                s5(v.tensor_scalar(S5["n"], S5["n"], MAGIC, None, ALU.subtract))
                s5(v.scalar_tensor_tensor(S5["r"], S5["n"], -TWO_PI_1, S5["th"], ALU.mult, ALU.add))
                s5(v.scalar_tensor_tensor(S5["r"], S5["n"], -TWO_PI_2, S5["r"], ALU.mult, ALU.add))
                s5(v.scalar_tensor_tensor(S5["r"], S5["n"], -TWO_PI_3, S5["r"], ALU.mult, ALU.add))
                v.tensor_scalar(S5["r0"], S5["r"], PI_BELOW, -PI_BELOW, ALU.min, ALU.max).then_inc(sem("angle_ready"), 1)
                v.wait_ge(sem("sin_ready"), l + 1)
                s5(v.tensor_tensor(S5["sh2"], S5["sinh"], S5["sinh"], ALU.mult))
                s5(v.tensor_scalar(S5["cos"], S5["sh2"], -2.0, 1.0, ALU.mult, ALU.add))
                v.tensor_copy(cos_t[:, :, 1:2], S5["cos"].unsqueeze(2)).then_inc(sem("rot_start"), 1)
                v.tensor_copy(sin_t[:, :, 1:2], S5["sin"].unsqueeze(2)).then_inc(sem("rot_start"), 1)
                s5(v.tensor_tensor(S5["a_re"], S5["rho"], S5["cos"], ALU.mult))
                s5(v.tensor_tensor(S5["a_im"], S5["rho"], S5["sin"], ALU.mult))
                s5(v.tensor_scalar(S5["am1"], S5["a_re"], 1.0, None, ALU.subtract))
                s5(v.tensor_tensor(S5["t1"], lr, lr, ALU.mult))
                s5(v.tensor_tensor(S5["t2"], li, li, ALU.mult))
                s5(v.tensor_tensor(S5["den"], S5["t1"], S5["t2"], ALU.add))
                s5(v.reciprocal(S5["rden"], S5["den"]))
                s5(v.tensor_tensor(S5["k1"], S5["am1"], lr, ALU.mult))
                s5(v.tensor_tensor(S5["k2"], S5["a_im"], li, ALU.mult))
                s5(v.tensor_tensor(S5["k1"], S5["k1"], S5["k2"], ALU.add))
                s5(v.tensor_tensor(S5["k_re"], S5["k1"], S5["rden"], ALU.mult))
                s5(v.tensor_tensor(S5["k3"], S5["a_im"], lr, ALU.mult))
                s5(v.tensor_tensor(S5["k4"], S5["am1"], li, ALU.mult))
                s5(v.tensor_tensor(S5["k3"], S5["k3"], S5["k4"], ALU.subtract))
                s5(v.tensor_tensor(S5["k_im"], S5["k3"], S5["rden"], ALU.mult))
                gate_diag(0, l * 3, l * MODS + 1, 1)
                with v.Fori(0, TRIPS[0]) as it:
                    for j in range(2):
                        ffn_chunk(l, 0, it + 1, j)
                tile = ff_tile(l, 0, 5, 0)
                for ft in range(2):
                    w_out_low(0, ft, tile + ft)
                ffn_tile(0, tile)
                kre = S5["k_re"].unsqueeze(2).to_broadcast([P, 8, 16])
                kim = S5["k_im"].unsqueeze(2).to_broadcast([P, 8, 16])
                bt = [diag[:, k * P:(k + 1) * P].rearrange("p (i c) -> p i c", c=16) for k in range(4)]
                v.wait_ge(sem("gate_spread"), l * 6 + 2)
                s5(v.tensor_tensor(bt[0], b_raw[:, 0, :, :], kre, ALU.mult))
                s5(v.tensor_tensor(bt[1], b_raw[:, 1, :, :], kim, ALU.mult))
                s5(v.tensor_tensor(bt[2], b_raw[:, 1, :, :], kre, ALU.mult))
                s5(v.tensor_tensor(bt[3], b_raw[:, 0, :, :], kim, ALU.mult))
                for two_ in range(2):
                    ph = slice(64 * two_, 64 * two_ + 64)
                    v.tensor_tensor(b_blk[ph, 0, :, 16 * two_:16 * two_ + 16], bt[0][ph], bt[1][ph], ALU.subtract
                                    ).then_inc(sem("b_blk_ready"), 1)
                    v.tensor_tensor(b_blk[ph, 1, :, 16 * two_:16 * two_ + 16], bt[2][ph], bt[3][ph], ALU.add
                                    ).then_inc(sem("b_blk_ready"), 1)
                for k, sign in ((0, 1.0), (1, -1.0)):
                    v.scalar_tensor_tensor(c_blk[:, k, :, :], c_blk[:, k, :, :], sign,
                                           block_mask[:, :].unsqueeze(1).to_broadcast([P, 2, P]), ALU.mult, ALU.mult
                                           ).then_inc(sem("c_blk_ready"), 1)
                assert step[0] == STEPS

                ffn_tile(1, tile)
                mod_cols(slice(24, 64), slice(0, 40), l * ADA_PER_LAYER + (ADA_FIRST + ADA_BLOCKS[0]))
                mod_ab(1, 0, l * 3 + 1, l * MODS + 2)
                mod_ab(2, 1, l * 3 + 2, l * MODS + 2)
                deepnorm(l, 0)
                evac_uT(1, l * 24 + 8, l * 3 + 2)

                v.wait_ge(sem("b_blk_ready"), l * 4 + 4)
                for hf in range(2):
                    gate_diag(1, l * 3 + 1, l * MODS + 2, hf)

                def tiles2(ap):
                    return ap.rearrange("p (a b) -> p a b", a=2)

                def s5_rotate_in(b):
                    v.wait_ge(sem("bu_ready"), l * 4 + (b + 1))
                    if b >= 2:
                        v.wait_ge(sem("rotated_in"), l * 8 + 2 * (b - 1))
                    tl = slice(2 * b, 2 * b + 2)
                    bk = 2 * (b % 2)
                    re, im = PS[:, bk:bk + 2, 0:T], PS[:, bk:bk + 2, T:2 * T]
                    v.tensor_tensor(st_re[:, tl, :], re, cos_t[:, tl, :], ALU.mult)
                    v.tensor_tensor(tiles2(tmp[2 * (b % 2)]), im, sin_t[:, tl, :], ALU.mult)
                    v.tensor_tensor(st_im[:, tl, :], im, cos_t[:, tl, :], ALU.mult)
                    v.tensor_tensor(tiles2(tmp[2 * (b % 2) + 1]), re, sin_t[:, tl, :], ALU.mult).then_inc(sem("bu_read"), 1)

                def s5_scan(b):
                    v.wait_ge(sem("rotated_in"), l * 8 + 2 * (b + 1))
                    for i in (2 * b, 2 * b + 1):
                        for st in (st_re, st_im):
                            ins = v.tensor_tensor_scan(st[:, i, :], S5["rho"][:, i:i + 1].to_broadcast([P, T]), st[:, i, :],
                                                       0.0, ALU.mult, ALU.add)
                    ins.then_inc(sem("scanned"), 1)

                def s5_rotate_out(b):
                    v.wait_ge(sem("scanned"), l * 4 + (b + 1))
                    v.wait_ge(sem("rotated_in"), l * 8 + 8)
                    if b:
                        v.wait_ge(sem("rotated_out"), l * 8 + 2 * b)
                    tl = slice(2 * b, 2 * b + 2)
                    v.tensor_tensor(tiles2(tmp[0]), st_re[:, tl, :], cos_t[:, tl, :], ALU.mult)
                    v.tensor_tensor(tiles2(tmp[1]), st_im[:, tl, :], sin_t[:, tl, :], ALU.mult)
                    v.tensor_tensor(tiles2(tmp[2]), st_re[:, tl, :], sin_t[:, tl, :], ALU.mult)
                    v.tensor_tensor(tiles2(tmp[3]), st_im[:, tl, :], cos_t[:, tl, :], ALU.mult).then_inc(sem("rotating_out"), 1)

                v.wait_ge(sem("rot_step"), (l + 1) * ROT_STEPS)
                s5_rotate_in(0)
                s5_rotate_in(1)
                s5_scan(0)
                s5_rotate_in(2)
                s5_scan(1)
                s5_rotate_in(3)
                s5_scan(2)
                v.wait_ge(sem("ln_f_ready"), l + 1)
                lf, bsum, gmx = (work[3][0:H, k, 0:T] for k in (1, 2, 3))
                v.scalar_tensor_tensor(lf, rows[:, 1, :], 0.0, lf, ALU.min, ALU.subtract).then_inc(sem("lf_ready"), 1)
                s5_scan(3)
                v.wait_ge(sem("lf_ready"), l + 1)
                v.tensor_tensor_scan(bsum, ones[0:H, 0:1].to_broadcast([H, T]), lf, 0.0, ALU.mult, ALU.add
                                     ).then_inc(sem("bsum_ready"), 1)
                v.wait_ge(sem("bsum_ready"), l + 1)
                v.tensor_tensor(rows[:, 2, :], rows[:, 0, :], bsum, ALU.subtract).then_inc(sem("r_row_ready"), 1)
                v.wait_ge(sem("r_row_ready"), l + 1)
                v.tensor_tensor_scan(gmx, ones[0:H, 0:1].to_broadcast([H, T]), rows[:, 2, :], 0.0, ALU.mult, ALU.max
                                     ).then_inc(sem("gmx_ready"), 1)
                v.wait_ge(sem("gmx_ready"), l + 1)
                v.tensor_scalar(rows[:, 1, :], gmx, -1.0, None, ALU.mult).then_inc(sem("rows_ready"), 1)
                v.scalar_tensor_tensor(rows[:, 3, :], bsum, -1.0, gmx, ALU.mult, ALU.subtract).then_inc(sem("rows_ready"), 1)

                v.wait_ge(sem("idx_read"), l + 1)
                for h in range(H):
                    if h:
                        v.wait_ge(sem("idx_sum"), l * 8 + 2 * h)
                    for tt, cols in ((0, slice(0, P)), (1, slice(P, 384))):
                        w = tokv[:, tt, 192 + h:193 + h]
                        src = work[0][:, h, cols]
                        if h == 0:
                            v.tensor_scalar(sc[:, cols], src, w, None, ALU.mult).then_inc(sem("idx_sum"), 1)
                        else:
                            v.scalar_tensor_tensor(sc[:, cols], src, w, sc[:, cols], ALU.mult, ALU.add
                                                   ).then_inc(sem("idx_sum"), 1)
                v.wait_ge(sem("idx_sum"), l * 8 + 8)
                v.scalar_tensor_tensor(sc[:, :], sc[:, :], IDX_SCALE, mask_b[:, :], ALU.mult, ALU.add
                                       ).then_inc(sem("idx_score"), 1)
                settle(v)
                v.wait_ge(sem("idx_score"), l + 1)
                for k in range(TOPK // 8):
                    for tt, cols in ((0, slice(0, P)), (1, slice(P, 384))):
                        if k:
                            settle(v)
                            v.wait_ge(sem("top_taken"), l * 16 + (2 * (k - 1) + tt + 1))
                        v.max(m8[:, tt, :], sc[:, cols]).then_inc(sem("top_found"), 1)
                    for tt, cols in ((0, slice(0, P)), (1, slice(P, 384))):
                        v.wait_ge(sem("top_found"), l * 16 + (2 * k + tt + 1))
                        waited(v)
                        v.match_replace(sc[:, cols], m8[:, tt, :], sc[:, cols], TAKEN).then_inc(sem("top_taken"), 1)
                    if k % 2:
                        s5_rotate_out(k // 2)
                v.wait_ge(sem("top_taken"), l * 16 + 16)
                v.tensor_scalar(sc[:, :], sc[:, :], TAKEN / 2, NEG, ALU.is_gt, ALU.mult).then_inc(sem("sel_step"), 1)
                v.wait_ge(sem("sel_step"), l * 2 + 1)
                v.tensor_tensor(sc[:, :], sc[:, :], mask_b[:, :], ALU.add).then_inc(sem("sel_step"), 1)
                v.wait_ge(sem("sel_step"), l * 2 + 2)
                for h in range(H):
                    v.scalar_tensor_tensor(work[1][:, h, :], dist[:, :], -SLOPES_B[h], sc[:, :], ALU.mult, ALU.add
                                           ).then_inc(sem("bias_b"), 1)

                def logits(bias, dst, ready, read, mx, nmx, name, sink):
                    v.wait_ge(sem(ready), l + 1)
                    v.scalar_tensor_tensor(dst[:, :, :], PS[:, 0:4, 0:384], HD ** -0.5, bias[:, :, :], ALU.mult, ALU.add
                                           ).then_inc(sem(read), 1)
                    v.wait_ge(sem(read), l + 1)
                    for tt, cols in ((0, slice(0, P)), (1, slice(P, 384))):
                        v.tensor_reduce(heads(mx)[:, tt, :], dst[:, :, cols], AX, ALU.max).then_inc(sem(name + "_max"), 1)
                    v.wait_ge(sem(name + "_max"), l * 2 + 2)
                    if sink is not None:
                        v.tensor_tensor(mx, mx, sink, ALU.max).then_inc(sem(name + "_smax"), 1)
                        v.wait_ge(sem(name + "_smax"), l + 1)
                    v.tensor_scalar(nmx, mx, -1.0, None, ALU.mult).then_inc(sem(name + "_nmax"), 1)

                v.wait_ge(sem("bias_b"), l * 4 + 4)
                logits(work[1], work[0], "sb_ready", "sb_read", mx_b, nmx_b, "b", None)

                v.wait_ge(sem("z_read"), l * NZ + 16)
                for j in range(3, -1, -1):
                    lag = 3 - j
                    for t in range(4):
                        w = col(R_CW, 4 * j + t)
                        if lag == 0:
                            v.tensor_scalar(qkT[:, t, :], qk_raw[:, t, :], w, col(R_CB, t), ALU.mult, ALU.add
                                            ).then_inc(sem("conv_step"), 1)
                        else:
                            v.wait_ge(sem("conv_step"), l * 16 + (4 * (lag - 1) + t + 1))
                            v.scalar_tensor_tensor(qkT[:, t, lag:T], qk_raw[:, t, 0:T - lag], w, qkT[:, t, lag:T],
                                                   ALU.mult, ALU.add).then_inc(sem("conv_step"), 1)

                v.wait_ge(sem("b_exp"), l * 8 + 8)
                v.reciprocal(ri_b, rs_b).then_inc(sem("rib_ready"), 1)

                sk = sinks_sb[:, :, :].rearrange("p t h -> p (t h)")
                v.wait_ge(sem("bias_a_ready"), 4)
                logits(bias_a, work[2], "sa_ready", "sa_read", mx_a, nmx_a, "a", sk)
                v.tensor_tensor(ds_a, sk, mx_a, ALU.subtract).then_inc(sem("sink_arg"), 1)

                v.wait_ge(sem("yd_ready"), l + 1)
                v.wait_ge(sem("rotated_out"), l * 8 + 8)
                for t in range(2):
                    v.scalar_tensor_tensor(tmp[0][:, t * T:(t + 1) * T], udT[:, t, :], col(R_DS, t), PS[:, 7, t * T:(t + 1) * T],
                                           ALU.mult, ALU.add).then_inc(sem("yd_read"), 1)
                v.wait_ge(sem("conv_tanh"), l + 1)
                v.scalar_tensor_tensor(qkT[:, :, :].rearrange("p a b -> p (a b)"), qk_tanh, 1.0,
                                       qkT[:, :, :].rearrange("p a b -> p (a b)"), ALU.add, ALU.mult).then_inc(sem("qk_ready"), 1)
                v.wait_ge(sem("qk_ready"), l + 1)
                ptb = work[1][:, :, :].rearrange("p h n -> p (h n)")
                for b in range(3):
                    v.wait_ge(sem("ptb_turned"), l * 3 + (b + 1))
                    v.tensor_copy(ptb[:, b * 512:(b + 1) * 512], PS[:, 4 + b, :]).then_inc(sem("ptb_ready"), 1)
                v.wait_ge(sem("gelu_sq"), l + 1)
                v.tensor_scalar(tmp[1], tmp[1], GELU_C, 1.0, ALU.mult, ALU.add).then_inc(sem("gelu_step"), 1)
                v.wait_ge(sem("gelu_step"), l * 2 + 1)
                v.tensor_tensor(tmp[1], tmp[1], tmp[0], ALU.mult).then_inc(sem("gelu_step"), 1)
                v.wait_ge(sem("a_exp"), l * 9 + 9)
                v.tensor_tensor(rs_a, rs_a, es_a, ALU.add).then_inc(sem("rsa_sum"), 1)
                v.wait_ge(sem("rsa_sum"), l + 1)
                v.reciprocal(ri_a, rs_a).then_inc(sem("ria_ready"), 1)
                v.wait_ge(sem("gelu_tanh"), l + 1)
                v.scalar_tensor_tensor(tmp[3], tmp[1], 1.0, tmp[0], ALU.add, ALU.mult).then_inc(sem("yg_ready"), 1)
                v.wait_ge(sem("glu_tanh"), l + 1)
                v.scalar_tensor_tensor(tmp[0], tmp[2], 1.0, tmp[3], ALU.add, ALU.mult).then_inc(sem("od_step"), 1)
                v.wait_ge(sem("od_step"), l + 1)
                v.tensor_scalar(oT[:, 6:8, :].rearrange("p a b -> p (a b)"), tmp[0], 0.25, None, ALU.mult
                                ).then_inc(sem("od_ready"), 1)

                v.wait_ge(sem("cols_turned"), l + 1)
                v.tensor_copy(rcol, PS[:, 6, 0:8]).then_inc(sem("cols_ready"), 1)
                v.tensor_copy(nmcol, PS[:, 6, 8:16]).then_inc(sem("cols_ready"), 1)
                v.wait_ge(sem("cols_ready"), l * 2 + 2)
                v.wait_ge(sem("g_spread"), l + 1)
                for h in range(H):
                    g = PS[:, 4 + h // 2, (h % 2) * T:(h % 2 + 1) * T]
                    v.scalar_tensor_tensor(work[0][:, h, 0:T], g, heads(rcol)[:, 0, h:h + 1], mask_c[:, :], ALU.add, ALU.add)
                    ins = v.scalar_tensor_tensor(work[0][:, h, T:384], g[:, P:T], heads(rcol)[:, 1, h:h + 1], mask_c[:, 0:P],
                                                 ALU.add, ALU.add)
                ins.then_inc(sem("w_args_ready"), 1)
                v.wait_ge(sem("st_ready"), l + 1)
                v.wait_ge(sem("w_exp"), l + 1)
                v.scalar_tensor_tensor(work[0][:, :, :], PS[:, 4:8, 0:384], HD ** -0.5 / 4, work[0][:, :, :], ALU.mult, ALU.mult
                                       ).then_inc(sem("pc_ready"), 1)
                v.wait_ge(sem("num_ready"), l + 1)
                num = PS[:, 4:6, 0:260].rearrange("p t (h e) -> p t h e", h=H)
                v.wait_ge(sem("den_ready"), l + 1)
                v.tensor_tensor(dmx, den, enm, ALU.max).then_inc(sem("den_step"), 1)
                v.wait_ge(sem("den_step"), l * 2 + 1)
                v.reciprocal(rden_c, dmx).then_inc(sem("den_step"), 1)
                v.wait_ge(sem("den_step"), l * 2 + 2)

                def over_e(ap):
                    return ap.unsqueeze(2).to_broadcast([P, 8, HD])

                for tt in range(2):
                    v.tensor_tensor(hs[:, tt, :, :], num[:, tt, :, 0:HD],
                                    heads(rden_c)[:, tt, :].unsqueeze(2).to_broadcast([P, H, HD]), ALU.mult
                                    ).then_inc(sem("hs_ready"), 1)
                hs8 = hs[:, :, :, :].rearrange("p t h e -> p (t h) e")
                hn8 = hn[:, :, :, :].rearrange("p t h e -> p (t h) e")
                v.wait_ge(sem("hs_ready"), l * 2 + 2)
                v.tensor_reduce(s1, hs8, AX, ALU.add).then_inc(sem("hn_step"), 1)
                v.wait_ge(sem("hn_step"), l * 5 + 1)
                v.tensor_scalar(mu, s1, 1.0 / HD, None, ALU.mult).then_inc(sem("hn_step"), 1)
                v.wait_ge(sem("hn_step"), l * 5 + 2)
                v.tensor_tensor(hs8, hs8, over_e(mu), ALU.subtract).then_inc(sem("hn_step"), 1)
                v.wait_ge(sem("hn_step"), l * 5 + 3)
                v.tensor_tensor(hn8, hs8, hs8, ALU.mult).then_inc(sem("hn_step"), 1)
                v.wait_ge(sem("hn_step"), l * 5 + 4)
                v.tensor_reduce(s2, hn8, AX, ALU.add).then_inc(sem("hn_step"), 1)
                v.wait_ge(sem("hn_step"), l * 5 + 5)
                v.tensor_scalar(var_c, s2, 1.0 / HD, LN_EPS, ALU.mult, ALU.add).then_inc(sem("varc_ready"), 1)
                v.wait_ge(sem("rstdc_ready"), l + 1)
                v.tensor_tensor(hn8, hs8, over_e(rstd_c), ALU.mult).then_inc(sem("hn_ready"), 1)
                v.wait_ge(sem("hn_turned"), l + 1)
                v.wait_ge(sem("sig_ready"), l + 1)
                for t in range(2):
                    v.scalar_tensor_tensor(oT[:, 4 + t, :], PS[:, 6, t * T:(t + 1) * T], col(R_MHG, t), sig_o[:, t, :],
                                           ALU.mult, ALU.mult).then_inc(sem("oc_ready"), 1)
                w_in_low(G_FFN2 % 2, 0, ff_tile(l, 1, 0, 0))
                deepnorm(l, 1)
                evac_uT(2, l * 24 + 16, l * 3 + 3, l * 2 + 1)
                w_in_low(G_FFN2 % 2, 1, ff_tile(l, 1, 0, 0) + 1)

                for j in range(2):
                    ffn_chunk(l, 1, 0, j)
                with v.Fori(0, TRIPS[1]) as it:
                    for j in range(2):
                        ffn_chunk(l, 1, it + 1, j)
                ffn_chunk(l, 1, 4, 0)
                mod_cols(slice(64, 72), slice(0, 8), (l + 1) * ADA_PER_LAYER + ADA_FIRST)
                mod_cols(slice(0, 24), slice(8, 32), (l + 1) * ADA_PER_LAYER + ADA_FIRST)
                gate_diag(2, l * 3 + 2, l * MODS + 3, 0)
                ffn_chunk(l, 1, 4, 1)
                gate_diag(2, l * 3 + 2, l * MODS + 3, 1)
                ffn_chunk(l, 1, 5, 0)
                mod_ab(0, 2, l * 3 + 3, l * MODS + 4)
                with v.If(l < DEPTH - 1):
                    w_in_low(0, 0, ff_tile(l + 1, 0, 0, 0))
                deepnorm(l, 2)
                evac_uT(0, l * 24 + 24, l * 3 + 4, l * 2 + 2)
                with v.If(l < DEPTH - 1):
                    w_in_low(0, 1, ff_tile(l + 1, 0, 0, 0) + 1)

        @block.scalar
        def _(a):
            a.wait_ge(sem("c_loaded"), 16)
            a.activation(cs[:, :], c_sb[:, :], ACT.Silu).then_inc(sem("cs_ready"), 1)

            def evac_uT(s, turned, ab, split=None):
                dst = uT if split is None else uT_lo
                a.wait_ge(sem("mod_step"), ab * 3)
                for j in range(4):
                    if j % 2 == 0:
                        a.wait_ge(sem("x_turned"), turned + (TURN_ORDER.index(j + 1) + 1))
                    a.activation(dst[:, j, :], PS[:, 4 + j // 2, (j % 2) * T:(j % 2 + 1) * T], ACT.Identity, bias=mod_b[:, s, j:j + 1],
                                 scale=mod_a[:, s, j:j + 1]).then_inc(sem("uT_act"), 1)
                    if j % 2 and split is not None:
                        a.wait_ge(sem("uT_act"), turned // 2 + (j + 1))
                        a.activation(u_hi[:, j - 1:j + 1, :], uT_lo[:, j - 1:j + 1, :], ACT.Copy).then_inc(sem("uT_high_act"), 1)

            def normalise(l, s):
                n = l * 3 + s
                for tt, cols in ((0, slice(0, D)), (1, slice(512, D))):
                    a.wait_ge(sem("nmr_ready"), n * 2 + (tt + 1))
                    a.activation(xn[:, tt, cols], xn[:, tt, cols], ACT.Identity, bias=nmr[:, tt:tt + 1],
                                 scale=rstd[:, tt:tt + 1]).then_inc(sem("xn_act"), 1)

            def copy_gate(n, factor, hf):
                a.wait_ge(sem("gate_spread"), n * 2 + (hf + 1))
                a.activation(gate_bc[:, hf * 512:(hf + 1) * 512], PS[:, 7, :], ACT.Copy, scale=factor
                             ).then_inc(sem("gate_ready"), 1)

            def silu_tile(ft, tile):
                a.wait_ge(sem("ag_ready"), tile + (ft + 3))
                a.wait_ge(sem("h_done"), tile + (ft + 1))
                a.activation(silu_ring[:, ft, :], PS[:, 4 + ft, 0:T], ACT.Silu).then_inc(sem("silu_ready"), 1)

            def w_in_high(slot, ft, tile):
                a.wait_ge(sem("ag_ready"), tile + 1)
                a.activation(w_in_hi[ft][:, :, :, :], w_in_tile(w_in_ring, slot, ft), ACT.Copy).then_inc(sem("w_in_high"), 1)

            def w_out_high(l, f, it, j):
                g = (0, G_FFN2)[f] + j
                slot = g % 2
                a.wait_ge(sem(f"w_out_loaded{slot}"), ring_use(l, g, it) * 16 + 16)
                a.wait_ge(sem(f"w_out_used{1 - slot}"), ring_use(l, g - 1, it) + 2)
                for ft in range(2):
                    a.activation(w_out_hi[ft][:, :], w_out_ring[slot][:, ft, :], ACT.Copy).then_inc(sem("w_out_high"), 1)

            def ffn_chunk(l, f, it, j):
                last = isinstance(it, int) and it * 2 + j == CHUNKS - 1
                slot = ((0, G_FFN2)[f] + j) % 2
                tile = ff_tile(l, f, it, j)
                for ft in range(2):
                    silu_tile(ft, tile)
                    if not last:
                        if ft == 0:
                            a.wait_ge(sem(f"w_in_loaded{1 - slot}"), in_loads(l, f, it, j + 1))
                        w_in_high(1 - slot, ft, tile + (2 + ft))
                if not last:
                    w_out_high(l, f, it, j + 1)

            evac_uT(0, 0, 1, 0)
            a.wait_ge(sem("w_in_loaded0"), in_loads(0, 0, 0, 0))
            for ft in range(2):
                w_in_high(0, ft, ft)
            with a.Fori(0, DEPTH) as l:
                w_out_high(l, 0, 0, 0)
                for j in range(2):
                    ffn_chunk(l, 0, 0, j)
                copy_gate(l * 3, 0.5, 0)
                a.wait_ge(sem("prm_ready"), l + 1)
                a.activation(S5["dt"], log_dt[:, :], ACT.Exp).then_inc(sem("dt_ready"), 1)
                a.wait_ge(sem("lrdt_ready"), l + 1)
                a.activation(S5["rho"], S5["lrdt"], ACT.Exp)
                a.wait_ge(sem("angle_ready"), l + 1)
                a.activation(S5["sin"], S5["r0"], ACT.Sin)
                a.activation(S5["sinh"], S5["r0"], ACT.Sin, scale=0.5).then_inc(sem("sin_ready"), 1)
                with a.Fori(0, TRIPS[0]) as it:
                    for j in range(2):
                        ffn_chunk(l, 0, it + 1, j)
                copy_gate(l * 3, 0.5, 1)
                ffn_chunk(l, 0, 5, 0)
                a.wait_ge(sem("bb_turned"), l + 1)
                a.activation(bbT[:, :, :, :].rearrange("p a b c -> p (a b c)"), PS[:, 7, :], ACT.Copy).then_inc(sem("bbT_ready"), 1)
                a.wait_ge(sem("c_turned"), l + 1)
                a.activation(cT[:, :, :, :].rearrange("p a b c -> p (a b c)"), PS[:, 7, :], ACT.Copy).then_inc(sem("cT_ready"), 1)
                normalise(l, 0)
                evac_uT(1, l * 24 + 8, l * 3 + 2)

                def z_in(n):
                    a.wait_ge(sem("z_ready"), l * NZ + (n + 1))
                    return PS[:, 4 + n % 4, 0:T]

                def z_copy(n, dst, w=T):
                    a.activation(dst, z_in(n)[:, 0:w], ACT.Copy).then_inc(sem("z_read"), 1)

                z_copy(0, udT[:, 0, :])
                z_copy(1, udT[:, 1, :])
                for hf in range(2):
                    copy_gate(l * 3 + 1, 1.0, hf)
                z_copy(2, kiT[:, :])
                z_copy(3, cqT[:, :])
                z_copy(4, tokv[:, 0, :], 196)
                z_copy(5, tokv[:, 1, :], 196)
                z_copy(6, kbT[:, :])
                a.wait_ge(sem("ln_bc_used"), l * 3 + 2)
                for n in (7, 8):
                    a.activation(rows[:, n - 7, :], z_in(n)[0:H, :], ACT.Identity, bias=gate_bias[:, n - 7:n - 6]
                                 ).then_inc(sem("z_read"), 1)
                z_copy(9, qiT[:, :])
                z_copy(10, qbT[:, 0, :])
                z_copy(11, qbT[:, 1, :])
                e_row, ln_row = work[3][0:H, 0, 0:T], work[3][0:H, 1, 0:T]
                a.wait_ge(sem("z_read"), l * NZ + 12)
                a.activation(e_row, rows[:, 1, :], ACT.Abs).then_inc(sem("f_step"), 1)
                a.wait_ge(sem("f_step"), l * 2 + 1)
                a.activation(e_row, e_row, ACT.Exp, scale=-1.0).then_inc(sem("f_step"), 1)
                a.wait_ge(sem("f_step"), l * 2 + 2)
                a.activation(ln_row, e_row, ACT.Ln, bias=1.0).then_inc(sem("ln_f_ready"), 1)
                z_copy(12, qk_raw[:, 0, :])
                z_copy(13, qk_raw[:, 1, :])
                a.wait_ge(sem("idx_ready"), l + 1)
                a.activation(work[0][:, :, :], PS[:, 0:4, 0:384], ACT.Relu).then_inc(sem("idx_read"), 1)
                z_copy(14, qk_raw[:, 2, :])
                z_copy(15, qk_raw[:, 3, :])
                for n in range(16, 18):
                    z_copy(n, qaT[:, n - 16, :])
                for n in range(18, 20):
                    z_copy(n, kaT[:, n - 18, :])
                a.wait_ge(sem("vaug_ones"), 1)
                for n in (20, 21):
                    a.activation(vaug[:, n - 20, :, 0:HD], z_in(n).rearrange("p (h e) -> p h e", h=H), ACT.Copy
                                 ).then_inc(sem("z_read"), 1)
                def exps(p, nmx, rs, name, ready):
                    a.wait_ge(sem(ready), l + 1)
                    for tt, cols in ((0, slice(0, P)), (1, slice(P, 384))):
                        for h in range(H):
                            a.activation(p[:, h, cols], p[:, h, cols], ACT.Exp, bias=heads(nmx)[:, tt, h:h + 1],
                                         accum_out=heads(rs)[:, tt, h:h + 1]).then_inc(sem(name), 1)

                exps(work[0], nmx_b, rs_b, "b_exp", "b_nmax")
                for n in (22, 23):
                    a.activation(sig_o[:, n - 22, :], z_in(n), ACT.Tanh, scale=0.5).then_inc(sem("z_read"), 1)

                a.wait_ge(sem("conv_step"), l * 16 + 16)
                a.wait_ge(sem("sb_read"), l + 1)
                a.activation(qk_tanh, qkT[:, :, :].rearrange("p a b -> p (a b)"), ACT.Tanh, scale=0.5).then_inc(sem("conv_tanh"), 1)
                exps(work[2], nmx_a, rs_a, "a_exp", "a_nmax")
                a.wait_ge(sem("sink_arg"), l + 1)
                a.activation(es_a, ds_a, ACT.Exp).then_inc(sem("a_exp"), 1)
                a.wait_ge(sem("yd_read"), l * 2 + 2)
                a.activation(tmp[1], tmp[0], ACT.Square).then_inc(sem("gelu_sq"), 1)
                pta = work[3][:, :, :].rearrange("p h n -> p (h n)")
                a.wait_ge(sem("gelu_step"), l * 2 + 2)
                a.activation(tmp[1], tmp[1], ACT.Tanh, scale=GELU_S).then_inc(sem("gelu_tanh"), 1)
                a.wait_ge(sem("ob_ready"), l + 1)
                a.activation(oT[:, 2:4, :].rearrange("p a b -> p (a b)"), PS[:, 4, :], ACT.Copy).then_inc(sem("ob_read"), 1)
                a.wait_ge(sem("rows_ready"), l * 2 + 2)
                for b in range(3):
                    a.wait_ge(sem("pta_turned"), l * 3 + (b + 1))
                    a.activation(pta[:, b * 512:(b + 1) * 512], PS[:, 4 + b, :], ACT.Copy).then_inc(sem("pta_ready"), 1)
                a.wait_ge(sem("gb_half_ready"), l + 1)
                a.wait_ge(sem("glu_ready"), l + 1)
                for t in range(2):
                    ins = a.activation(tmp[2][:, t * T:(t + 1) * T], PS[:, 7, t * T:(t + 1) * T], ACT.Tanh, scale=0.25,
                                       bias=gb_half[:, t:t + 1])
                ins.then_inc(sem("glu_tanh"), 1)
                a.wait_ge(sem("oa_ready"), l + 1)
                a.activation(oT[:, 0:2, :].rearrange("p a b -> p (a b)"), PS[:, 4, :], ACT.Copy).then_inc(sem("oa_read"), 1)
                a.wait_ge(sem("cols_ready"), l * 2 + 2)
                a.activation(enm, nmcol, ACT.Exp)
                a.wait_ge(sem("w_args_ready"), l + 1)
                a.activation(work[0][:, :, :], work[0][:, :, :], ACT.Exp).then_inc(sem("w_exp"), 1)
                a.wait_ge(sem("num_ready"), l + 1)
                a.activation(heads(den), PS[:, 4:6, 0:260].rearrange("p t (h e) -> p t h e", h=H)[:, :, :, 64], ACT.Abs
                             ).then_inc(sem("den_ready"), 1)
                a.wait_ge(sem("hn_turned"), l + 1)
                a.wait_ge(sem(f"w_in_loaded{G_FFN2 % 2}"), in_loads(l, 1, 0, 0))
                for ft in range(2):
                    w_in_high(G_FFN2 % 2, ft, ff_tile(l, 1, 0, 0) + ft)
                normalise(l, 1)
                evac_uT(2, l * 24 + 16, l * 3 + 3, l * 2 + 1)

                w_out_high(l, 1, 0, 0)
                for j in range(2):
                    ffn_chunk(l, 1, 0, j)
                with a.Fori(0, TRIPS[1]) as it:
                    for j in range(2):
                        ffn_chunk(l, 1, it + 1, j)
                ffn_chunk(l, 1, 4, 0)
                copy_gate(l * 3 + 2, 0.5, 0)
                ffn_chunk(l, 1, 4, 1)
                copy_gate(l * 3 + 2, 0.5, 1)
                ffn_chunk(l, 1, 5, 0)
                with a.If(l < DEPTH - 1):
                    a.wait_ge(sem("w_in_loaded0"), in_loads(l + 1, 0, 0, 0))
                    for ft in range(2):
                        w_in_high(0, ft, ff_tile(l + 1, 0, 0, 0) + ft)
                normalise(l, 2)
                evac_uT(0, l * 24 + 24, l * 3 + 4, l * 2 + 2)

        @block.gpsimd
        def _(g):
            for buf in (ada_w_sb, ada_w_2):
                g.memset(buf[:, 8, :], 0.0).then_inc(sem("pad_zeroed"), 1)
            g.memset(ident[:, :], 0.0).then_inc(sem("const_step"), 1)
            g.memset(ones[:, :], 1.0).then_inc(sem("const_step"), 1)
            g.memset(neg_half[:, :], -0.5).then_inc(sem("const_step"), 1)
            g.memset(zeros_bf[:, :], 0.0).then_inc(sem("const_step"), 1)
            g.memset(mask_c[:, :], 0.0).then_inc(sem("const_step"), 1)
            bm = rot_flat[:, 384:512].rearrange("p (q two c) -> p q two c", two=2, c=16)
            g.memset(rot_flat[:, 384:512], 0.0).then_inc(sem("const_step"), 1)
            g.wait_ge(sem("const_step"), 6)
            g.memset(bm[0:64, :, 0, :], 1.0).then_inc(sem("const_step"), 1)
            g.memset(bm[64:128, :, 1, :], 1.0).then_inc(sem("const_step"), 1)
            g.wait_ge(sem("const_step"), 8)
            g.affine_select(out=ident[:, :], in_=ident[:, :], compare_op=ALU.not_equal, fill=1.0, base=0,
                            pattern=[[-1, P]], channel_multiplier=1).then_inc(sem("const_step"), 1)
            g.affine_select(out=mask_c[:, :], in_=mask_c[:, :], compare_op=ALU.is_ge, fill=NEG, base=0,
                            pattern=[[1, T]], channel_multiplier=-1).then_inc(sem("const_step"), 1)
            g.iota(dist[:, 0:P], pattern=[[1, P]], base=0, channel_multiplier=-1,
                   allow_small_or_imprecise_dtypes=True).then_inc(sem("const_step"), 1)
            g.iota(dist[:, P:384], pattern=[[1, T]], base=-P, channel_multiplier=-1,
                   allow_small_or_imprecise_dtypes=True).then_inc(sem("const_step"), 1)
            for m in (mask_a, mask_b[:, :]):
                g.memset(m, 0.0).then_inc(sem("const_step"), 1)
            g.wait_ge(sem("const_step"), 14)
            for m in (mask_a, mask_b[:, :]):
                g.memset(m[0:64, 64:128], NEG).then_inc(sem("const_step"), 1)
                g.memset(m[0:64, P + 192:P + 256], NEG).then_inc(sem("const_step"), 1)
            g.memset(mask_a[64:128, P:P + 64], NEG).then_inc(sem("const_step"), 1)
            g.wait_ge(sem("const_step"), 19)
            g.sem_inc(sem("ln_bc_used"), 1)
            g.wait_ge(sem("x_loaded"), 32)
            g.sem_inc(sem("x_ready"), 2)

            def residual(l, s):
                n = l * 3 + s
                for tt in range(2):
                    g.wait_ge(sem("var_ready"), n * 2 + (tt + 1))
                    g.tensor_tensor(rstd[:, tt:tt + 1], var_eps[:, tt:tt + 1], neg_half[:, 0:1], ALU.pow
                                    ).then_inc(sem("rstd_ready"), 1)
                g.wait_ge(sem("ln_bc_loaded"), (n + 1) * 32)
                for tt in range(2):
                    g.wait_ge(sem("xn_act"), n * 2 + (tt + 1))
                    if tt == 1:
                        g.wait_ge(sem("xn_dve"), n + 1)
                    g.tensor_tensor(x_sb[:, tt, :], xn[:, tt, :], ln_bc[:, 0, :], ALU.mult).then_inc(sem("x_step"), 1)
                    g.wait_ge(sem("x_step"), n * 2 + (tt + 1))
                    g.tensor_tensor(x_sb[:, tt, :], x_sb[:, tt, :], ln_bc[:, 1, :], ALU.add).then_inc(sem("x_ready"), 1)
                g.wait_ge(sem("x_ready"), n * 2 + 4)
                g.sem_inc(sem("ln_bc_used"), 1)

            with g.Fori(0, DEPTH) as l:
                g.wait_ge(sem("rot_start"), l * 2 + 4)
                steps = [(m, 1, m) for m in (1, 2, 4, 8, 16, 32, 64)] + [(P, 1, 64), (P, 65, 63)]
                for k, (m, first, w) in enumerate(steps):
                    lo = slice(first, first + w)
                    hi = slice(m + first, m + first + w)
                    t4 = [rot_flat[:, 512 * q:512 * q + 8 * w].rearrange("p (i n) -> p i n", i=8) for q in range(4)]
                    cm = cos_t[:, :, m:m + 1].to_broadcast([P, 8, w])
                    sm = sin_t[:, :, m:m + 1].to_broadcast([P, 8, w])
                    if k:
                        g.wait_ge(sem("rot_step"), l * ROT_STEPS + 6 * k)
                    g.tensor_tensor(t4[0], cos_t[:, :, lo], cm, ALU.mult).then_inc(sem("rot_step"), 1)
                    g.tensor_tensor(t4[1], sin_t[:, :, lo], sm, ALU.mult).then_inc(sem("rot_step"), 1)
                    g.tensor_tensor(t4[2], sin_t[:, :, lo], cm, ALU.mult).then_inc(sem("rot_step"), 1)
                    g.tensor_tensor(t4[3], cos_t[:, :, lo], sm, ALU.mult).then_inc(sem("rot_step"), 1)
                    g.wait_ge(sem("rot_step"), l * ROT_STEPS + (6 * k + 4))
                    g.tensor_tensor(cos_t[:, :, hi], t4[0], t4[1], ALU.subtract).then_inc(sem("rot_step"), 1)
                    g.tensor_tensor(sin_t[:, :, hi], t4[2], t4[3], ALU.add).then_inc(sem("rot_step"), 1)
                residual(l, 0)
                for b in range(4):
                    tl = slice(2 * b, 2 * b + 2)
                    g.wait_ge(sem("bu_read"), l * 4 + (b + 1))
                    t_re, t_im = (tmp[2 * (b % 2) + q].rearrange("p (a b) -> p a b", a=2) for q in range(2))
                    g.tensor_tensor(st_re[:, tl, :], st_re[:, tl, :], t_re, ALU.add).then_inc(sem("rotated_in"), 1)
                    g.tensor_tensor(st_im[:, tl, :], st_im[:, tl, :], t_im, ALU.subtract).then_inc(sem("rotated_in"), 1)
                for b in range(4):
                    tl = slice(2 * b, 2 * b + 2)
                    g.wait_ge(sem("rotating_out"), l * 4 + (b + 1))
                    t4 = [tmp[q].rearrange("p (a b) -> p a b", a=2) for q in range(4)]
                    g.tensor_tensor(st_re[:, tl, :], t4[0], t4[1], ALU.subtract).then_inc(sem("rotated_out"), 1)
                    g.tensor_tensor(st_im[:, tl, :], t4[2], t4[3], ALU.add).then_inc(sem("rotated_out"), 1)
                g.tensor_scalar(gb_half[:, 0:2], prm[:, R_GB:R_GB + 2], 0.5, 0.0, ALU.mult, ALU.add).then_inc(sem("gb_half_ready"), 1)

                def normalise(p, ri, ready, signal):
                    g.wait_ge(sem(ready), l + 1)
                    for tt, c0, w in ((0, 0, P), (1, P, T)):
                        g.tensor_tensor(p[:, :, c0:c0 + w], p[:, :, c0:c0 + w],
                                        heads(ri)[:, tt, :].unsqueeze(2).to_broadcast([P, H, w]), ALU.mult
                                        ).then_inc(sem(signal), 1)

                normalise(work[0], ri_b, "rib_ready", "pb_ready")
                g.wait_ge(sem("z_read"), l * NZ + NZ)
                waited(g)
                g.tensor_scalar(sig_o[:, :, :], sig_o[:, :, :], 0.5, 0.5, ALU.mult, ALU.add).then_inc(sem("sig_ready"), 1)
                normalise(work[2], ri_a, "ria_ready", "pa_ready")
                g.wait_ge(sem("varc_ready"), l + 1)
                g.tensor_tensor(rstd_c, var_c, neg_half[:, :], ALU.pow).then_inc(sem("rstdc_ready"), 1)
                settle(g)
                g.wait_ge(sem("od_ready"), l + 1)
                g.memset(ada_w_sb[:, 8, :], 0.0).then_inc(sem("pad_zeroed"), 1)
                residual(l, 1)
                residual(l, 2)


_INS = ["x", "c", "ada_w", "ada_b", "ln_g", "ln_b", "ffn_w13", "ffn_w2", "w_in", "w_out", "sinks", "w_uq", "w_iq",
        "conv_w", "conv_b", "ig_b", "fg_b", "mh_norm_g", "lam_re", "lam_im", "log_step", "b_re", "b_im", "c_re",
        "c_im", "d_skip", "glu_w", "glu_b"]


def kernel(**inputs):
    import numpy as _np
    import concourse.bacc as _bacc
    from concourse import mybir as _mybir
    from concourse.bass_utils import run_bass_kernel_spmd as _run

    nc = _bacc.Bacc("TRN2", target_bir_lowering=False, num_devices=1)
    arrays, args = {}, []
    for name in _INS:
        a = _np.ascontiguousarray(inputs[name])
        arrays[f"in_{name}_dram"] = a
        args.append(nc.dram_tensor(f"in_{name}_dram", a.shape, _mybir.dt.from_np(a.dtype), kind="ExternalInput").ap())
    args.append(nc.dram_tensor("out_0_dram", (1, T, D), _mybir.dt.from_np(_np.dtype("float32")), kind="ExternalOutput").ap())
    trunk(nc, *args)
    r = _run(nc, [arrays], core_ids=[0])
    return r.results[0]["out_0_dram"]
```
